# Optimizing a Trainium2 kernel written in Bass

```python
import math
import jax, jax.numpy as jnp
from jax import lax
import numpy as np

D_MODEL = 1024
BATCH = 1
SEQ = 512
DEPTH = 2
DEC_BATCH = 8
DEC_SEQ = 8
PAST_LEN = 1024
PAGE_SIZE = 128

N_EVEN = (DEPTH + 1) // 2
N_ODD = DEPTH // 2
ATT_HEADS = 8
HEAD_DIM = 64
ATT_WIDTH = ATT_HEADS * HEAD_DIM
MOBA_BLOCK = 256
MOBA_TOPK = 3
Q_BLOCK = 128
LRU_WIDTH = 512
LRU_BLOCKS = 8
LRU_BLOCK_DIM = LRU_WIDTH // LRU_BLOCKS
LRU_C = 8.0
CONV_W = 4
EVEN_IN = 3 * ATT_WIDTH + 2 * LRU_WIDTH
EVEN_MIX = ATT_WIDTH + LRU_WIDTH
SSD_INNER = 2 * D_MODEL
SSD_HEAD_DIM = 64
SSD_HEADS = SSD_INNER // SSD_HEAD_DIM
SSD_GROUPS = 8
SSD_HPG = SSD_HEADS // SSD_GROUPS
SSD_STATE = 128
SSD_CHUNK = 128
SSD_CONV_DIM = SSD_INNER + 2 * SSD_GROUPS * SSD_STATE
SSD_IN = SSD_INNER + SSD_CONV_DIM + SSD_HEADS
D_FF = 2816
N_EXPERTS = 8
TOP_K = 2
D_FF_EXPERT = 1408
DN_ALPHA = (2 * DEPTH) ** 0.25
DN_BETA = (8 * DEPTH) ** -0.25
LN_EPS = 1e-5
RMS_EPS = 1e-6

kernel_name = 'moba_rglru_ssd_hybrid_step'

F32 = jnp.float32

def layer_norm(x, g, b):
    xf = x.astype(F32)
    mu = jnp.mean(xf, -1, keepdims=True)
    var = jnp.mean(jnp.square(xf - mu), -1, keepdims=True)
    return ((xf - mu) * lax.rsqrt(var + LN_EPS) * g + b).astype(x.dtype)

def causal_conv(x, buf, w, b):
    L = x.shape[1]
    xp = jnp.concatenate([buf.astype(x.dtype), x], axis=1)
    y = b
    for t in range(CONV_W):
        y = y + xp[:, t:t + L] * w[t]
    return y.astype(x.dtype), xp[:, L:]

def rg_lru(u, h0, w_a, b_a, w_x, b_x, lam):
    Bn, L, _ = u.shape
    ub = u.astype(F32).reshape(Bn, L, LRU_BLOCKS, LRU_BLOCK_DIM)
    gate_r = jax.nn.sigmoid(jnp.einsum('blnd,nde->blne', ub, w_a.astype(F32)) + b_a)
    gate_i = jax.nn.sigmoid(jnp.einsum('blnd,nde->blne', ub, w_x.astype(F32)) + b_x)
    log_a = -LRU_C * gate_r * jax.nn.softplus(-lam.astype(F32))
    a = jnp.exp(log_a).reshape(Bn, L, LRU_WIDTH)
    bterm = (jnp.sqrt(-jnp.expm1(2.0 * log_a)) * (gate_i * ub)).reshape(Bn, L, LRU_WIDTH)
    bterm = bterm.at[:, 0].add(a[:, 0] * h0.astype(F32))

    def combine(left, right):
        return left[0] * right[0], right[0] * left[1] + right[1]

    _, h = lax.associative_scan(combine, (a, bterm), axis=1)
    return h, h[:, -1]

def moba_select(q, means, n_past, k_sel):
    s = jnp.einsum('bqhd,bnhd->bqhn', q.astype(F32), means)
    past = jnp.arange(means.shape[1])[None, :] < n_past[:, None]
    s = jnp.where(past[:, None, :], s, -jnp.inf)
    _, idx = lax.top_k(s, k_sel)
    valid = jnp.arange(k_sel)[None, :] < n_past[:, None]
    return idx, valid

def gather_blocks(blocks, idx):
    Bn, H = blocks.shape[0], blocks.shape[3]
    b_ix = jnp.arange(Bn)[:, None, None, None]
    h_ix = jnp.arange(H)[None, None, :, None]
    return blocks[b_ix, idx, :, h_ix, :]

def moba_core(q, k_own, v_own, own_mask, k_sel=None, v_sel=None, sel_valid=None):
    qf = q.astype(F32) * (HEAD_DIM ** -0.5)
    lo = jnp.einsum('bqhd,bkhd->bqhk', qf, k_own.astype(F32))
    lo = jnp.where(own_mask[:, None, :], lo, -jnp.inf)
    if k_sel is None:
        p = jax.nn.softmax(lo, axis=-1)
        out = jnp.einsum('bqhk,bkhd->bqhd', p, v_own.astype(F32))
    else:
        ls = jnp.einsum('bqhd,bqhskd->bqhsk', qf, k_sel.astype(F32))
        ls = jnp.where(sel_valid[:, None, :, None], ls, -jnp.inf)
        Bn, Q, H, S, K = ls.shape
        p = jax.nn.softmax(jnp.concatenate([ls.reshape(Bn, Q, H, S * K), lo], -1), axis=-1)
        ps = p[..., :S * K].reshape(Bn, Q, H, S, K)
        po = p[..., S * K:]
        out = (jnp.einsum('bqhsk,bqhskd->bqhd', ps, v_sel.astype(F32))
               + jnp.einsum('bqhk,bkhd->bqhd', po, v_own.astype(F32)))
    return out.astype(q.dtype)

def moba_prompt(q, k, v):
    Bn, S, H, D = q.shape
    nb = -(-S // MOBA_BLOCK)
    pad = nb * MOBA_BLOCK - S
    kp = jnp.pad(k, ((0, 0), (0, pad), (0, 0), (0, 0)))
    vp = jnp.pad(v, ((0, 0), (0, pad), (0, 0), (0, 0)))
    kb = kp.reshape(Bn, nb, MOBA_BLOCK, H, D)
    vb = vp.reshape(Bn, nb, MOBA_BLOCK, H, D)
    means = jnp.mean(kb.astype(F32), axis=2)
    k_sel = min(MOBA_TOPK, nb - 1)

    def one(i):
        q0 = i * Q_BLOCK
        j = q0 // MOBA_BLOCK
        qi = lax.dynamic_slice_in_dim(q, q0, Q_BLOCK, axis=1)
        ko = lax.dynamic_slice_in_dim(kp, j * MOBA_BLOCK, MOBA_BLOCK, axis=1)
        vo = lax.dynamic_slice_in_dim(vp, j * MOBA_BLOCK, MOBA_BLOCK, axis=1)
        qpos = q0 + jnp.arange(Q_BLOCK)
        kpos = j * MOBA_BLOCK + jnp.arange(MOBA_BLOCK)
        own_mask = kpos[None, :] <= qpos[:, None]
        if k_sel == 0:
            return moba_core(qi, ko, vo, own_mask)
        idx, valid = moba_select(qi, means, jnp.full((Q_BLOCK,), j), k_sel)
        return moba_core(qi, ko, vo, own_mask, gather_blocks(kb, idx), gather_blocks(vb, idx), valid)

    out = lax.map(one, jnp.arange(S // Q_BLOCK))
    return out.transpose(1, 0, 2, 3, 4).reshape(Bn, S, H * D)

def moba_sample(q, k, v, cache_k, cache_v, page_table):
    Bn, T, H, D = q.shape
    past = page_table.shape[1] * cache_k.shape[1]
    kp = cache_k[page_table].reshape(Bn, past, H, D)
    vp = cache_v[page_table].reshape(Bn, past, H, D)
    cur = past // MOBA_BLOCK
    start = cur * MOBA_BLOCK
    ko = jnp.concatenate([kp[:, start:].astype(k.dtype), k], axis=1)
    vo = jnp.concatenate([vp[:, start:].astype(v.dtype), v], axis=1)
    qpos = past + jnp.arange(T)
    kpos = start + jnp.arange(past - start + T)
    own_mask = kpos[None, :] <= qpos[:, None]
    k_sel = min(MOBA_TOPK, cur)
    if k_sel == 0:
        return moba_core(q, ko, vo, own_mask).reshape(Bn, T, H * D)
    kb = kp[:, :start].reshape(Bn, cur, MOBA_BLOCK, H, D)
    vb = vp[:, :start].reshape(Bn, cur, MOBA_BLOCK, H, D)
    means = jnp.mean(kb.astype(F32), axis=2)
    idx, valid = moba_select(q, means, jnp.full((T,), cur), k_sel)
    out = moba_core(q, ko, vo, own_mask, gather_blocks(kb, idx), gather_blocks(vb, idx), valid)
    return out.reshape(Bn, T, H * D)

def even_mixer(x, kv, conv_buf, h0, w_in, conv_w, conv_b, w_a, b_a, w_x, b_x, lam, w_out):
    Bn, L, _ = x.shape
    proj = x @ w_in
    q, k, v, u, gate = jnp.split(proj, [ATT_WIDTH, 2 * ATT_WIDTH, 3 * ATT_WIDTH, 3 * ATT_WIDTH + LRU_WIDTH], axis=-1)
    q = q.reshape(Bn, L, ATT_HEADS, HEAD_DIM)
    k = k.reshape(Bn, L, ATT_HEADS, HEAD_DIM)
    v = v.reshape(Bn, L, ATT_HEADS, HEAD_DIM)
    if kv is None:
        att = moba_prompt(q, k, v)
    else:
        att = moba_sample(q, k, v, kv[0], kv[1], kv[2])
    uc, conv_new = causal_conv(u, conv_buf, conv_w, conv_b)
    h, h_last = rg_lru(uc, h0, w_a, b_a, w_x, b_x, lam)
    rec = (h * jax.nn.gelu(gate.astype(F32))).astype(x.dtype)
    y = jnp.concatenate([att, rec], axis=-1) @ w_out
    return y, k, v, h_last.astype(h0.dtype), conv_new.astype(conv_buf.dtype)

def ssd_chunked(x, dt, A, bm, cm, h0, chunk):
    Bn, L, G, E, P = x.shape
    nc = L // chunk
    xf = x.astype(F32).reshape(Bn, nc, chunk, G, E, P)
    bf = bm.astype(F32).reshape(Bn, nc, chunk, G, SSD_STATE)
    cf = cm.astype(F32).reshape(Bn, nc, chunk, G, SSD_STATE)
    dtc = dt.reshape(Bn, nc, chunk, G, E)
    cs = jnp.cumsum(dtc * A, axis=2)
    cst = jnp.moveaxis(cs, 2, -1)
    causal = jnp.tril(jnp.ones((chunk, chunk), bool))
    decay_ls = jnp.exp(jnp.where(causal, cst[..., :, None] - cst[..., None, :], -jnp.inf))
    cb = jnp.einsum('bclgn,bcsgn->bcgls', cf, bf)
    m = cb[:, :, :, None] * decay_ls * jnp.moveaxis(dtc, 2, -1)[..., None, :]
    y = jnp.einsum('bcgels,bcsgep->bclgep', m, xf)
    decay_end = jnp.exp(cs[:, :, -1:] - cs)
    states = jnp.einsum('bclgn,bclge,bclgep->bcgepn', bf, decay_end * dtc, xf)
    chunk_decay = jnp.exp(cs[:, :, -1])

    def step(h, inp):
        dec, st = inp
        return dec[..., None, None] * h + st, h

    h_last, h_prev = lax.scan(step, h0, (jnp.moveaxis(chunk_decay, 1, 0), jnp.moveaxis(states, 1, 0)))
    h_prev = jnp.moveaxis(h_prev, 0, 1)
    y = y + jnp.einsum('bclgn,bcgepn,bclge->bclgep', cf, h_prev, jnp.exp(cs))
    return y.reshape(Bn, L, G, E, P), h_last

def ssd_mixer(x, conv_buf, h0, w_in, conv_w, conv_b, dt_bias, a_log, d_skip, norm_g, w_out):
    Bn, L, _ = x.shape
    proj = x @ w_in
    z, xbc, dt = jnp.split(proj, [SSD_INNER, SSD_INNER + SSD_CONV_DIM], axis=-1)
    xbc, conv_new = causal_conv(xbc, conv_buf, conv_w, conv_b)
    xbc = jax.nn.silu(xbc)
    xs, bm, cm = jnp.split(xbc, [SSD_INNER, SSD_INNER + SSD_GROUPS * SSD_STATE], axis=-1)
    xs = xs.reshape(Bn, L, SSD_GROUPS, SSD_HPG, SSD_HEAD_DIM)
    bm = bm.reshape(Bn, L, SSD_GROUPS, SSD_STATE)
    cm = cm.reshape(Bn, L, SSD_GROUPS, SSD_STATE)
    dt = jax.nn.softplus(dt.astype(F32) + dt_bias).reshape(Bn, L, SSD_GROUPS, SSD_HPG)
    A = -jnp.exp(a_log.astype(F32)).reshape(SSD_GROUPS, SSD_HPG)
    h0g = h0.astype(F32).reshape(Bn, SSD_GROUPS, SSD_HPG, SSD_HEAD_DIM, SSD_STATE)
    y, h_last = ssd_chunked(xs, dt, A, bm, cm, h0g, math.gcd(L, SSD_CHUNK))
    y = y + d_skip.astype(F32).reshape(SSD_GROUPS, SSD_HPG, 1) * xs.astype(F32)
    y = y.reshape(Bn, L, SSD_INNER) * jax.nn.silu(z.astype(F32))
    yg = y.reshape(Bn, L, SSD_GROUPS, SSD_INNER // SSD_GROUPS)
    yg = yg * lax.rsqrt(jnp.mean(jnp.square(yg), -1, keepdims=True) + RMS_EPS)
    y = (yg.reshape(Bn, L, SSD_INNER) * norm_g).astype(x.dtype)
    h_last = h_last.reshape(Bn, SSD_HEADS, SSD_HEAD_DIM, SSD_STATE).astype(h0.dtype)
    return y @ w_out, h_last, conv_new.astype(conv_buf.dtype)

def swiglu(x, w1, w3, w2):
    return (jax.nn.silu(x @ w1) * (x @ w3)) @ w2

def moe_swiglu(x, router, w1, w3, w2):
    logits = (x @ router).astype(F32)
    top_v, top_i = lax.top_k(logits, TOP_K)
    gates = jax.nn.softmax(top_v, axis=-1)
    out = jnp.zeros(x.shape, F32)
    for e in range(N_EXPERTS):
        g_e = jnp.sum(jnp.where(top_i == e, gates, 0.0), axis=-1)
        out = out + g_e[..., None] * swiglu(x, w1[e], w3[e], w2[e])
    return out.astype(x.dtype)

def run_trunk(x, kv, lru_conv0, lru_h0, ssd_conv0, ssd_h0, p):
    ks, vs, lru_h, lru_cv, ssm_h, ssd_cv = [], [], [], [], [], []
    for layer in range(DEPTH):
        i = layer // 2
        if layer % 2 == 0:
            kv_i = None if kv is None else (kv[0][i], kv[1][i], kv[2])
            mix, k, v, h, cv = even_mixer(x, kv_i, lru_conv0[i], lru_h0[i], p['w_in_even'][i], p['lru_conv_w'][i],
                                          p['lru_conv_b'][i], p['lru_w_a'][i], p['lru_b_a'][i], p['lru_w_x'][i],
                                          p['lru_b_x'][i], p['lru_lambda'][i], p['w_out_even'][i])
            ks.append(k)
            vs.append(v)
            lru_h.append(h)
            lru_cv.append(cv)
            x = layer_norm(DN_ALPHA * x + mix, p['ln_mix_g'][layer], p['ln_mix_b'][layer])
            ff = swiglu(x, p['ffn_w1'][i], p['ffn_w3'][i], p['ffn_w2'][i])
        else:
            mix, h, cv = ssd_mixer(x, ssd_conv0[i], ssd_h0[i], p['ssd_w_in'][i], p['ssd_conv_w'][i], p['ssd_conv_b'][i],
                                   p['ssd_dt_bias'][i], p['ssd_a_log'][i], p['ssd_d'][i], p['ssd_norm_g'][i],
                                   p['ssd_w_out'][i])
            ssm_h.append(h)
            ssd_cv.append(cv)
            x = layer_norm(DN_ALPHA * x + mix, p['ln_mix_g'][layer], p['ln_mix_b'][layer])
            ff = moe_swiglu(x, p['moe_router'][i], p['moe_w1'][i], p['moe_w3'][i], p['moe_w2'][i])
        x = layer_norm(DN_ALPHA * x + ff, p['ln_ffn_g'][layer], p['ln_ffn_b'][layer])
    return (x, jnp.stack(ks), jnp.stack(vs), jnp.stack(lru_h), jnp.stack(lru_cv),
            jnp.stack(ssm_h), jnp.stack(ssd_cv))

def setup_inputs(seed: int = 0) -> dict:
    key = jax.random.key(seed)
    keys = iter(jax.random.split(key, 64))

    def nrm(shape, scale):
        return jax.random.normal(next(keys), shape, F32) * scale

    def unif(shape, lo, hi):
        return jax.random.uniform(next(keys), shape, F32, lo, hi)

    n_pages = PAST_LEN // PAGE_SIZE
    n_pool = (DEC_BATCH * n_pages * 5) // 4
    perm = jax.random.permutation(next(keys), n_pool)
    page_table = perm[:DEC_BATCH * n_pages].reshape(DEC_BATCH, n_pages).astype(jnp.int32)
    a0 = unif((N_EVEN, LRU_BLOCKS, LRU_BLOCK_DIM), 0.9, 0.999)
    dt0 = jnp.exp(unif((N_ODD, SSD_HEADS), math.log(1e-3), math.log(1e-1)))
    return {
        'x_prompt': nrm((BATCH, SEQ, D_MODEL), 1.0),
        'x_sample': nrm((DEC_BATCH, DEC_SEQ, D_MODEL), 1.0),
        'cache_k': nrm((N_EVEN, n_pool, PAGE_SIZE, ATT_HEADS, HEAD_DIM), 1.0),
        'cache_v': nrm((N_EVEN, n_pool, PAGE_SIZE, ATT_HEADS, HEAD_DIM), 1.0),
        'page_table': page_table,
        'state_lru_h': nrm((N_EVEN, DEC_BATCH, LRU_WIDTH), 0.5),
        'state_lru_conv': nrm((N_EVEN, DEC_BATCH, CONV_W - 1, LRU_WIDTH), 1.0),
        'state_ssm': nrm((N_ODD, DEC_BATCH, SSD_HEADS, SSD_HEAD_DIM, SSD_STATE), 0.1),
        'state_ssd_conv': nrm((N_ODD, DEC_BATCH, CONV_W - 1, SSD_CONV_DIM), 1.0),
        'w_in_even': nrm((N_EVEN, D_MODEL, EVEN_IN), D_MODEL ** -0.5),
        'lru_conv_w': nrm((N_EVEN, CONV_W, LRU_WIDTH), CONV_W ** -0.5),
        'lru_conv_b': nrm((N_EVEN, LRU_WIDTH), 0.02),
        'lru_w_a': nrm((N_EVEN, LRU_BLOCKS, LRU_BLOCK_DIM, LRU_BLOCK_DIM), LRU_BLOCK_DIM ** -0.5),
        'lru_b_a': nrm((N_EVEN, LRU_BLOCKS, LRU_BLOCK_DIM), 0.02),
        'lru_w_x': nrm((N_EVEN, LRU_BLOCKS, LRU_BLOCK_DIM, LRU_BLOCK_DIM), LRU_BLOCK_DIM ** -0.5),
        'lru_b_x': nrm((N_EVEN, LRU_BLOCKS, LRU_BLOCK_DIM), 0.02),
        'lru_lambda': jnp.log(a0) - jnp.log1p(-a0),
        'w_out_even': nrm((N_EVEN, EVEN_MIX, D_MODEL), EVEN_MIX ** -0.5 * DN_BETA),
        'ssd_w_in': nrm((N_ODD, D_MODEL, SSD_IN), D_MODEL ** -0.5),
        'ssd_conv_w': nrm((N_ODD, CONV_W, SSD_CONV_DIM), CONV_W ** -0.5),
        'ssd_conv_b': nrm((N_ODD, SSD_CONV_DIM), 0.02),
        'ssd_dt_bias': dt0 + jnp.log(-jnp.expm1(-dt0)),
        'ssd_a_log': jnp.log(unif((N_ODD, SSD_HEADS), 1.0, 16.0)),
        'ssd_d': 1.0 + nrm((N_ODD, SSD_HEADS), 0.02),
        'ssd_norm_g': 1.0 + nrm((N_ODD, SSD_INNER), 0.02),
        'ssd_w_out': nrm((N_ODD, SSD_INNER, D_MODEL), SSD_INNER ** -0.5 * DN_BETA),
        'ffn_w1': nrm((N_EVEN, D_MODEL, D_FF), D_MODEL ** -0.5),
        'ffn_w3': nrm((N_EVEN, D_MODEL, D_FF), D_MODEL ** -0.5),
        'ffn_w2': nrm((N_EVEN, D_FF, D_MODEL), D_FF ** -0.5 * DN_BETA),
        'moe_router': nrm((N_ODD, D_MODEL, N_EXPERTS), D_MODEL ** -0.5),
        'moe_w1': nrm((N_ODD, N_EXPERTS, D_MODEL, D_FF_EXPERT), D_MODEL ** -0.5),
        'moe_w3': nrm((N_ODD, N_EXPERTS, D_MODEL, D_FF_EXPERT), D_MODEL ** -0.5),
        'moe_w2': nrm((N_ODD, N_EXPERTS, D_FF_EXPERT, D_MODEL), D_FF_EXPERT ** -0.5 * DN_BETA),
        'ln_mix_g': 1.0 + nrm((DEPTH, D_MODEL), 0.02),
        'ln_mix_b': nrm((DEPTH, D_MODEL), 0.02),
        'ln_ffn_g': 1.0 + nrm((DEPTH, D_MODEL), 0.02),
        'ln_ffn_b': nrm((DEPTH, D_MODEL), 0.02),
    }

def reference(x_prompt, x_sample, cache_k, cache_v, page_table, state_lru_h, state_lru_conv, state_ssm,
              state_ssd_conv, w_in_even, lru_conv_w, lru_conv_b, lru_w_a, lru_b_a, lru_w_x, lru_b_x, lru_lambda,
              w_out_even, ssd_w_in, ssd_conv_w, ssd_conv_b, ssd_dt_bias, ssd_a_log, ssd_d, ssd_norm_g, ssd_w_out,
              ffn_w1, ffn_w3, ffn_w2, moe_router, moe_w1, moe_w3, moe_w2, ln_mix_g, ln_mix_b, ln_ffn_g, ln_ffn_b):
    p = dict(w_in_even=w_in_even, lru_conv_w=lru_conv_w, lru_conv_b=lru_conv_b, lru_w_a=lru_w_a,
             lru_b_a=lru_b_a, lru_w_x=lru_w_x, lru_b_x=lru_b_x, lru_lambda=lru_lambda, w_out_even=w_out_even,
             ssd_w_in=ssd_w_in, ssd_conv_w=ssd_conv_w, ssd_conv_b=ssd_conv_b, ssd_dt_bias=ssd_dt_bias,
             ssd_a_log=ssd_a_log, ssd_d=ssd_d, ssd_norm_g=ssd_norm_g, ssd_w_out=ssd_w_out,
             ffn_w1=ffn_w1, ffn_w3=ffn_w3, ffn_w2=ffn_w2, moe_router=moe_router, moe_w1=moe_w1,
             moe_w3=moe_w3, moe_w2=moe_w2, ln_mix_g=ln_mix_g, ln_mix_b=ln_mix_b, ln_ffn_g=ln_ffn_g,
             ln_ffn_b=ln_ffn_b)
    bp = x_prompt.shape[0]
    dtp = x_prompt.dtype
    lru_conv0 = jnp.zeros((N_EVEN, bp, CONV_W - 1, LRU_WIDTH), dtp)
    lru_h0 = jnp.zeros((N_EVEN, bp, LRU_WIDTH), dtp)
    ssd_conv0 = jnp.zeros((N_ODD, bp, CONV_W - 1, SSD_CONV_DIM), dtp)
    ssd_h0 = jnp.zeros((N_ODD, bp, SSD_HEADS, SSD_HEAD_DIM, SSD_STATE), dtp)
    y_prompt, k_prompt, v_prompt, lru_h_prompt, lru_conv_prompt, ssm_prompt, ssd_conv_prompt = run_trunk(
        x_prompt, None, lru_conv0, lru_h0, ssd_conv0, ssd_h0, p)
    y_sample, k_sample, v_sample, lru_h_sample, lru_conv_sample, ssm_sample, ssd_conv_sample = run_trunk(
        x_sample, (cache_k, cache_v, page_table), state_lru_conv, state_lru_h, state_ssd_conv, state_ssm, p)
    return (y_prompt, y_sample, k_prompt, v_prompt, k_sample, v_sample, lru_h_prompt, lru_h_sample,
            lru_conv_prompt, lru_conv_sample, ssm_prompt, ssm_sample, ssd_conv_prompt, ssd_conv_sample)


_drawn_inputs = setup_inputs


def setup_inputs(seed=0):
    import zlib

    import numpy as np

    out = dict(_drawn_inputs(seed))
    spreads = {}
    factors = {'cache_k': 2.897,
     'cache_v': 2.831,
     'lru_b_a': 8.0,
     'lru_b_x': 7.539,
     'ssd_d': 3.95,
     'ssd_norm_g': 6.278}
    for name, (base, spread) in spreads.items():
        noise = np.random.default_rng([zlib.crc32(name.encode()), seed]).standard_normal(out[name].shape)
        drawn = base * np.exp(spread * noise) if base else spread * noise
        out[name] = __import__('jax').numpy.asarray(drawn.astype(out[name].dtype))
    for name, factor in factors.items():
        out[name] = (out[name] * factor).astype(out[name].dtype)
    return out
```

```python
from contextlib import ExitStack

import numpy as np

import concourse.bass as bass
from concourse import mybir

F32 = mybir.dt.float32
I32 = mybir.dt.int32
ALU = mybir.AluOpType
ACT = mybir.ActivationFunctionType
AX = mybir.AxisListType.X
ds = bass.ds

P = 128
D = 1024
KD = D // P
SEQ, DEC_B, DEC_T = 512, 8, 8
NS = DEC_B * DEC_T
T = SEQ + NS
HALF = T // 2
NCH = SEQ // P
CONV_W = 4
HIST = CONV_W - 1
PADT = HIST + SEQ + DEC_B * (HIST + DEC_T)
HEADS, HD = 8, 64
AW = HEADS * HD
AT = AW // P
LT = 512 // P
PAGE, NPAGES, NPOOL = 128, 8, 80
QUAD = 4
BLK = 256
NBLK = NPAGES * PAGE // BLK
FF, FT = 2816, 2816 // P
SG, SH, SN = 8, 32, 128
XT, BC = 2048 // P, 8
XBC = XT + 2 * BC
SCONV = XBC * P
SIN = 2048 + SCONV + SH
NE, FE, FET = 8, 1408, 1408 // P
ALPHA = float(4 ** 0.25)
LN_EPS, RMS_EPS = 1e-5, 1e-6
NEG = -1e30
SLOTS = 4
KMAX = 11
CW = 2 * P
MOE_SLOTS = 5

C_L1 = 0
C_L2 = C_L1 + 10
C_L3 = C_L2 + KD // 2
C_L4 = C_L3 + FT
C_XBC = C_L4 + KD
C_DT = C_XBC + XBC // 2
C_Z = C_DT + 1
C_L6 = C_Z + XT // 2
C_MOE = C_L6 + KD
PER_E = FET + KD // 2


class Chain:

    def __init__(self, eng, sem):
        self.eng, self.sem, self.n, self.turn = eng, sem, 0, 0

    def __call__(self, ins):
        ins.then_inc(self.sem, 1)
        self.n += 1
        self.eng.wait_ge(self.sem, self.n + self.turn)

    def enter(self, i, per):
        self.per, self.n0, self.turn = per, self.n, i * per

    def leave(self, turns):
        assert self.n - self.n0 == self.per
        self.n, self.turn = self.n0 + turns * self.per, 0


def build(nc, I, O):
    ctx = ExitStack()
    with ctx:
        def sb(name, shape, dt=F32):
            return ctx.enter_context(nc.sbuf_tensor(name, shape, dt))

        def sem(name):
            return ctx.enter_context(nc.semaphore(name))

        ring = sb("ring", [P, SLOTS, KMAX, CW])
        xT = sb("xT", [P, KD, T])
        par = sb("par", [P, 3, P])
        lru_h0 = sb("lru_h0", [P, LT, DEC_B])
        lru_hist = sb("lru_hist", [P, LT, DEC_B * HIST])
        ssd_hist = sb("ssd_hist", [P, XBC, DEC_B * HIST])
        ssd_tail = sb("ssd_tail", [P, XBC, HIST + DEC_B * HIST])
        lru_tail = sb("lru_tail", [P, LT, 36])
        ident = sb("ident", [P, P])
        ones = sb("ones", [P, P])
        qk_mask = sb("qk_mask", [P, P])
        sl_mask = sb("sl_mask", [P, P])
        seq_mask = sb("seq_mask", [NS, NS])
        seq_maskT = sb("seq_maskT", [NS, NS])
        expand = sb("expand", [NS, 4, P])
        of_seq = sb("of_seq", [NS, DEC_B])
        run_row = sb("run_row", [SH, T])
        tri = sb("tri", [P, 8, 8])
        gate_w = sb("gate_w", [P, 2, LT, P])
        router = sb("router", [P, KD, NE])
        dt_par = sb("dt_par", [SH, 4])
        eps = sb("eps", [P, 2])
        pages = sb("pages", [1, DEC_B * NPAGES], I32)
        stat = sb("stat", [P, 160])
        ARENA = nc.sbuf_bytes_remaining // 4 - 16
        arena = sb("arena", [P, ARENA])
        ps = ctx.enter_context(nc.psum_tensor("ps", [P, 8, 512], F32))

        def at(off, *dims):
            n = int(np.prod(dims))
            assert off + n <= ARENA, (off, dims, ARENA)
            v = arena[:, off:off + n]
            if len(dims) == 2:
                return v.rearrange("p (a b) -> p a b", a=dims[0])
            if len(dims) == 3:
                return v.rearrange("p (a b c) -> p a b c", a=dims[0], b=dims[1])
            return v

        proj = at(0, 20, T)
        cat = at(11520, 8, T)
        xin = at(16128, 5, D)
        shist_in = at(21248, SCONV)
        par_in = at(25344, 3, P)
        h0_in = at(25728, 512)
        lhist_in = at(26240, 512)
        u_pad = at(16128, LT, PADT)
        uc = at(18540, LT, T)
        u_acc = at(28356, PADT)
        lru_a = at(21444, LT * T)
        lru_t = at(23748, LT * T)
        lru_i = at(26052, LT * T)
        qx = at(6912, AT, DEC_B, NS)
        k_tok = at(8960, 5, AW)
        v_tok = at(16128, 5, AW)
        kv = [at(18688 + 2048 * n, QUAD, AW) for n in range(4)]
        pp = at(26880, 2, 512)
        ppt = at(27904, 2, 512)
        ks_T = at(28928, AT, NS)
        kt = [at(2048 * n, AT, QUAD * PAGE) for n in range(3)]
        p_s = at(29184, NPAGES * PAGE + NS)
        p_sT = at(30272, 9, P)
        hid = at(0, FT, T)
        sq = at(15552, KD, T)
        std = at(20160, T)
        rstd = at(20736, T)
        xbc = at(0, XBC, T)
        raw = at(18432, 4, PADT)
        acc = at(20844, 2, PADT)
        rows = at(18432, 4, T)
        DTR, CSR, ECR, WDR = range(4)
        tmpr = at(21472, 5, T)
        tok = at(20736, 3, 5 * SH)
        dec_p = at(21216, SH * NCH)
        dec_s = at(21344, XT, DEC_B)
        b_tok = at(21472, 5, P)
        x_dt = at(22112, 5, 256)
        x_w = at(23392, 5, 256)
        state = at(24672, NCH, 256)
        b_seq = at(25696, DEC_B, P)
        h0n = at(26720, DEC_B, P)
        h0t = at(27744, DEC_B, P)
        exs = at(28768, T)
        e_buf = at(29344, T)
        m_buf = at(29920, T)
        t_buf = at(30496, T)
        d_exp = stat[:, 0:XT]
        st_out = at(31072, 2, P)
        z_s = at(18432, 2, T)
        z_q = at(19584, 2, T)
        z_r = at(20736, T)
        z_i = at(21312, T)
        e_hid = at(0, FET, T)
        yacc = at(6336, KD, T)
        gb = at(10944, NE, T)
        slot4 = at(21312, KMAX, CW)
        g_w = at(24128, 40 * 8 * 3)
        gT = at(25088, T)
        tail_s = at(26000, SCONV)
        tail_l = at(30096, 512)
        y_out = at(0, 5, D)

        conv_w_s = par[:, 0, :].rearrange("p (w t) -> p w t", w=CONV_W)
        conv_b_s = par[:, 1, 0:32]
        norm_g = par[:, 1, 32:48]
        ln_g = [par[:, 1, 48:56], par[:, 1, 80:88], par[:, 1, 56:64], par[:, 1, 88:96]]
        ln_b = [par[:, 1, 64:72], par[:, 1, 96:104], par[:, 1, 72:80], par[:, 1, 104:112]]
        conv_w_l = par[:, 2, 0:16].rearrange("p (w t) -> p w t", w=CONV_W)
        conv_b_l = par[:, 2, 16:20]
        b_gate = [par[:, 2, 20:24], par[:, 2, 24:28]]
        lam = par[:, 2, 28:32]

        loaded = [sem(f"loaded{s}") for s in range(SLOTS)]
        moe_loaded = [sem(f"moe_loaded{s}") for s in range(MOE_SLOTS)]
        used = sem("used")
        in_x, in_par, in_hist = sem("in_x"), sem("in_par"), sem("in_hist")
        in_gatew, in_small, in_router, in_pages = sem("in_gatew"), sem("in_small"), sem("in_router"), sem("in_pages")
        const_ok, pool_c, dve_c, act_c = sem("const_ok"), sem("pool_c"), sem("dve_c"), sem("act_c")
        x_tr, x_up = sem("x_tr"), sem("x_up")
        p_tr, p_up = sem("p_tr"), sem("p_up")
        stages = ["l1", "l2", "l3", "l4", "xb", "dt", "z", "l6", "eu", "ed"]
        first = dict(l1=C_L1, l2=C_L2, l3=C_L3, l4=C_L4, xb=C_XBC, dt=C_DT, z=C_Z, l6=C_L6)
        per_unit = dict(l4=2, l6=2)

        def done(stage, n):
            return SLOTS + first[stage] + per_unit.get(stage, 1) * (n + 1)

        free = {s: sem(f"free_{s}") for s in stages}
        free_act1 = sem("free_act1")
        silu_ok = {s: sem(f"silu_{s}") for s in ("l3", "eu")}
        ln_ready = sem("ln_ready")
        ln_mu, ln_c, ln_sq, ln_var, ln_std, ln_n, ln_out = [sem(f"ln_{n}") for n in ("mu", "c", "sq", "var", "std", "n", "out")]
        uc_ok, gr_mm, gr_ok, gi_mm, gi_ok = [sem(n) for n in ("uc_ok", "gr_mm", "gr_ok", "gi_mm", "gi_ok")]
        lam_e, lam_u, lam_l = sem("lam_e"), sem("lam_u"), sem("lam_l")
        la_ok, a_ok, a2_ok, s_ok, g_ok, rec_ok = [sem(n) for n in ("la_ok", "a_ok", "a2_ok", "s_ok", "g_ok", "rec_ok")]
        lru_end = sem("lru_end")
        kvt_tr, kvt_up, kvt_up_a, kv_out = sem("kvt_tr"), sem("kvt_up"), sem("kvt_up_a"), sem("kv_out")
        qx_ok = sem("qx_ok")
        sc_mm, mx_ok, ex_ok, pn_ok, pt_mm, pt_ok, o_mm, o_up = [sem(n) for n in ("sc_mm", "mx_ok", "ex_ok", "pn_ok", "pt_mm", "pt_ok", "o_mm", "o_up")]
        kv_in = [sem(f"kv_in{n}") for n in range(4)]
        kt_mm, kt_dve, kt_act, qs_mm = sem("kt_mm"), sem("kt_dve"), sem("kt_act"), sem("qs_mm")
        s_bias, s_ex, s_pn, s_ptm, s_ptu, s_o, s_ou = [sem(n) for n in ("s_bias", "s_ex", "s_pn", "s_ptm", "s_ptu", "s_o", "s_ou")]
        cv_raw, cv_y, cv_s = sem("cv_raw"), sem("cv_y"), sem("cv_s")
        ap_e, dt_a, dt_e, dt_u, dt_l, cs_ok, ec_ok, row_ok = [sem(n) for n in ("ap_e", "dt_a", "dt_e", "dt_u", "dt_l", "cs_ok", "ec_ok", "row_ok")]
        dg_ok, tk_mm, tk_up = sem("dg_ok"), sem("tk_mm"), sem("tk_up")
        g_mm, g_up, g_up_a, st_mm, st_up = [sem(n) for n in ("g_mm", "g_up", "g_up_a", "st_mm", "st_up")]
        h0_in_s, h0_tr, h0_up = sem("h0_in_s"), sem("h0_tr"), sem("h0_up")
        yi_mm, ex_up, cs_mm, e_ok, m_ok, yt_mm, y_ok = [sem(n) for n in ("yi_mm", "ex_up", "cs_mm", "e_ok", "m_ok", "yt_mm", "y_ok")]
        ss_mm, ss_ok, ss_out = sem("ss_mm"), sem("ss_ok"), sem("ss_out")
        fs_mm, fs_up, fs_out = sem("fs_mm"), sem("fs_up"), sem("fs_out")
        z_gate, z_sqd, z_sum, z_rt, z_ok = [sem(n) for n in ("z_gate", "z_sqd", "z_sum", "z_rt", "z_ok")]
        tl_mm, tl_up, tl_out = sem("tl_mm"), sem("tl_up"), sem("tl_out")
        rt_mm, rt_d, rt_e, rt_g, gt_mm, gt_up, gb_mm, gb_up = [sem(n) for n in ("rt_mm", "rt_d", "rt_e", "rt_g", "gt_mm", "gt_up", "gb_mm", "gb_up")]
        out_mm, out_up, out_st = sem("out_mm"), sem("out_up"), sem("out_st")

        block = ctx.enter_context(nc.Block())

        def cols(w, k0, nk, c0):
            return w[k0 * P:(k0 + nk) * P, :].rearrange("(k p) n -> p k n", p=P)[:, :, ds(c0, CW)]

        @block.sync
        def _(sp):
            for c in range(NCH):
                sp.dma_start(xin[:, c, :], I["x_prompt"][0, c * P:(c + 1) * P, :]).then_inc(in_x, 16)
            sp.dma_start(xin[0:NS, NCH, :], I["x_sample"].rearrange("b t d -> (b t) d")).then_inc(in_x, 16)

            def load(c, i, parts):
                slot = c % SLOTS
                sp.wait_ge(used, c + 1 + SLOTS * i)
                for dst, src in parts(ring[:, slot]):
                    sp.dma_start(dst, src).then_inc(loaded[slot], 16)

            def pair(w, k0, nk, c0):
                h = nk // 2
                return lambda s: [(s[:, 0:h, :], cols(w, k0, h, c0)), (s[:, h:nk, :], cols(w, k0 + h, nk - h, c0))]

            def up(w1, w3, c0):
                def tile(w):
                    return w.rearrange("(k p) n -> p k n", p=P)[:, :, ds(c0, P)]
                return lambda s: [(s[:, 0:KD, 0:P], tile(w1)), (s[:, 0:KD, P:CW], tile(w3))]

            w = I["w_in_even"][0]
            with sp.Fori(0, 2) as i:
                for j in range(SLOTS):
                    load(C_L1 + j, i, pair(w, 0, KD, (i * SLOTS + j) * CW))
            for j in range(8, 10):
                load(C_L1 + j, 0, pair(w, 0, KD, j * CW))

            sp.wait_ge(in_pages, 16)
            sp.wait_ge(lru_end, 1)
            for pr in range(DEC_B // 2):
                for which, cache in ((0, I["cache_k"]), (1, I["cache_v"])):
                    for q in range(4):
                        if which == 1:
                            sp.wait_ge(kt_mm, 4 * (4 * pr + q + 1))
                        elif pr > 0:
                            sp.wait_ge(s_o, 2 * (pr - 1) + q // 2 + 1)
                        for pg in range(QUAD):
                            at_page = (2 * pr + q // 2) * NPAGES + (q % 2) * QUAD + pg
                            page = sp.value_load(pages[0:1, at_page:at_page + 1], min_val=0, max_val=NPOOL - 1)
                            sp.dma_start(kv[q][:, pg, :], cache[0][page].rearrange("t h d -> t (h d)")).then_inc(kv_in[q], 16)
            w = I["w_out_even"][0]
            for j in range(KD // 2):
                load(C_L2 + j, 0, pair(w, 0, KD, j * CW))
            w1, w3 = I["ffn_w1"][0], I["ffn_w3"][0]
            with sp.Fori(0, FT // SLOTS) as i:
                for j in range(SLOTS):
                    load(C_L3 + j, i, up(w1, w3, (i * SLOTS + j) * P))
            for j in range(FT // SLOTS * SLOTS, FT):
                load(C_L3 + j, 0, up(w1, w3, j * P))
            w = I["ffn_w2"][0]
            for j in range(KD // 2):
                for h in range(2):
                    load(C_L4 + 2 * j + h, 0, pair(w, KMAX * h, KMAX, j * CW))
            w = I["ssd_w_in"][0]
            with sp.Fori(0, XBC // 2 // SLOTS) as i:
                for j in range(SLOTS):
                    load(C_XBC + j, i, pair(w, 0, KD, (i * SLOTS + j) * CW + 2048))
            load(C_DT, 0, lambda s: [
                (s[:, 4 * h:4 * h + 4, 0:SH],
                 w[4 * h * P:(4 * h + 4) * P, 2048 + SCONV:SIN].rearrange("(k p) n -> p k n", p=P)) for h in range(2)])
            with sp.Fori(0, XT // 2 // SLOTS) as i:
                for j in range(SLOTS):
                    load(C_Z + j, i, pair(w, 0, KD, (i * SLOTS + j) * CW))
            w = I["ssd_w_out"][0]
            for j in range(KD // 2):
                for h in range(2):
                    load(C_L6 + 2 * j + h, 0, pair(w, 8 * h, 8, j * CW))
            moe_slot = [slot4] + [ring[:, (C_MOE + m) % SLOTS] for m in range(SLOTS)]
            with sp.Fori(0, NE) as e:
                w1, w3, w2 = (I[n][0][e] for n in ("moe_w1", "moe_w3", "moe_w2"))
                for m in range(PER_E):
                    s = m % MOE_SLOTS
                    sp.wait_ge(used, C_MOE + m + PER_E * e)
                    parts = up(w1, w3, m * P) if m < FET else pair(w2, 0, FET, (m - FET) * CW)
                    for dst, src in parts(moe_slot[s]):
                        sp.dma_start(dst, src).then_inc(moe_loaded[s], 16)

        @block.gpsimd
        def _(pool):
            def rowsof(ap, n):
                return ap.rearrange("o (t p) -> (o t) p", p=P)
            ld = pool.dma_start
            ld(par_in[:, 0, :], I["ssd_conv_w"][0].rearrange("w (t p) -> (w t) p", p=P)).then_inc(in_par, 16)
            for lo, name in ((0, "ssd_conv_b"), (32, "ssd_norm_g"), (48, "ln_mix_g"), (64, "ln_mix_b"),
                             (80, "ln_ffn_g"), (96, "ln_ffn_b")):
                src = rowsof(I[name], 0)
                ld(par_in[lo:lo + src.shape[0], 1, :], src).then_inc(in_par, 16)
            ld(par_in[0:16, 2, :], I["lru_conv_w"][0].rearrange("w (t p) -> (w t) p", p=P)).then_inc(in_par, 16)
            ld(par_in[16:20, 2, :], rowsof(I["lru_conv_b"], 0)).then_inc(in_par, 16)
            for lo, name in ((20, "lru_b_a"), (24, "lru_b_x"), (28, "lru_lambda")):
                ld(par_in[lo:lo + 4, 2, :], I[name][0].rearrange("(t h) d -> t (h d)", h=2)).then_inc(in_par, 16)
            ld(h0_in[0:DEC_B, :], I["state_lru_h"][0]).then_inc(in_hist, 16)
            ld(lhist_in[0:DEC_B * HIST, :], I["state_lru_conv"][0].rearrange("b t d -> (b t) d")).then_inc(in_hist, 16)
            ld(shist_in[0:DEC_B * HIST, :], I["state_ssd_conv"][0].rearrange("b t d -> (b t) d")).then_inc(in_hist, 16)
            ld(pages[0:1, :], I["page_table"].rearrange("b (o n) -> o (b n)", o=1)).then_inc(in_pages, 16)
            ld(router[:], I["moe_router"][0].rearrange("(k p) e -> p k e", p=P)).then_inc(in_router, 16)
            for n, name in enumerate(("ssd_dt_bias", "ssd_a_log", "ssd_d")):
                ld(dt_par[:, n:n + 1], I[name].rearrange("o h -> h o")).then_inc(in_small, 16)

            link = Chain(pool, pool_c)
            pool.memset(ident[:], 0.0)
            pool.memset(ones[:], 1.0)
            pool.memset(qk_mask[:], 0.0)
            pool.memset(sl_mask[:], 0.0)
            pool.memset(seq_mask[:], 0.0)
            pool.memset(seq_maskT[:], 0.0)
            pool.memset(expand[:], 0.0)
            pool.memset(of_seq[:], 1.0)
            pool.memset(run_row[:], 1.0)
            pool.memset(tri[:], 0.0)
            pool.memset(eps[:, 0:1], LN_EPS)
            pool.memset(eps[:, 1:2], RMS_EPS)
            link(pool.memset(gate_w[:], 0.0))
            for hh in range(2):
                for n, name in enumerate(("lru_w_a", "lru_w_x")):
                    src = I[name][0].rearrange("(t h) d e -> h d t e", h=2)[hh]
                    ld(gate_w[64 * hh:64 * hh + 64, n, :, 64 * hh:64 * hh + 64], src).then_inc(in_gatew, 16)
            sel = pool.affine_select
            sel(out=ident[:], in_=ident[:], compare_op=ALU.not_equal, fill=1.0, base=0, pattern=[[-1, P]], channel_multiplier=1)
            sel(out=qk_mask[:], in_=qk_mask[:], compare_op=ALU.is_ge, fill=NEG, base=0, pattern=[[-1, P]], channel_multiplier=1)
            sel(out=sl_mask[:], in_=sl_mask[:], compare_op=ALU.is_ge, fill=NEG, base=0, pattern=[[1, P]], channel_multiplier=-1)
            sm = seq_mask[:].rearrange("p (b t) -> p b t", t=DEC_T)
            smt = seq_maskT[:].rearrange("p (b t) -> p b t", t=DEC_T)
            sel(out=sm, in_=sm, compare_op=ALU.is_ge, fill=NEG, base=0, pattern=[[DEC_T, DEC_B], [1, DEC_T]], channel_multiplier=-1)
            sel(out=smt, in_=smt, compare_op=ALU.is_ge, fill=NEG, base=0, pattern=[[-DEC_T, DEC_B], [-1, DEC_T]], channel_multiplier=1)
            sel(out=of_seq[:], in_=of_seq[:], compare_op=ALU.is_ge, fill=0.0, base=0, pattern=[[-DEC_T, DEC_B]], channel_multiplier=1)
            for pr in range(4):
                v = expand[:, pr, :].rearrange("p (b h q) -> p b h q", b=2, h=HEADS)
                sel(out=v, in_=v, compare_op=ALU.not_equal, fill=1.0, base=-2 * DEC_T * pr,
                    pattern=[[-DEC_T, 2], [0, HEADS], [-1, DEC_T]], channel_multiplier=1)
            for e in range(1, NE):
                pool.memset(tri[:, e, 0:e], 1.0)
            pool.memset(run_row[:, 0:SEQ:P], 0.0)
            link(pool.memset(run_row[:, SEQ:T:DEC_T], 0.0))
            sel(out=sm, in_=sm, compare_op=ALU.is_ge, fill=NEG, base=0, pattern=[[-DEC_T, DEC_B], [0, DEC_T]], channel_multiplier=1)
            sel(out=smt, in_=smt, compare_op=ALU.is_ge, fill=NEG, base=DEC_T - 1, pattern=[[DEC_T, DEC_B], [0, DEC_T]], channel_multiplier=-1)
            sel(out=of_seq[:], in_=of_seq[:], compare_op=ALU.is_ge, fill=0.0, base=DEC_T - 1, pattern=[[DEC_T, DEC_B]],
                channel_multiplier=-1).then_inc(const_ok, 1)

            st = pool.dma_start
            pool.wait_ge(kvt_up, 8)
            pool.wait_ge(kvt_up_a, 8)
            for t_, pn, sn in ((k_tok, "k_prompt", "k_sample"), (v_tok, "v_prompt", "v_sample")):
                dst = O[pn][0, 0].rearrange("(c p) h d -> p c (h d)", p=P)
                st(dst, t_[:, 0:NCH, :]).then_inc(kv_out, 16)
                st(O[sn][0].rearrange("b t h d -> (b t) (h d)"), t_[0:NS, NCH, :]).then_inc(kv_out, 16)
            for g in range(SG):
                for j in range(2):
                    t = 2 * g + j
                    if t >= 1:
                        pool.wait_ge(ss_out, 16 * t)
                    if t == 0:
                        pool.wait_ge(row_ok, 1)
                    pool.dma_start(h0n[:], I["state_ssm"][0].rearrange("b (t h) p n -> t (h p) b n", h=2)[t]).then_inc(h0_in_s, 16)
                    pool.wait_ge(ss_ok, t + 1)
                    st(O["ssm_sample"][0].rearrange("b (t h) p n -> t (h p) b n", h=2)[t], h0n[:]).then_inc(ss_out, 16)
                pool.wait_ge(fs_up, g + 1)
                st(O["ssm_prompt"][0, 0].rearrange("(g t h) p n -> g (h p) t n", h=2, t=2)[g], st_out[:]).then_inc(fs_out, 16)
            pool.wait_ge(tl_up, 9)
            st(O["ssd_conv_prompt"][0, 0], tail_s[0:HIST, :]).then_inc(tl_out, 16)
            st(O["ssd_conv_sample"][0].rearrange("b t d -> (b t) d"), tail_s[HIST:HIST + DEC_B * HIST, :]).then_inc(tl_out, 16)
            st(O["lru_h_prompt"][0], tail_l[0:1, :]).then_inc(tl_out, 16)
            st(O["lru_h_sample"][0], tail_l[1:9, :]).then_inc(tl_out, 16)
            st(O["lru_conv_prompt"][0, 0], tail_l[9:12, :]).then_inc(tl_out, 16)
            st(O["lru_conv_sample"][0].rearrange("b t d -> (b t) d"), tail_l[12:36, :]).then_inc(tl_out, 16)
            for c in range(NCH + 1):
                pool.wait_ge(out_up, 2 * (c + 1))
                if c < NCH:
                    st(O["y_prompt"][0, c * P:(c + 1) * P, :], y_out[:, c, :]).then_inc(out_st, 16)
                else:
                    st(O["y_sample"].rearrange("b t d -> (b t) d"), y_out[0:NS, c, :]).then_inc(out_st, 16)
            pool.wait_ge(kv_out, 64)
            pool.wait_ge(ss_out, 16 * XT)
            pool.wait_ge(fs_out, 16 * SG)
            pool.wait_ge(tl_out, 96)
            pool.wait_ge(out_st, 16 * 5)

        def of_samples(a):
            return a[:, SEQ + HIST:].rearrange("p (b t) -> p b t", t=HIST + DEC_T)[:, :, 0:DEC_T]

        CHUNKS = [(P, c * P) for c in range(NCH)] + [(NS, SEQ)]

        @block.tensor
        def _(pe):
            mmul, tr = pe.matmul, pe.transpose
            pe.sem_inc(used, SLOTS)

            def unit(stage, n, bank, parts, X, M=P):
                pe.wait_ge(free[stage], n + 1)
                if stage == "l1":
                    pe.wait_ge(free_act1, n + 1)
                total = sum(p[4] for p in parts)
                for s, v, _, _, _ in parts:
                    pe.wait_ge(s, v)
                tiles = 1 if M < P else 2
                for q, (_, _, slot, k0, nk) in enumerate(parts):
                    for j in range(tiles):
                        for k in range(nk):
                            for h in range(2):
                                last = mmul(ps[0:M, bank + 2 * j + h, 0:HALF], slot[:, k, j * P:j * P + M],
                                            X[:, k0 + k, HALF * h:HALF * (h + 1)],
                                            start=(k0 + k == 0), stop=(k0 + k == total - 1))
                    last.then_inc(used, 1)

            def part(c, i=0, k0=0, nk=KD):
                return (loaded[c % SLOTS], 32 * (c // SLOTS + 1 + i), ring[:, c % SLOTS], k0, nk)

            def linear(stage, c0, units, X):
                turns = units // SLOTS
                with pe.Fori(0, turns) as i:
                    for j in range(SLOTS):
                        unit(stage, SLOTS * i + j, 4 * (j % 2), [part(c0 + j, i)], X)
                for j in range(turns * SLOTS, units):
                    unit(stage, j, 4 * (j % 2), [part(c0 + j)], X)

            def layer_norm(n):
                pe.wait_ge(ln_ready, n + 1)
                for k in range(KD):
                    for h in range(2):
                        last = mmul(ps[:, h, 0:HALF], ones[:], xT[:, k, HALF * h:HALF * (h + 1)], start=(k == 0), stop=(k == KD - 1))
                last.then_inc(ln_mu, 1)
                for k in range(KD):
                    pe.wait_ge(ln_sq, KD * n + k + 1)
                    for h in range(2):
                        last = mmul(ps[:, 2 + h, 0:HALF], ones[:], sq[:, k, HALF * h:HALF * (h + 1)], start=(k == 0), stop=(k == KD - 1))
                last.then_inc(ln_var, 1)
                pe.wait_ge(ln_out, KD * (n + 1))

            pe.wait_ge(const_ok, 1)
            pe.wait_ge(in_x, 80)
            for k in range(KD):
                if k >= 4:
                    pe.wait_ge(x_up, k - 3)
                b = 2 * (k % 4)
                for c, (n, _) in enumerate(CHUNKS):
                    last = tr(ps[:, b + c // 4, (c % 4) * P:(c % 4) * P + n], xin[0:n, c, k * P:(k + 1) * P], ident[0:n, 0:n])
                last.then_inc(x_tr, 1)
            pe.wait_ge(x_up, KD)
            pe.wait_ge(in_par, 16 * 12)
            pe.wait_ge(in_hist, 48)
            for n, r in enumerate((P, 112, 32)):
                last = tr(ps[:, 0, n * P:n * P + r], par_in[0:r, n, :], ident[0:r, 0:r])
            for t in range(LT):
                tr(ps[:, 1, t * DEC_B:(t + 1) * DEC_B], h0_in[0:DEC_B, t * P:(t + 1) * P], ident[0:DEC_B, 0:DEC_B])
                tr(ps[:, 1, 64 + t * 24:64 + (t + 1) * 24], lhist_in[0:24, t * P:(t + 1) * P], ident[0:24, 0:24])
            for t in range(XBC):
                last = tr(ps[:, 2 + t // 16, (t % 16) * 24:(t % 16 + 1) * 24], shist_in[0:24, t * P:(t + 1) * P], ident[0:24, 0:24])
            last.then_inc(p_tr, 1)

            linear("l1", C_L1, 10, xT)
            pe.wait_ge(free["l1"], 12)
            pe.wait_ge(free_act1, 12)
            pe.wait_ge(uc_ok, 1)
            pe.wait_ge(in_gatew, 64)
            for gate, done in ((0, gr_mm), (1, gi_mm)):
                if gate:
                    pe.wait_ge(gr_ok, LT)
                for t in range(LT):
                    for h in range(2):
                        last = mmul(ps[:, 2 * t + h, 0:HALF], gate_w[:, gate, t, :], uc[:, t, HALF * h:HALF * (h + 1)], start=True, stop=True)
                    last.then_inc(done, 1)
            pe.wait_ge(gi_ok, LT)

            pe.wait_ge(lru_end, 1)
            for n in range(8):
                if n >= 4:
                    pe.wait_ge(kvt_up, n - 3)
                    pe.wait_ge(kvt_up_a, n - 3)
                b = 2 * (n % 4)
                for c, (m, c0) in enumerate(CHUNKS):
                    last = tr(ps[0:m, b + c // 4, (c % 4) * P:(c % 4 + 1) * P], proj[:, 4 + n, c0:c0 + m], ident[:])
                last.then_inc(kvt_tr, 1)
            pe.wait_ge(kvt_up, 8)
            pe.wait_ge(kvt_up_a, 8)

            NQ = HEADS * NCH

            def scores(n):
                h, qt = n // NCH, n % NCH
                r = 64 * (h % 2)
                if n >= 2:
                    pe.wait_ge(ex_ok, n - 1)
                w = (qt + 1) * P
                mmul(ps[:, n % 2, 0:w], proj[r:r + 64, h // 2, qt * P:(qt + 1) * P], proj[r:r + 64, 4 + h // 2, 0:w], start=True, stop=False)
                mmul(ps[:, n % 2, w - P:w], ident[:], qk_mask[:], start=False, stop=True).then_inc(sc_mm, 1)

            scores(0)
            for n in range(NQ):
                h, qt = n // NCH, n % NCH
                if n + 1 < NQ:
                    scores(n + 1)
                pe.wait_ge(pn_ok, n + 1)
                if n >= 2:
                    pe.wait_ge(pt_ok, n - 1)
                for c in range(qt + 1):
                    last = tr(ps[:, 2 + n % 2, c * P:(c + 1) * P], pp[:, n % 2, c * P:(c + 1) * P], ident[:])
                last.then_inc(pt_mm, 1)
                pe.wait_ge(pt_ok, n + 1)
                if n % 8 == 0 and n >= 16:
                    pe.wait_ge(o_up, n // 8 - 1)
                r, b = 64 * (h % 2), 4 + (h // 2) % 2
                for c in range(qt + 1):
                    last = mmul(ps[r:r + 64, b, qt * P:(qt + 1) * P], v_tok[:, c, h * HD:(h + 1) * HD], ppt[:, n % 2, c * P:(c + 1) * P],
                                start=(c == 0), stop=(c == qt))
                last.then_inc(o_mm, 1)
            pe.wait_ge(o_up, 4)
            pe.wait_ge(qx_ok, 1)

            for pr in range(DEC_B // 2):
                for q in range(4):
                    b2, n = q // 2, 4 * pr + q
                    pe.wait_ge(kv_in[q], 16 * QUAD * (2 * pr + 1))
                    for t in range(AT):
                        m = 4 * n + t
                        if m >= 4:
                            pe.wait_ge(kt_dve if t % 2 == 0 else kt_act, 2 * (n - 1) + t // 2 + 1)
                        for pg in range(QUAD):
                            last = tr(ps[:, t, pg * P:(pg + 1) * P], kv[q][:, pg, t * P:(t + 1) * P], ident[:])
                        last.then_inc(kt_mm, 1)
                    pe.wait_ge(kt_dve, 2 * n + 2)
                    pe.wait_ge(kt_act, 2 * n + 2)
                    if q == 0 and pr > 0:
                        pe.wait_ge(s_ex, pr)
                        pe.wait_ge(s_ptu, 3 * pr)
                    for t in range(AT):
                        last = mmul(ps[64 * b2:64 * b2 + 64, 4 + q % 2, :], qx[:, t, 2 * pr + b2, :], kt[n % 3][:, t, :],
                                    start=(t == 0), stop=(t == AT - 1))
                    if q % 2 == 1:
                        for t in range(AT):
                            mmul(ps[64 * b2:64 * b2 + 64, 6, 0:NS], qx[:, t, 2 * pr + b2, :], ks_T[:, t, :], start=(t == 0), stop=False)
                        last = mmul(ps[64 * b2:64 * b2 + 64, 6, 0:NS], expand[:, pr, 64 * b2:64 * b2 + 64], seq_maskT[:], start=False, stop=True)
                    last.then_inc(qs_mm, 1)
                pe.wait_ge(s_pn, pr + 1)
                for rnd, b in ((0, 7), (1, 6), (2, 7)):
                    if rnd == 0 and pr > 0:
                        pe.wait_ge(s_ou, 2 * pr)
                    if rnd == 2:
                        pe.wait_ge(s_ptu, 3 * pr + 1)
                    for c in range(4 * rnd, min(4 * rnd + 4, 9)):
                        n = P if c < 8 else NS
                        last = tr(ps[0:n, b, (c % 4) * P:(c % 4 + 1) * P], p_s[:, c * P:c * P + n], ident[:])
                    last.then_inc(s_ptm, 1)
                pe.wait_ge(s_ptu, 3 * pr + 3)
                for b2 in range(2):
                    for h in range(2):
                        pe.wait_ge(kv_in[2 * b2 + h], 16 * QUAD * (2 * pr + 2))
                    for t in range(AT):
                        o = ps[:, 7, (4 * b2 + t) * 16:(4 * b2 + t + 1) * 16]
                        r = 64 * b2 + 16 * t
                        for c in range(NPAGES):
                            mmul(o, kv[2 * b2 + c // QUAD][:, c % QUAD, t * P:(t + 1) * P], p_sT[:, c, r:r + 16], start=(c == 0), stop=False)
                        last = mmul(o, v_tok[0:NS, NCH, t * P:(t + 1) * P], p_sT[0:NS, 8, r:r + 16], start=False, stop=True)
                    last.then_inc(s_o, 1)
            pe.wait_ge(s_ou, 8)

            for j in range(KD // 2):
                unit("l2", j, 4 * (j % 2), [part(C_L2 + j)], cat)
            layer_norm(0)
            linear("l3", C_L3, FT, xT)
            pe.wait_ge(free["l3"], FT + 2)
            for j in range(KD // 2):
                unit("l4", j, 4 * (j % 2), [part(C_L4 + 2 * j, 0, 0, KMAX), part(C_L4 + 2 * j + 1, 0, KMAX, KMAX)], hid)
            layer_norm(1)

            linear("xb", C_XBC, XBC // 2, xT)
            unit("dt", 0, 0, [part(C_DT)], xT, M=SH)
            pe.wait_ge(row_ok, 1)
            for n, src in enumerate((DTR, CSR, WDR)):
                for c, (m, c0) in enumerate(CHUNKS):
                    last = tr(ps[0:m, 2 + n, c * SH:(c + 1) * SH], rows[0:SH, src, c0:c0 + m], ident[0:SH, 0:SH])
            mmul(ps[:, 5, 0:SH * NCH], ones[0:SH, :], tmpr[0:SH, 1, 0:SH * NCH], start=True, stop=True)
            for t in range(XT):
                for hh in range(2):
                    sel = ident[0:SH, 2 * t + hh:2 * t + hh + 1].broadcast_to([SH, 64])
                    mmul(ps[64 * hh:64 * hh + 64, 6, t * 8:t * 8 + 8], sel, rows[0:SH, ECR, SEQ + DEC_T - 1:T:DEC_T], start=True, stop=True)
                    last = mmul(ps[64 * hh:64 * hh + 64, 6, 128 + t:129 + t], sel, dt_par[:, 2:3], start=True, stop=True)
            last.then_inc(tk_mm, 1)

            for g in range(SG):
                Bt, Ct = xbc[:, XT + g, :], xbc[:, XT + BC + g, :]
                if g == 0:
                    pe.wait_ge(tk_up, 1)
                else:
                    pe.wait_ge(fs_up, g)
                    pe.wait_ge(ss_ok, 2 * g)
                for c in range(NCH):
                    mmul(ps[:, 0, c * P:(c + 1) * P], Bt[:, c * P:(c + 1) * P], Ct[:, c * P:(c + 1) * P], start=True, stop=True)
                mmul(ps[0:NS, 1, 0:NS], Bt[:, SEQ:T], Ct[:, SEQ:T], start=True, stop=True)
                for c in range(NCH):
                    tr(ps[:, 2, c * P:(c + 1) * P], Bt[:, c * P:(c + 1) * P], ident[:])
                    for j in range(2):
                        tr(ps[:, 3 + j, c * P:(c + 1) * P], xbc[:, 2 * g + j, c * P:(c + 1) * P], ident[:])
                tr(ps[0:NS, 1, P:2 * P], Bt[:, SEQ:T], ident[:])
                for j in range(2):
                    last = tr(ps[0:NS, 1, (2 + j) * P:(3 + j) * P], xbc[:, 2 * g + j, SEQ:T], ident[:])
                last.then_inc(g_mm, 1)
                pe.wait_ge(g_up, g + 1)
                for c in range(NCH):
                    last = mmul(ps[:, 5 + c // 2, (c % 2) * 256:(c % 2 + 1) * 256], b_tok[:, c, :], x_w[:, c, :], start=True, stop=True)
                last.then_inc(st_mm, 1)
                for j in range(2):
                    t = 2 * g + j
                    pe.wait_ge(h0_in_s, 16 * (t + 1))
                    if t >= 1:
                        pe.wait_ge(ss_ok, t)
                        pe.wait_ge(y_ok, t)
                    for b in range(DEC_B):
                        last = tr(ps[:, 3 + b // 4, (b % 4) * P:(b % 4 + 1) * P], h0n[:, b, :], ident[:])
                    last.then_inc(h0_tr, 1)
                    pe.wait_ge(h0_up, t + 1)
                    pe.wait_ge(st_up, g + 1)
                    for c in range(1, NCH):
                        mmul(ps[:, 3, c * P:(c + 1) * P], state[:, c - 1, j * P:(j + 1) * P], Ct[:, c * P:(c + 1) * P], start=True, stop=True)
                    for b in range(DEC_B):
                        mmul(ps[:, 3, 8 * b:8 * b + 8], h0t[:, b, :], Ct[:, SEQ + 8 * b:SEQ + 8 * b + 8], start=True, stop=True)
                    for hh in range(2):
                        sel = ident[0:SH, 2 * t + hh:2 * t + hh + 1].broadcast_to([SH, 64])
                        mmul(ps[64 * hh:64 * hh + 64, 6, :], sel, rows[0:SH, ECR, 0:SEQ], start=True, stop=True)
                        last = mmul(ps[64 * hh:64 * hh + 64, 7, 0:64], sel, rows[0:SH, ECR, SEQ:T], start=True, stop=True)
                    last.then_inc(yi_mm, 1)
                    for hh in range(2):
                        h = 2 * t + hh
                        b = 4 + hh
                        if hh == 0:
                            pe.wait_ge(ex_up, t + 1)
                        sel = ident[0:SH, h:h + 1].broadcast_to([SH, P])
                        mmul(ps[:, b, :], sel, rows[0:SH, CSR, 0:SEQ], start=True, stop=False)
                        mmul(ps[:, b, :], ident[:], sl_mask[:].unsqueeze(1).broadcast_to([P, NCH, P]), start=False, stop=True)
                        o = ps[0:NS, 7, 192 + 64 * hh:256 + 64 * hh]
                        mmul(o, ident[0:SH, h:h + 1].broadcast_to([SH, NS]), rows[0:SH, CSR, SEQ:T], start=True, stop=False)
                        last = mmul(o, ident[0:NS, 0:NS], seq_mask[:], start=False, stop=True)
                    last.then_inc(cs_mm, 1)
                    for hh in range(2):
                        h = 2 * t + hh
                        pe.wait_ge(m_ok, h + 1)
                        hc = (2 * j + hh) * 64
                        for c in range(NCH):
                            mmul(ps[64 * hh:64 * hh + 64, 2, c * P:(c + 1) * P], x_dt[:, c, hc:hc + 64], m_buf[:, c * P:(c + 1) * P], start=True, stop=True)
                        last = mmul(ps[64 * hh:64 * hh + 64, 6, 0:NS], x_dt[0:NS, NCH, hc:hc + 64], m_buf[0:NS, SEQ:T], start=True, stop=True)
                        last.then_inc(yt_mm, 1)
                    pe.wait_ge(e_ok, 2 * t + 2)
                    for hf in range(2):
                        last = mmul(ps[:, 4 + hf, :], x_w[0:NS, NCH, j * P:(j + 1) * P], b_seq[0:NS, 4 * hf:4 * hf + 4, :].rearrange("p b n -> p (b n)"), start=True, stop=True)
                    last.then_inc(ss_mm, 1)
                pe.wait_ge(y_ok, 2 * g + 2)
                for j in range(2):
                    last = tr(ps[:, 3, j * P:(j + 1) * P], state[:, NCH - 1, j * P:(j + 1) * P], ident[:])
                last.then_inc(fs_mm, 1)
            pe.wait_ge(fs_up, SG)
            pe.wait_ge(ss_ok, XT)

            def z_unit(i, j):
                n = SLOTS * i + j
                unit("z", n, 0, [part(C_Z + j, i)], xT)
                pe.wait_ge(z_sqd, n + 1)
                pe.wait_ge(z_rt, n + 1)
                for k in range(2):
                    for h in range(2):
                        last = mmul(ps[:, 4 + h, 0:HALF], ones[:], z_q[:, k, HALF * h:HALF * (h + 1)], start=(k == 0), stop=(k == 1))
                last.then_inc(z_sum, 1)
            with pe.Fori(0, XT // 2 // SLOTS) as i:
                for j in range(SLOTS):
                    z_unit(i, j)
            pe.wait_ge(z_ok, XT // 2 + 1)
            for j in range(KD // 2):
                unit("l6", j, 4 * (j % 2), [part(C_L6 + 2 * j, 0, 0, 8), part(C_L6 + 2 * j + 1, 0, 8, 8)], xbc)
            layer_norm(2)
            for n in range(9):
                if n >= 2:
                    pe.wait_ge(tl_up, n - 1)
                for q in range(4):
                    t = 4 * n + q
                    if n < 8:
                        last = tr(ps[0:27, n % 2, q * P:(q + 1) * P], ssd_tail[:, t, :], ident[:])
                    else:
                        last = tr(ps[0:36, n % 2, q * P:(q + 1) * P], lru_tail[:, q, :], ident[:])
                last.then_inc(tl_mm, 1)
            pe.wait_ge(tl_up, 9)
            pe.wait_ge(in_router, 16)
            for c, (m, c0) in enumerate(CHUNKS):
                for k in range(KD):
                    last = mmul(ps[0:m, 4, c * NE:(c + 1) * NE], xT[:, k, c0:c0 + m], router[:, k, :], start=(k == 0), stop=(k == KD - 1))
            last.then_inc(rt_mm, 1)
            pe.wait_ge(rt_g, 1)
            for c, (m, c0) in enumerate(CHUNKS):
                last = tr(ps[0:NE, 4 + c // 4, (c % 4) * P:(c % 4) * P + m], stat[0:m, c * NE:(c + 1) * NE], ident[0:m, 0:m])
            last.then_inc(gt_mm, 1)
            pe.wait_ge(gt_up, 1)
            for e in range(NE):
                if e >= 4:
                    pe.wait_ge(gb_up, e - 3)
                for h in range(2):
                    last = mmul(ps[:, 2 * (e % 4) + h, 0:HALF], ident[0:NE, e:e + 1].broadcast_to([NE, P]), gT[0:NE, HALF * h:HALF * (h + 1)], start=True, stop=True)
                last.then_inc(gb_mm, 1)
            pe.wait_ge(gb_up, NE)
            moe_slot = [slot4] + [ring[:, (C_MOE + m) % SLOTS] for m in range(SLOTS)]
            with pe.Fori(0, NE) as e:
                for m in range(PER_E):
                    s = m % MOE_SLOTS
                    up = m < FET
                    n = m if up else m - FET
                    if not up and n == 0:
                        pe.wait_ge(free["eu"], FET * e + FET + 2)
                    unit("eu" if up else "ed", (FET if up else KD // 2) * e + n, 4 * (m % 2),
                         [(moe_loaded[s], 32 * (3 * e + m // MOE_SLOTS + 1), moe_slot[s], 0, KD if up else FET)], xT if up else e_hid)
                pe.wait_ge(free["ed"], (KD // 2) * e + KD // 2 + 2)
            layer_norm(3)
            for c, (m, c0) in enumerate(CHUNKS):
                for hf in range(2):
                    n = 2 * c + hf
                    if n >= 4:
                        pe.wait_ge(out_up, n - 3)
                    for k in range(4):
                        last = tr(ps[0:m, n % 4, k * P:(k + 1) * P], xT[:, 4 * hf + k, c0:c0 + m], ident[:])
                    last.then_inc(out_mm, 1)

        @block.scalar
        def _(act):
            f = act.activation
            link = Chain(act, act_c)

            def banks(b):
                return ps[:, b:b + 2, 0:HALF]

            def halves(v):
                return v.rearrange("p (h n) -> p h n", h=2)

            def layer_norm(n):
                for k in range(KD):
                    act.wait_ge(ln_c, KD * n + k + 1)
                    f(sq[:, k, :], xT[:, k, :], ACT.Square).then_inc(ln_sq, 1)
                act.wait_ge(ln_var, n + 1)
                f(halves(std), banks(2), ACT.Sqrt, bias=eps[:, 0:1], scale=1.0 / D).then_inc(ln_std, 1)
                for k in range(KD):
                    act.wait_ge(ln_n, KD * n + k + 1)
                    f(xT[:, k, :], xT[:, k, :], ACT.Identity, bias=ln_b[n][:, k:k + 1], scale=ln_g[n][:, k:k + 1]).then_inc(ln_out, 1)

            act.wait_ge(const_ok, 1)
            act.wait_ge(p_up, 1)
            act.sem_inc(free_act1, 2)

            def l1(n, j):
                act.wait_ge(used, done("l1", n))
                f(halves(proj[:, ds(2 * n + 1, 1), :].rearrange("p o n -> p (o n)")), banks(4 * (j % 2) + 2), ACT.Copy).then_inc(free_act1, 1)
            with act.Fori(0, 2) as i:
                for j in range(SLOTS):
                    l1(SLOTS * i + j, j)
            for j in range(2):
                l1(8 + j, j)

            act.wait_ge(lam_e, 1)
            f(stat[:, 8:12], stat[:, 4:8], ACT.Exp, scale=-1.0).then_inc(lam_e, 1)
            act.wait_ge(lam_u, 1)
            f(stat[:, 16:20], stat[:, 12:16], ACT.Ln).then_inc(lam_l, 1)
            for t in range(LT):
                act.wait_ge(gr_mm, t + 1)
                f(halves(lru_a[:, t * T:(t + 1) * T]), banks(2 * t), ACT.Sigmoid, bias=b_gate[0][:, t:t + 1]).then_inc(gr_ok, 1)
            for t in range(LT):
                act.wait_ge(gi_mm, t + 1)
                f(halves(lru_i[:, t * T:(t + 1) * T]), banks(2 * t), ACT.Sigmoid, bias=b_gate[1][:, t:t + 1]).then_inc(gi_ok, 1)
            act.wait_ge(la_ok, 1)
            link(f(lru_t[:], lru_a[:], ACT.Tanh, scale=-1.0))
            f(lru_a[:], lru_a[:], ACT.Exp).then_inc(a_ok, 1)
            f(proj[:, 16:20, :], proj[:, 16:20, :], ACT.Gelu_apprx_tanh).then_inc(g_ok, 1)
            act.wait_ge(a2_ok, 1)
            f(lru_t[:], lru_t[:], ACT.Sqrt).then_inc(s_ok, 1)

            act.wait_ge(lru_end, 1)
            for n in range(8):
                act.wait_ge(kvt_tr, n + 1)
                dst = (k_tok if n < 4 else v_tok)
                f(dst[0:NS, NCH, (n % 4) * P:(n % 4 + 1) * P], ps[0:NS, 2 * (n % 4) + 1, 0:P], ACT.Copy).then_inc(kvt_up_a, 1)

            NQ = HEADS * NCH
            for n in range(NQ + 1):
                if n < NQ:
                    w = (n % NCH + 1) * P
                    act.wait_ge(mx_ok, n + 1)
                    if n >= 2:
                        act.wait_ge(pt_mm, n - 1)
                    f(pp[:, n % 2, 0:w], ps[:, n % 2, 0:w], ACT.Exp, bias=stat[:, 34 + n % 2:35 + n % 2], scale=HD ** -0.5,
                      accum_out=stat[:, 36 + n % 2:37 + n % 2]).then_inc(ex_ok, 1)
                if n >= 1:
                    m = n - 1
                    w = (m % NCH + 1) * P
                    act.wait_ge(pt_mm, m + 1)
                    if m >= 2:
                        act.wait_ge(o_mm, m - 1)
                    f(ppt[:, m % 2, 0:w], ps[:, 2 + m % 2, 0:w], ACT.Copy).then_inc(pt_ok, 1)

            for pr in range(DEC_B // 2):
                for q in range(4):
                    n = 4 * pr + q
                    if n >= 3:
                        act.wait_ge(qs_mm, n - 2)
                    for t in (1, 3):
                        act.wait_ge(kt_mm, 4 * n + t + 1)
                        f(kt[n % 3][:, t, :], ps[:, t, :], ACT.Copy).then_inc(kt_act, 1)
                act.wait_ge(s_bias, pr + 1)
                if pr:
                    act.wait_ge(s_ptm, 3 * pr)
                for n in range(NBLK):
                    f(p_s[:, BLK * n:BLK * (n + 1)], ps[:, 4 + n // 2, (n % 2) * BLK:(n % 2 + 1) * BLK], ACT.Exp,
                      bias=stat[:, 40 + n:41 + n], scale=HD ** -0.5, accum_out=stat[:, 48 + n:49 + n])
                f(p_s[:, NBLK * BLK:], ps[:, 6, 0:NS], ACT.Exp, bias=stat[:, 44:45], scale=HD ** -0.5,
                  accum_out=stat[:, 52:53]).then_inc(s_ex, 1)
                if pr:
                    act.wait_ge(s_o, 2 * pr)
                for rnd, b in ((0, 7), (1, 6)):
                    act.wait_ge(s_ptm, 3 * pr + rnd + 1)
                    f(p_sT[:, 4 * rnd:4 * rnd + 4, :].rearrange("p c n -> p (c n)"), ps[:, b, :], ACT.Copy).then_inc(s_ptu, 1)
                act.wait_ge(s_ptm, 3 * pr + 3)
                f(p_sT[0:NS, 8, :], ps[0:NS, 7, 0:P], ACT.Copy).then_inc(s_ptu, 1)

            act.wait_ge(kv_out, 64)
            layer_norm(0)

            def silu3(n, j):
                act.wait_ge(used, done("l3", n))
                f(halves(hid[:, ds(n, 1), :].rearrange("p o n -> p (o n)")), banks(4 * (j % 2)), ACT.Silu).then_inc(silu_ok["l3"], 1)
            with act.Fori(0, FT // SLOTS) as i:
                for j in range(SLOTS):
                    silu3(SLOTS * i + j, j)
            for j in range(2):
                silu3(FT // SLOTS * SLOTS + j, j)
            layer_norm(1)

            act.sem_inc(free["xb"], 2)
            act.sem_inc(cv_s, 1)

            def raw_out(n, j):
                act.wait_ge(used, done("xb", n))
                act.wait_ge(cv_y, n + 1)
                b, s = 4 * (j % 2), 2 * (j % 2)
                f(raw[:, s:s + 2, HIST:HIST + HALF], ps[:, b:b + 4:2, 0:HALF], ACT.Copy)
                f(raw[:, s:s + 2, HIST + HALF:HIST + SEQ], ps[:, b + 1:b + 4:2, 0:SEQ - HALF], ACT.Copy)
                for q in range(2):
                    smp = raw[:, s + q, HIST + SEQ:].rearrange("p (b t) -> p b t", t=HIST + DEC_T)
                    last = f(smp[:, :, HIST:], ps[:, b + 1 + 2 * q, SEQ - HALF:HALF].rearrange("p (b t) -> p b t", t=DEC_T), ACT.Copy)
                last.then_inc(free["xb"], 1)

            def conv_silu(n):
                act.wait_ge(cv_y, n + 3)
                f(xbc[:, ds(2 * n, 2), 0:SEQ], acc[:, :, 0:SEQ], ACT.Silu)
                for q in range(2):
                    last = f(xbc[:, ds(2 * n + q, 1), SEQ:T].rearrange("p o (b t) -> p (o b) t", t=DEC_T), of_samples(acc[:, q, :]), ACT.Silu)
                last.then_inc(cv_s, 1)
            with act.Fori(0, XBC // 2 // SLOTS) as i:
                for j in range(SLOTS):
                    raw_out(SLOTS * i + j, j)
                    conv_silu(SLOTS * i + j)

            act.wait_ge(dt_a, 1)
            f(tmpr[0:SH, 2, :], tmpr[0:SH, 1, :], ACT.Exp, scale=-1.0)
            f(dt_par[:, 3:4], dt_par[:, 1:2], ACT.Exp).then_inc(dt_e, 1)
            act.wait_ge(dt_u, 1)
            f(tmpr[0:SH, 1, :], tmpr[0:SH, 3, :], ACT.Ln).then_inc(dt_l, 1)
            act.wait_ge(cs_ok, 1)
            f(rows[0:SH, ECR, :], rows[0:SH, CSR, :], ACT.Exp)
            f(tmpr[0:SH, 0, :], tmpr[0:SH, 0, :], ACT.Exp).then_inc(ec_ok, 1)

            for g in range(SG):
                act.wait_ge(g_mm, g + 1)
                f(b_tok[:, 0:NCH, :].rearrange("p c n -> p (c n)"), ps[:, 2, :], ACT.Copy).then_inc(g_up_a, 1)
                for j in range(2):
                    t = 2 * g + j
                    act.wait_ge(h0_tr, t + 1)
                    f(h0t[:].rearrange("p (u b) n -> p u (b n)", u=2), ps[:, 3:5, :], ACT.Copy).then_inc(h0_up, 1)
                    act.wait_ge(yi_mm, t + 1)
                    f(exs[:, 0:SEQ], ps[:, 6, :], ACT.Copy)
                    f(exs[:, SEQ:T], ps[:, 7, 0:NS], ACT.Copy).then_inc(ex_up, 1)
                    for hh in range(2):
                        h = 2 * t + hh
                        act.wait_ge(cs_mm, t + 1)
                        act.wait_ge(m_ok, h)
                        for c in range(NCH):
                            f(e_buf[:, c * P:(c + 1) * P], ps[:, 4 + hh, c * P:(c + 1) * P], ACT.Exp, bias=tok[:, 1, c * SH + h:c * SH + h + 1])
                        f(e_buf[0:NS, SEQ:T], ps[0:NS, 7, 192 + 64 * hh:256 + 64 * hh], ACT.Exp,
                          bias=tok[0:NS, 1, NCH * SH + h:NCH * SH + h + 1]).then_inc(e_ok, 1)

            act.sem_inc(free["z"], 1)
            act.sem_inc(z_rt, 1)

            def z_unit(i, j):
                n = SLOTS * i + j
                act.wait_ge(used, done("z", n))
                act.wait_ge(z_gate, n + 1)
                f(z_s[:].rearrange("p k (h n) -> p (k h) n", h=2), ps[:, 0:4, 0:HALF], ACT.Silu).then_inc(free["z"], 1)
                act.wait_ge(z_gate, n + 2)
                f(z_q[:], xbc[:, ds(2 * n, 2), :], ACT.Square).then_inc(z_sqd, 1)
                act.wait_ge(z_sum, n + 1)
                act.wait_ge(z_ok, n + 1)
                f(halves(z_r), banks(4), ACT.Sqrt, bias=eps[:, 1:2], scale=1.0 / (2 * P)).then_inc(z_rt, 1)
            with act.Fori(0, XT // 2 // SLOTS) as i:
                for j in range(SLOTS):
                    z_unit(i, j)
            layer_norm(2)
            act.wait_ge(rt_d, 1)
            f(g_w[:, 0:5], g_w[:, 5:10], ACT.Exp).then_inc(rt_e, 1)
            with act.Fori(0, NE) as e:
                for m in range(FET):
                    act.wait_ge(used, SLOTS + C_MOE + PER_E * e + m + 1)
                    if m == 0:
                        act.wait_ge(used, SLOTS + C_MOE + PER_E * e)
                    f(halves(e_hid[:, m, :]), banks(4 * (m % 2)), ACT.Silu).then_inc(silu_ok["eu"], 1)
            layer_norm(3)

        @block.vector
        def _(dve):
            link = Chain(dve, dve_c)
            tt, tsc, stt, cp = dve.tensor_tensor, dve.tensor_scalar, dve.scalar_tensor_tensor, dve.tensor_copy

            def banks(b):
                return ps[:, b:b + 2, 0:HALF]

            def halves(v):
                return v.rearrange("p (h n) -> p h n", h=2)

            def layer_norm(n):
                dve.wait_ge(ln_mu, n + 1)
                mu = banks(0)
                link(tsc(halves(std), mu, 1.0 / D, None, ALU.mult))
                for k in range(KD):
                    tt(xT[:, k, :], xT[:, k, :], std[:], ALU.subtract).then_inc(ln_c, 1)
                dve.wait_ge(ln_std, n + 1)
                link(dve.reciprocal(rstd[:], std[:]))
                for k in range(KD):
                    tt(xT[:, k, :], xT[:, k, :], rstd[:], ALU.mult).then_inc(ln_n, 1)

            def residual(stage, n, bank, last=None):
                dve.wait_ge(used, done(stage, n))
                for q in range(2):
                    i = stt(halves(xT[:, 2 * n + q, :]), halves(xT[:, 2 * n + q, :]), ALPHA, banks(bank + 2 * q), ALU.mult, ALU.add)
                i.then_inc(last or free[stage], 1)

            for k in range(KD):
                dve.wait_ge(x_tr, k + 1)
                b = 2 * (k % 4)
                cp(xT[:, k, 0:SEQ], ps[:, b, :])
                cp(xT[:, k, SEQ:T], ps[:, b + 1, 0:NS]).then_inc(x_up, 1)
            dve.wait_ge(p_tr, 1)
            cp(par[:, 0, :], ps[:, 0, 0:P])
            cp(par[:, 1, 0:112], ps[:, 0, P:P + 112])
            cp(par[:, 2, 0:32], ps[:, 0, 2 * P:2 * P + 32])
            cp(lru_h0[:].rearrange("p t b -> p (t b)"), ps[:, 1, 0:LT * DEC_B])
            cp(lru_hist[:].rearrange("p t n -> p (t n)"), ps[:, 1, 64:64 + LT * 24])
            for u in range(2):
                last = cp(ssd_hist[:, 16 * u:16 * u + 16, :].rearrange("p t n -> p (t n)"), ps[:, 2 + u, 0:384])
            last.then_inc(p_up, 1)
            dve.wait_ge(p_up, 1)
            dve.sem_inc(free["l1"], 2)

            def l1(n, j):
                dve.wait_ge(used, done("l1", n))
                cp(halves(proj[:, ds(2 * n, 1), :].rearrange("p o n -> p (o n)")), banks(4 * (j % 2))).then_inc(free["l1"], 1)
            with dve.Fori(0, 2) as i:
                for j in range(SLOTS):
                    l1(SLOTS * i + j, j)
            for j in range(2):
                l1(8 + j, j)

            dve.wait_ge(free_act1, 12)
            dve.wait_ge(free["l1"], 12)
            padded = u_pad[:, :, HIST + SEQ:].rearrange("p t (b n) -> p t b n", b=DEC_B)
            dve.memset(u_pad[:, :, 0:HIST], 0.0)
            cp(u_pad[:, :, HIST:HIST + SEQ], proj[:, 12:16, 0:SEQ])
            for t in range(LT):
                cp(padded[:, t, :, 0:HIST], lru_hist[:, t, :].rearrange("p (b n) -> p b n", b=DEC_B))
                cp(padded[:, t, :, HIST:], proj[:, 12 + t, SEQ:T].rearrange("p (b n) -> p b n", b=DEC_B))
                cp(lru_tail[:, t, 12:36].rearrange("p (b n) -> p b n", b=DEC_B),
                   proj[:, 12 + t, SEQ:T].rearrange("p (b n) -> p b n", b=DEC_B)[:, :, DEC_T - HIST:])
            link(cp(lru_tail[:, :, 9:12], proj[:, 12:16, SEQ - HIST:SEQ]))
            N = PADT - HIST
            for t in range(LT):
                link(tsc(u_acc[:, 0:N], u_pad[:, t, 3:3 + N], conv_w_l[:, 3, t:t + 1], conv_b_l[:, t:t + 1], ALU.mult, ALU.add))
                for w in (2, 1):
                    link(stt(u_acc[:, 0:N], u_pad[:, t, w:w + N], conv_w_l[:, w, t:t + 1], u_acc[:, 0:N], ALU.mult, ALU.add))
                link(stt(u_acc[:, 0:N], u_pad[:, t, 0:N], conv_w_l[:, 0, t:t + 1], u_acc[:, 0:N], ALU.mult, ALU.add))
                cp(uc[:, t, 0:SEQ], u_acc[:, 0:SEQ])
                link(cp(uc[:, t, SEQ:T].rearrange("p (b n) -> p b n", b=DEC_B), of_samples(u_acc[:])))
            dve.sem_inc(uc_ok, 1)
            c4 = lambda n: stat[:, 4 * n:4 * n + 4]
            stt(c4(1), lam, -1.0, lam, ALU.mult, ALU.max).then_inc(lam_e, 1)
            dve.wait_ge(lam_e, 2)
            link(tsc(c4(3), c4(2), 1.0, None, ALU.add))
            link(tsc(c4(5), c4(3), -1.0, None, ALU.add))
            dve.sem_inc(lam_u, 1)
            link(tsc(c4(6), c4(5), 0.0, None, ALU.is_equal))
            link(tt(c4(5), c4(5), c4(6), ALU.add))
            link(dve.reciprocal(c4(5), c4(5)))
            dve.wait_ge(lam_l, 1)
            link(tt(c4(4), c4(4), c4(6), ALU.add))
            link(tt(c4(4), c4(4), c4(2), ALU.mult))
            link(tt(c4(4), c4(4), c4(5), ALU.mult))
            link(tsc(c4(7), lam, -1.0, 0.0, ALU.mult, ALU.max))
            link(tt(c4(7), c4(7), c4(4), ALU.add))
            link(tsc(c4(7), c4(7), -8.0, None, ALU.mult))
            for t in range(LT):
                dve.wait_ge(gr_ok, t + 1)
                last = tsc(lru_a[:, t * T:(t + 1) * T], lru_a[:, t * T:(t + 1) * T], stat[:, 28 + t:29 + t], None, ALU.mult)
            last.then_inc(la_ok, 1)
            dve.wait_ge(gi_ok, LT)
            link(tt(lru_i[:], lru_i[:], uc[:].rearrange("p t n -> p (t n)"), ALU.mult))
            dve.wait_ge(a_ok, 1)
            a2 = u_pad[:].rearrange("p t n -> p (t n)")[:, 0:LT * T]
            link(tt(a2, lru_a[:], lru_a[:], ALU.mult))
            stt(lru_t[:], a2, 1.0, lru_t[:], ALU.add, ALU.mult).then_inc(a2_ok, 1)
            dve.wait_ge(s_ok, 1)
            link(tt(lru_i[:], lru_i[:], lru_t[:], ALU.mult))
            a3 = lru_a[:].rearrange("p (t n) -> p t n", t=LT)
            b3 = lru_i[:].rearrange("p (t n) -> p t n", t=LT)
            a0, b0 = a3[:, :, SEQ:T:DEC_T], b3[:, :, SEQ:T:DEC_T]
            h1 = stat[:, 64:96].rearrange("p (t b) -> p t b", t=LT)
            link(tt(h1, a0, lru_h0[:], ALU.mult))
            tt(b0, b0, h1, ALU.add)
            link(dve.memset(a0, 0.0))
            link(dve.memset(a3[:, :, 0:1], 0.0))
            ucf = uc[:].rearrange("p t n -> p (t n)")
            link(dve.tensor_tensor_scan(ucf, lru_a[:], lru_i[:], 0.0, ALU.mult, ALU.add))
            cp(lru_tail[:, :, 0:1], uc[:, :, SEQ - 1:SEQ])
            cp(lru_tail[:, :, 1:9], uc[:, :, SEQ + DEC_T - 1:T:DEC_T])
            dve.wait_ge(g_ok, 1)
            tt(cat[:, AT:, :], uc[:], proj[:, 16:20, :], ALU.mult).then_inc(lru_end, 1)
            dve.wait_ge(lru_end, 1)

            for n in range(8):
                dve.wait_ge(kvt_tr, n + 1)
                dst = (k_tok if n < 4 else v_tok)
                cp(dst[:, 0:NCH, (n % 4) * P:(n % 4 + 1) * P], ps[:, 2 * (n % 4), :].rearrange("p (c d) -> p c d", c=NCH)).then_inc(kvt_up, 1)
            link(dve.memset(qx[:], 0.0))
            for t in range(AT):
                for hh in range(2):
                    r = 64 * hh
                    cp(qx[r:r + 64, t, :, 16 * t + 8 * hh:16 * t + 8 * hh + 8],
                       proj[r:r + 64, t, SEQ:T].rearrange("p (b n) -> p b n", b=DEC_B))
            cp(ks_T[:], proj[:, 4:8, SEQ:T]).then_inc(qx_ok, 1)

            NQ = HEADS * NCH

            def o_out(u):
                dve.wait_ge(o_mm, 8 * u + 8)
                cp(cat[:, u, 0:SEQ], ps[:, 4 + u % 2, :]).then_inc(o_up, 1)
            for n in range(NQ + 1):
                if n < NQ:
                    w = (n % NCH + 1) * P
                    dve.wait_ge(sc_mm, n + 1)
                    mx, neg = stat[:, 32 + n % 2:33 + n % 2], stat[:, 34 + n % 2:35 + n % 2]
                    link(dve.tensor_reduce(mx, ps[:, n % 2, 0:w], AX, ALU.max))
                    tsc(neg, mx, -(HD ** -0.5), None, ALU.mult).then_inc(mx_ok, 1)
                if n >= 1:
                    m = n - 1
                    w = (m % NCH + 1) * P
                    dve.wait_ge(ex_ok, m + 1)
                    rc = stat[:, 38 + m % 2:39 + m % 2]
                    link(dve.reciprocal(rc, stat[:, 36 + m % 2:37 + m % 2]))
                    tsc(pp[:, m % 2, 0:w], pp[:, m % 2, 0:w], rc, None, ALU.mult).then_inc(pn_ok, 1)
                if n >= 2 and (n - 2) % 8 == 7:
                    o_out((n - 2) // 8)
            o_out(3)

            for pr in range(DEC_B // 2):
                for q in range(4):
                    n = 4 * pr + q
                    if n >= 3:
                        dve.wait_ge(qs_mm, n - 2)
                    for t in (0, 2):
                        dve.wait_ge(kt_mm, 4 * n + t + 1)
                        cp(kt[n % 3][:, t, :], ps[:, t, :]).then_inc(kt_dve, 1)
                dve.wait_ge(qs_mm, 4 * pr + 4)
                if pr:
                    dve.wait_ge(s_pn, pr)
                S = ps[:, 4:6, :].rearrange("p u (n k) -> p (u n) k", k=BLK)
                bs, bm = stat[:, 56:60], stat[:, 60:65]
                dve.tensor_reduce(bs, S, AX, ALU.add)
                dve.tensor_reduce(bm[:, 0:NBLK], S, AX, ALU.max)
                link(dve.tensor_reduce(bm[:, NBLK:], ps[:, 6, 0:NS], AX, ALU.max))
                gt = stat[:, 96:112].rearrange("p (a b) -> p a b", a=NBLK)
                eq = stat[:, 112:128].rearrange("p (a b) -> p a b", a=NBLK)
                mine, other = bs.unsqueeze(2).broadcast_to([P, NBLK, NBLK]), bs.unsqueeze(1).broadcast_to([P, NBLK, NBLK])
                tt(gt, other, mine, ALU.is_gt)
                link(tt(eq, other, mine, ALU.is_equal))
                link(tt(eq, eq, tri[:, 0:NBLK, 0:NBLK], ALU.mult))
                link(tt(gt, gt, eq, ALU.add))
                rank = stat[:, 128:132]
                link(dve.tensor_reduce(rank, gt, AX, ALU.add))
                pen = stat[:, 132:136]
                link(tsc(pen, rank, float(NBLK - 1), NEG, ALU.is_ge, ALU.mult))
                link(tt(bm[:, 0:NBLK], bm[:, 0:NBLK], pen, ALU.add))
                link(dve.tensor_reduce(stat[:, 136:137], bm, AX, ALU.max))
                link(tsc(stat[:, 44:45], stat[:, 136:137], -(HD ** -0.5), None, ALU.mult))
                tsc(stat[:, 40:44], pen, stat[:, 44:45], None, ALU.add).then_inc(s_bias, 1)
                dve.wait_ge(s_ex, pr + 1)
                link(dve.tensor_reduce(stat[:, 137:138], stat[:, 48:53], AX, ALU.add))
                link(dve.reciprocal(stat[:, 138:139], stat[:, 137:138]))
                tsc(p_s[:], p_s[:], stat[:, 138:139], None, ALU.mult).then_inc(s_pn, 1)
                dve.wait_ge(s_o, 2 * pr + 2)
                for hh in range(2):
                    r = 64 * hh
                    for b2 in range(2):
                        c0 = SEQ + DEC_T * (2 * pr + b2)
                        i = cp(cat[r:r + 64, 0:AT, c0:c0 + DEC_T],
                               ps[r:r + 64, 7, 64 * b2:64 * b2 + 64].rearrange("p (t n) -> p t n", t=AT)[:, :, 8 * hh:8 * hh + 8])
                    i.then_inc(s_ou, 1)

            dve.wait_ge(s_ou, 8)
            dve.sem_inc(free["l2"], 2)
            for j in range(KD // 2):
                residual("l2", j, 4 * (j % 2), ln_ready if j == 3 else None)
            layer_norm(0)
            dve.wait_ge(ln_out, KD)
            dve.sem_inc(free["l3"], 2)

            def mul3(n, j):
                dve.wait_ge(silu_ok["l3"], n + 1)
                v = halves(hid[:, ds(n, 1), :].rearrange("p o n -> p (o n)"))
                tt(v, v, banks(4 * (j % 2) + 2), ALU.mult).then_inc(free["l3"], 1)
            with dve.Fori(0, FT // SLOTS) as i:
                for j in range(SLOTS):
                    mul3(SLOTS * i + j, j)
            for j in range(2):
                mul3(FT // SLOTS * SLOTS + j, j)
            dve.sem_inc(free["l4"], 2)
            for j in range(KD // 2):
                residual("l4", j, 4 * (j % 2), ln_ready if j == 3 else None)
            layer_norm(1)

            link(dve.memset(raw[:, :, 0:HIST], 0.0))
            dve.sem_inc(cv_y, 2)

            def conv(n, j):
                dve.wait_ge(free["xb"], n + 3)
                s = 2 * (j % 2)
                for q in range(2):
                    smp = raw[:, s + q, HIST + SEQ:].rearrange("p (b t) -> p b t", b=DEC_B)
                    cp(smp[:, :, 0:HIST], ssd_hist[:, ds(2 * n + q, 1), :].rearrange("p o (b t) -> p (o b) t", b=DEC_B))
                    cp(ssd_tail[:, ds(2 * n + q, 1), HIST:].rearrange("p o (b t) -> p (o b) t", b=DEC_B), smp[:, :, DEC_T:])
                link(cp(ssd_tail[:, ds(2 * n, 2), 0:HIST], raw[:, s:s + 2, SEQ:SEQ + HIST]))
                dve.wait_ge(cv_s, n + 1)
                for w in (3, 2, 1, 0):
                    for q in range(2):
                        x = raw[:, s + q, w:w + N]
                        cw = conv_w_s[:, w, ds(2 * n + q, 1)]
                        if w == 3:
                            i = tsc(acc[:, q, 0:N], x, cw, conv_b_s[:, ds(2 * n + q, 1)], ALU.mult, ALU.add)
                        else:
                            i = stt(acc[:, q, 0:N], x, cw, acc[:, q, 0:N], ALU.mult, ALU.add)
                    if w:
                        link(i)
                i.then_inc(cv_y, 1)
            with dve.Fori(0, XBC // 2 // SLOTS) as i:
                link.enter(i, 4 * SLOTS)
                for j in range(SLOTS):
                    conv(SLOTS * i + j, j)
            link.leave(XBC // 2 // SLOTS)

            dve.sem_inc(free["dt"], 1)
            dve.wait_ge(used, done("dt", 0))
            dve.wait_ge(cv_s, XBC // 2 + 1)
            dve.wait_ge(in_small, 48)
            R = lambda n: tmpr[0:SH, n, :]
            W = lambda n: rows[0:SH, n, :]
            link(tsc(halves(R(0)), ps[0:SH, 0:2, 0:HALF], dt_par[:, 0:1], None, ALU.add))
            stt(R(1), R(0), -1.0, R(0), ALU.mult, ALU.max).then_inc(dt_a, 1)
            dve.wait_ge(dt_e, 1)
            link(tsc(dt_par[:, 3:4], dt_par[:, 3:4], -1.0, None, ALU.mult))
            link(tsc(R(3), R(2), 1.0, None, ALU.add))
            tsc(R(4), R(3), -1.0, None, ALU.add).then_inc(dt_u, 1)
            dve.wait_ge(dt_l, 1)
            link(tsc(R(3), R(4), 0.0, None, ALU.is_equal))
            link(tt(R(4), R(4), R(3), ALU.add))
            link(dve.reciprocal(R(4), R(4)))
            link(tt(R(1), R(1), R(3), ALU.add))
            link(tt(R(1), R(1), R(2), ALU.mult))
            link(tt(R(1), R(1), R(4), ALU.mult))
            link(stt(W(DTR), R(0), 0.0, R(1), ALU.max, ALU.add))
            link(tsc(R(0), W(DTR), dt_par[:, 3:4], None, ALU.mult))
            link(dve.tensor_tensor_scan(W(CSR), run_row[:], R(0), 0.0, ALU.mult, ALU.add))
            csp = W(CSR)[:, 0:SEQ].rearrange("p (c n) -> p c n", c=NCH)
            css = W(CSR)[:, SEQ:T].rearrange("p (c n) -> p c n", c=DEC_B)
            tt(R(0)[:, 0:SEQ].rearrange("p (c n) -> p c n", c=NCH), csp[:, :, P - 1:P].broadcast_to([SH, NCH, P]), csp, ALU.subtract)
            tt(R(0)[:, SEQ:T].rearrange("p (c n) -> p c n", c=DEC_B), css[:, :, DEC_T - 1:DEC_T].broadcast_to([SH, DEC_B, DEC_T]), css,
               ALU.subtract).then_inc(cs_ok, 1)
            dve.wait_ge(ec_ok, 1)
            tt(R(1)[:, 0:SH * NCH].rearrange("p (h c) -> p h c", h=SH), ident[0:SH, 0:SH].unsqueeze(2).broadcast_to([SH, SH, NCH]),
               W(ECR)[:, P - 1:SEQ:P].unsqueeze(1).broadcast_to([SH, SH, NCH]), ALU.mult)
            tt(W(WDR), R(0), W(DTR), ALU.mult).then_inc(row_ok, 1)
            dve.wait_ge(tk_mm, 1)
            for n, sc in enumerate((1.0, -1.0, 1.0)):
                tsc(tok[:, n, 0:NCH * SH], ps[:, 2 + n, 0:NCH * SH], sc, None, ALU.mult)
                tsc(tok[0:NS, n, NCH * SH:], ps[0:NS, 2 + n, NCH * SH:5 * SH], sc, None, ALU.mult)
            cp(dec_p[:], ps[:, 5, 0:SH * NCH])
            cp(dec_s[:].rearrange("p t b -> p (t b)"), ps[:, 6, 0:P])
            cp(d_exp, ps[:, 6, P:P + XT]).then_inc(tk_up, 1)
            dve.wait_ge(tk_up, 1)

            for g in range(SG):
                dve.wait_ge(g_mm, g + 1)
                for dst, which in ((x_dt, 0), (x_w, 2)):
                    fac = tok[:, which, 0:NCH * SH].rearrange("p (c h) -> p c h", c=NCH)
                    for j in range(2):
                        h = 4 * g + 2 * j
                        tt(dst[:, 0:NCH, j * P:(j + 1) * P].rearrange("p c (h n) -> p c h n", h=2),
                           ps[:, 3 + j, :].rearrange("p (c h n) -> p c h n", c=NCH, h=2),
                           fac[:, :, h:h + 2].unsqueeze(3).broadcast_to([P, NCH, 2, 64]), ALU.mult)
                    i = tt(dst[0:NS, NCH, :].rearrange("p (h n) -> p h n", h=4), ps[0:NS, 1, 256:512].rearrange("p (h n) -> p h n", h=4),
                           tok[0:NS, which, NCH * SH + 4 * g:NCH * SH + 4 * g + 4].unsqueeze(2).broadcast_to([NS, 4, 64]), ALU.mult)
                dve.wait_ge(g_up_a, g + 1)
                tt(b_seq[0:NS], ps[0:NS, 1, P:2 * P].unsqueeze(1).broadcast_to([NS, DEC_B, P]),
                   of_seq[:].unsqueeze(2).broadcast_to([NS, DEC_B, P]), ALU.mult).then_inc(g_up, 1)
                dve.wait_ge(st_mm, g + 1)
                dec = dec_p[:].rearrange("p (h c) -> p h c", h=SH)
                link(cp(state[:, 0, :], ps[:, 5, 0:256]))
                for c in range(1, NCH):
                    v = state[:, c, :].rearrange("p (h n) -> p h n", h=4)
                    link(tt(v, state[:, c - 1, :].rearrange("p (h n) -> p h n", h=4), dec[:, 4 * g:4 * g + 4, c:c + 1].broadcast_to([P, 4, 64]), ALU.mult))
                    link(tt(state[:, c, :], state[:, c, :], ps[:, 5 + c // 2, (c % 2) * 256:(c % 2 + 1) * 256], ALU.add))
                dve.sem_inc(st_up, 1)
                for j in range(2):
                    t = 2 * g + j
                    for hh in range(2):
                        h = 2 * t + hh
                        dve.wait_ge(e_ok, h + 1)
                        dve.wait_ge(yt_mm, h)
                        tt(m_buf[:, 0:SEQ], ps[:, 0, :], e_buf[:, 0:SEQ], ALU.mult)
                        tt(m_buf[0:NS, SEQ:T], ps[0:NS, 1, 0:NS], e_buf[0:NS, SEQ:T], ALU.mult).then_inc(m_ok, 1)
                    dve.wait_ge(yt_mm, 2 * t + 2)
                    tt(t_buf[:, P:SEQ], exs[:, P:SEQ], ps[:, 3, P:SEQ], ALU.mult)
                    tt(t_buf[:, SEQ:T], exs[:, SEQ:T], ps[:, 3, 0:NS], ALU.mult)
                    stt(xbc[:, t, 0:SEQ], xbc[:, t, 0:SEQ], d_exp[:, t:t + 1], ps[:, 2, :], ALU.mult, ALU.add)
                    link(stt(xbc[:, t, SEQ:T], xbc[:, t, SEQ:T], d_exp[:, t:t + 1], ps[:, 6, 0:NS], ALU.mult, ALU.add))
                    tt(xbc[:, t, P:T], xbc[:, t, P:T], t_buf[:, P:T], ALU.add).then_inc(y_ok, 1)
                    dve.wait_ge(ss_mm, t + 1)
                    link(tt(h0n[:], h0n[:], dec_s[:, t, :].unsqueeze(2).broadcast_to([P, DEC_B, P]), ALU.mult))
                    v = h0n[:].rearrange("p (u b) n -> p u (b n)", u=2)
                    tt(v, v, ps[:, 4:6, :], ALU.add).then_inc(ss_ok, 1)
                dve.wait_ge(fs_mm, g + 1)
                dve.wait_ge(fs_out, 16 * g)
                cp(st_out[:].rearrange("p a n -> p (a n)"), ps[:, 3, 0:2 * P]).then_inc(fs_up, 1)

            dve.sem_inc(z_gate, 1)
            dve.sem_inc(z_ok, 1)

            def z_unit(i, j):
                n = SLOTS * i + j
                v = xbc[:, ds(2 * n, 2), :]
                dve.wait_ge(free["z"], n + 2)
                tt(v, v, z_s[:], ALU.mult).then_inc(z_gate, 1)
                dve.wait_ge(z_rt, n + 2)
                link(dve.reciprocal(z_i[:], z_r[:]))
                for q in range(2):
                    y = xbc[:, ds(2 * n + q, 1), :].rearrange("p o n -> p (o n)")
                    last = stt(y, y, norm_g[:, ds(2 * n + q, 1)], z_i[:], ALU.mult, ALU.mult)
                last.then_inc(z_ok, 1)
            with dve.Fori(0, XT // 2 // SLOTS) as i:
                link.enter(i, SLOTS)
                for j in range(SLOTS):
                    z_unit(i, j)
            link.leave(XT // 2 // SLOTS)
            dve.wait_ge(z_ok, XT // 2 + 1)
            dve.sem_inc(free["l6"], 2)
            for j in range(KD // 2):
                residual("l6", j, 4 * (j % 2), ln_ready if j == 3 else None)
            layer_norm(2)
            dve.wait_ge(ss_out, 16 * XT)
            dve.wait_ge(fs_out, 16 * SG)
            for n in range(9):
                dve.wait_ge(tl_mm, n + 1)
                if n < 8:
                    cp(tail_s[0:27, n * 512:(n + 1) * 512], ps[0:27, n % 2, :]).then_inc(tl_up, 1)
                else:
                    cp(tail_l[0:36, :], ps[0:36, n % 2, :]).then_inc(tl_up, 1)

            for k in range(KD):
                dve.wait_ge(ln_out, 2 * KD + k + 1)
                tsc(yacc[:, k, :], xT[:, k, :], ALPHA, None, ALU.mult)
            lg, gts = stat[:, 40:80], stat[:, 0:40]
            link(dve.memset(lg, 0.0))
            dve.wait_ge(rt_mm, 1)
            cp(lg[:, 0:32], ps[:, 4, 0:32])
            link(cp(lg[0:NS, 32:40], ps[0:NS, 4, 32:40]))
            l3 = lg.rearrange("p (c e) -> p c e", c=5)
            gg = g_w[:, 10:90].rearrange("p (u n) -> p u n", u=2)
            gt = g_w[:, 100:140].rearrange("p (c e) -> p c e", c=5)
            rank = g_w[:, 140:180].rearrange("p (c e) -> p c e", c=5)
            sel = g_w[:, 180:220].rearrange("p (c e) -> p c e", c=5)
            link(dve.memset(rank, 0.0))
            for o in range(NE):
                other = l3[:, :, o:o + 1].broadcast_to([P, 5, NE])
                link(tt(gt, other, l3, ALU.is_gt))
                link(tt(rank, rank, gt, ALU.add))
                if o < NE - 1:
                    n = NE - 1 - o
                    link(tt(gt[:, :, 0:n], l3[:, :, o:o + 1].broadcast_to([P, 5, n]), l3[:, :, o + 1:], ALU.is_equal))
                    link(tt(rank[:, :, o + 1:], rank[:, :, o + 1:], gt[:, :, 0:n], ALU.add))
            best = [g_w[:, 220:225], g_w[:, 225:230]]
            for r in range(2):
                link(tsc(sel, rank, float(r), None, ALU.is_equal))
                link(tt(sel, sel, l3, ALU.mult))
                link(dve.tensor_reduce(best[r], sel, AX, ALU.add))
            tt(g_w[:, 5:10], best[1], best[0], ALU.subtract).then_inc(rt_d, 1)
            dve.wait_ge(rt_e, 1)
            link(tsc(best[0], g_w[:, 0:5], 1.0, None, ALU.add))
            link(dve.reciprocal(best[0], best[0]))
            link(tt(best[1], best[0], g_w[:, 0:5], ALU.mult))
            G = gts.rearrange("p (c e) -> p c e", c=5)
            for r in range(2):
                link(tsc(sel, rank, float(r), None, ALU.is_equal))
                link(tt(sel, sel, best[r].unsqueeze(2).broadcast_to([P, 5, NE]), ALU.mult))
                if r == 0:
                    link(cp(G, sel))
            tt(G, G, sel, ALU.add).then_inc(rt_g, 1)
            dve.wait_ge(gt_mm, 1)
            cp(gT[0:NE, 0:SEQ], ps[0:NE, 4, :])
            cp(gT[0:NE, SEQ:T], ps[0:NE, 5, 0:NS]).then_inc(gt_up, 1)
            for e in range(NE):
                dve.wait_ge(gb_mm, e + 1)
                cp(halves(gb[:, e, :]), banks(2 * (e % 4))).then_inc(gb_up, 1)
            dve.wait_ge(gb_up, NE)
            dve.sem_inc(free["eu"], 2)
            dve.sem_inc(free["ed"], 2)

            with dve.Fori(0, NE) as e:
                link.enter(e, FET)
                for m in range(FET):
                    dve.wait_ge(silu_ok["eu"], FET * e + m + 1)
                    v = halves(e_hid[:, m, :])
                    link(tt(v, v, banks(4 * (m % 2) + 2), ALU.mult))
                    tt(e_hid[:, m, :], e_hid[:, m, :], gb[:, ds(e, 1), :].rearrange("p o n -> p (o n)"), ALU.mult).then_inc(free["eu"], 1)
                for m in range(KD // 2):
                    dve.wait_ge(used, SLOTS + C_MOE + PER_E * e + FET + m + 1)
                    b = 4 * ((FET + m) % 2)
                    for q in range(2):
                        last = tt(halves(yacc[:, 2 * m + q, :]), halves(yacc[:, 2 * m + q, :]), banks(b + 2 * q), ALU.add)
                    last.then_inc(free["ed"], 1)
            link.leave(NE)
            dve.wait_ge(free["ed"], NE * (KD // 2) + 2)
            for k in range(KD):
                last = cp(xT[:, k, :], yacc[:, k, :])
            last.then_inc(ln_ready, 1)
            layer_norm(3)
            for n in range(10):
                dve.wait_ge(out_mm, n + 1)
                m = CHUNKS[n // 2][0]
                cp(y_out[0:m, n // 2, 512 * (n % 2):512 * (n % 2) + 512], ps[0:m, n % 4, :]).then_inc(out_up, 1)


_INS = ["x_prompt", "x_sample", "cache_k", "cache_v", "page_table", "state_lru_h", "state_lru_conv", "state_ssm",
        "state_ssd_conv", "w_in_even", "lru_conv_w", "lru_conv_b", "lru_w_a", "lru_b_a", "lru_w_x", "lru_b_x", "lru_lambda",
        "w_out_even", "ssd_w_in", "ssd_conv_w", "ssd_conv_b", "ssd_dt_bias", "ssd_a_log", "ssd_d", "ssd_norm_g", "ssd_w_out",
        "ffn_w1", "ffn_w3", "ffn_w2", "moe_router", "moe_w1", "moe_w3", "moe_w2", "ln_mix_g", "ln_mix_b", "ln_ffn_g", "ln_ffn_b"]
_OUTS = [("y_prompt", (1, SEQ, D)), ("y_sample", (DEC_B, DEC_T, D)),
         ("k_prompt", (1, 1, SEQ, HEADS, HD)), ("v_prompt", (1, 1, SEQ, HEADS, HD)),
         ("k_sample", (1, DEC_B, DEC_T, HEADS, HD)), ("v_sample", (1, DEC_B, DEC_T, HEADS, HD)),
         ("lru_h_prompt", (1, 1, 512)), ("lru_h_sample", (1, DEC_B, 512)),
         ("lru_conv_prompt", (1, 1, HIST, 512)), ("lru_conv_sample", (1, DEC_B, HIST, 512)),
         ("ssm_prompt", (1, 1, SH, 64, SN)), ("ssm_sample", (1, DEC_B, SH, 64, SN)),
         ("ssd_conv_prompt", (1, 1, HIST, SCONV)), ("ssd_conv_sample", (1, DEC_B, HIST, SCONV))]


def kernel(**inputs):
    import concourse.bacc as bacc
    from concourse.bass_utils import run_bass_kernel_spmd

    nc = bacc.Bacc("TRN2", target_bir_lowering=False, num_devices=1)
    arrays, I, O = {}, {}, {}
    for name in _INS:
        a = np.ascontiguousarray(inputs[name])
        arrays["in_" + name] = a
        I[name] = nc.dram_tensor("in_" + name, a.shape, mybir.dt.from_np(a.dtype), kind="ExternalInput").ap()
    for name, shape in _OUTS:
        O[name] = nc.dram_tensor("out_" + name, shape, F32, kind="ExternalOutput").ap()
    build(nc, I, O)
    r = run_bass_kernel_spmd(nc, [arrays], core_ids=[0])
    return tuple(r.results[0]["out_" + name] for name, _ in _OUTS)
```

```python
from contextlib import ExitStack

import numpy as np

import concourse.bass as bass
from concourse import mybir

F32 = mybir.dt.float32
F32R = mybir.dt.float32r
I32 = mybir.dt.int32
ALU = mybir.AluOpType
ACT = mybir.ActivationFunctionType
AX = mybir.AxisListType.X
ds = bass.ds

P = 128
D = 1024
KD = D // P
SEQ, DEC_B, DEC_T = 512, 8, 8
NS = DEC_B * DEC_T
T = SEQ + NS
HALF = T // 2
NCH = SEQ // P
CONV_W = 4
HIST = CONV_W - 1
PADT = HIST + SEQ + DEC_B * (HIST + DEC_T)
HEADS, HD = 8, 64
AW = HEADS * HD
AT = AW // P
LT = 512 // P
PAGE, NPAGES, NPOOL = 128, 8, 80
QUAD = 4
BLK = 256
NBLK = NPAGES * PAGE // BLK
FF, FT = 2816, 2816 // P
SG, SH, SN = 8, 32, 128
XT, BC = 2048 // P, 8
XBC = XT + 2 * BC
SCONV = XBC * P
SIN = 2048 + SCONV + SH
NE, FE, FET = 8, 1408, 1408 // P
ALPHA = float(4 ** 0.25)
LN_EPS, RMS_EPS = 1e-5, 1e-6
NEG = -1e30
SLOTS = 4
KMAX = 11
CW = 2 * P
RAW = 3
CAP = 192
RMAX = 13
BIG = 4096.0

C_L1 = 0
C_L2 = C_L1 + 10
C_L3 = C_L2 + KD // 2
C_L4 = C_L3 + FT
C_XBC = C_L4 + KD
C_DT = C_XBC + XBC // 2
C_Z = C_DT + 1
C_L6 = C_Z + XT // 2
C_MOE = C_L6 + KD
PER_E = FET + KD // 2
TILES = 2 * PER_E


class Chain:

    def __init__(self, eng, sem):
        self.eng, self.sem, self.n, self.turn = eng, sem, 0, 0

    def __call__(self, ins):
        ins.then_inc(self.sem, 1)
        self.n += 1
        self.eng.wait_ge(self.sem, self.n + self.turn)

    def enter(self, i, per):
        self.per, self.n0, self.turn = per, self.n, i * per

    def leave(self, turns):
        assert self.n - self.n0 == self.per
        self.n, self.turn = self.n0 + turns * self.per, 0


def build(nc, I, O):
    ctx = ExitStack()
    with ctx:
        def sb(name, shape, dt=F32):
            return ctx.enter_context(nc.sbuf_tensor(name, shape, dt))

        def sem(name):
            return ctx.enter_context(nc.semaphore(name))

        ring = sb("ring", [P, SLOTS, KMAX, CW])
        ring_base = nc.sbuf_base - 4 * SLOTS * KMAX * CW
        xT = sb("xT", [P, KD, T])
        par = sb("par", [P, 3, P])
        lru_h0 = sb("lru_h0", [P, LT, DEC_B])
        lru_hist = sb("lru_hist", [P, LT, DEC_B * HIST])
        ssd_hist = sb("ssd_hist", [P, XBC, DEC_B * HIST])
        ssd_tail = sb("ssd_tail", [P, XBC, HIST + DEC_B * HIST])
        lru_tail = sb("lru_tail", [P, LT, 36])
        ident = sb("ident", [P, P])
        ones = sb("ones", [P, P])
        qk_mask = sb("qk_mask", [P, P])
        sl_mask = sb("sl_mask", [P, P])
        seq_mask = sb("seq_mask", [NS, NS])
        seq_maskT = sb("seq_maskT", [NS, NS])
        expand = sb("expand", [NS, 4, P])
        of_seq = sb("of_seq", [NS, DEC_B])
        run_row = sb("run_row", [SH, T])
        tri = sb("tri", [P, 8, 8])
        gate_w = sb("gate_w", [P, 2, LT, P])
        router = sb("router", [P, KD, NE])
        dt_par = sb("dt_par", [SH, 4])
        eps = sb("eps", [P, 2])
        pages = sb("pages", [1, DEC_B * NPAGES], I32)
        stat = sb("stat", [P, 160])
        before = sb("before", [P, P])
        iota_i = sb("iota_i", [P, CAP], I32)
        expert_of = sb("expert_of", [1, 16], I32)
        n_rounds = sb("n_rounds", [1, 1], I32)
        ARENA = nc.sbuf_bytes_remaining // 4 - 16
        arena = sb("arena", [P, ARENA])
        arena_base = nc.sbuf_base - 4 * ARENA
        ps = ctx.enter_context(nc.psum_tensor("ps", [P, 8, 512], F32))

        def at(off, *dims):
            n = int(np.prod(dims))
            assert off + n <= ARENA, (off, dims, ARENA)
            v = arena[:, off:off + n]
            if len(dims) == 2:
                return v.rearrange("p (a b) -> p a b", a=dims[0])
            if len(dims) == 3:
                return v.rearrange("p (a b c) -> p a b c", a=dims[0], b=dims[1])
            return v

        def spare(slot, off, *dims):
            v = ring[:, slot].rearrange("p k n -> p (k n)")[:, off:off + int(np.prod(dims))]
            if len(dims) == 2:
                return v.rearrange("p (a b) -> p a b", a=dims[0])
            if len(dims) == 3:
                return v.rearrange("p (a b c) -> p a b c", a=dims[0], b=dims[1])
            return v

        def split_spare(name, slot, off, *dims):
            return nc.alloc_sbuf_tensor_at(name, [P, *dims], F32R, offset=ring_base + 4 * (slot * KMAX * CW + off))

        def split_at(name, off, *dims):
            return nc.alloc_sbuf_tensor_at(name, [P, *dims], F32R, offset=arena_base + 4 * off)

        proj = at(0, 20, T)
        cat = at(11520, 8, T)
        xin = at(16128, 5, D)
        shist_in = at(21248, SCONV)
        par_in = at(25344, 3, P)
        h0_in = at(25728, 512)
        lhist_in = at(26240, 512)
        u_pad = at(16128, LT, PADT)
        uc = at(18540, LT, T)
        u_acc = at(28356, PADT)
        lru_a = at(21444, LT * T)
        lru_t = at(23748, LT * T)
        lru_i = at(26052, LT * T)
        qx = at(6912, AT, DEC_B, NS)
        k_tok = at(8960, 5, AW)
        v_tok = at(16128, 5, AW)
        kv = [at(18688 + 2048 * n, QUAD, AW) for n in range(4)]
        pp = at(26880, 2, 512)
        ppt = at(27904, 2, 512)
        ks_T = at(28928, AT, NS)
        kt = [at(2048 * n, AT, QUAD * PAGE) for n in range(3)]
        p_s = at(29184, NPAGES * PAGE + NS)
        p_sT = at(30272, 9, P)
        hid = at(0, FT, T)
        sq = at(15552, KD, T)
        std = at(20160, T)
        rstd = at(20736, T)
        xbc = at(0, XBC, T)
        raw = at(18432, 4, PADT)
        acc = at(20844, 2, PADT)
        rows = at(18432, 4, T)
        DTR, CSR, ECR, WDR = range(4)
        tmpr = at(21472, 5, T)
        tok = at(20736, 3, 5 * SH)
        dec_p = at(21216, SH * NCH)
        dec_s = at(21344, XT, DEC_B)
        b_tok = at(21472, 5, P)
        x_dt = at(22112, 5, 256)
        x_w = at(23392, 5, 256)
        state = at(24672, NCH, 256)
        b_seq = at(25696, DEC_B, P)
        h0n = [spare(3, 1024 * n, DEC_B, P) for n in range(2)]
        ident_r = split_spare("ident_r", 3, 2048, P)
        sl_mask_r = split_spare("sl_mask_r", 3, 2176, P)
        cs_h, cs_l = split_spare("cs_h", 0, 0, SEQ), split_spare("cs_l", 3, 2304, SEQ)
        ebc = spare(0, 512, 2, T)
        ce = spare(0, 1664, 2, T)
        st_out = at(26720, 2, 2, P)
        h0t = at(27744, DEC_B, P)
        e_buf = at(28768, 2, T)
        m_buf = at(29920, 2, T)
        d_exp = stat[:, 0:XT]
        z_s = at(18432, 2, T)
        z_q = at(19584, 2, T)
        z_r = at(20736, T)
        z_i = at(21312, T)
        xt_h, xt_l = split_at("xt_h", 0, 5, D), split_at("xt_l", 5120, 5, D)
        xg_h, xg_l = split_at("xg_h", 10240, KD, CAP), split_at("xg_l", 11776, KD, CAP)
        h_h, h_l = split_at("h_h", 13312, FET, CAP), split_at("h_l", 15424, FET, CAP)
        yt_h, yt_l = split_at("yt_h", 13312, 2, D), split_at("yt_l", 15360, 2, D)
        w_h, w_l = split_at("w_h", 17536, RAW, KMAX, P), split_at("w_l", 21760, RAW, KMAX, P)
        hot = split_at("hot", 25984, 5, CAP)
        hotT = split_at("hotT", 26944, 2, T)
        yg = at(28096, KD, CAP)
        h_s = at(29632, 2, CAP)
        h_m = at(30016, 2, CAP)
        slot_of = at(30400, RMAX + 2, 5)
        gate_of = at(30480, RMAX + 2, 5)
        iota = at(30560, CAP)
        gate_now = at(30760, 5)
        slot_gate = at(30768, 2)
        g_w = at(24128, 1856)
        tail_s = at(26000, SCONV)
        tail_l = at(30096, 512)
        y_out = at(0, 5, D)

        conv_w_s = par[:, 0, :].rearrange("p (w t) -> p w t", w=CONV_W)
        conv_b_s = par[:, 1, 0:32]
        norm_g = par[:, 1, 32:48]
        ln_g = [par[:, 1, 48:56], par[:, 1, 80:88], par[:, 1, 56:64], par[:, 1, 88:96]]
        ln_b = [par[:, 1, 64:72], par[:, 1, 96:104], par[:, 1, 72:80], par[:, 1, 104:112]]
        conv_w_l = par[:, 2, 0:16].rearrange("p (w t) -> p w t", w=CONV_W)
        conv_b_l = par[:, 2, 16:20]
        b_gate = [par[:, 2, 20:24], par[:, 2, 24:28]]
        lam = par[:, 2, 28:32]

        loaded = [sem(f"loaded{s}") for s in range(SLOTS)]
        moe_loaded = [sem(f"moe_loaded{s}") for s in range(RAW)]
        used = sem("used")
        in_x, in_par, in_hist = sem("in_x"), sem("in_par"), sem("in_hist")
        in_gatew, in_small, in_router, in_pages = sem("in_gatew"), sem("in_small"), sem("in_router"), sem("in_pages")
        const_ok, pool_c, dve_c, act_c = sem("const_ok"), sem("pool_c"), sem("dve_c"), sem("act_c")
        x_tr, x_up = sem("x_tr"), sem("x_up")
        p_tr, p_up = sem("p_tr"), sem("p_up")
        stages = ["l1", "l2", "l3", "l4", "xb", "dt", "z", "l6"]
        first = dict(l1=C_L1, l2=C_L2, l3=C_L3, l4=C_L4, xb=C_XBC, dt=C_DT, z=C_Z, l6=C_L6)
        per_unit = dict(l4=2, l6=2)

        def done(stage, n):
            return SLOTS + first[stage] + per_unit.get(stage, 1) * (n + 1)

        free = {s: sem(f"free_{s}") for s in stages}
        free_act1 = sem("free_act1")
        silu_ok = {s: sem(f"silu_{s}") for s in ("l3",)}
        ln_ready = sem("ln_ready")
        ln_mu, ln_c, ln_sq, ln_var, ln_std, ln_n, ln_out = [sem(f"ln_{n}") for n in ("mu", "c", "sq", "var", "std", "n", "out")]
        uc_ok, gr_mm, gr_ok, gi_mm, gi_ok = [sem(n) for n in ("uc_ok", "gr_mm", "gr_ok", "gi_mm", "gi_ok")]
        lam_e, lam_u, lam_l = sem("lam_e"), sem("lam_u"), sem("lam_l")
        la_ok, a_ok, a2_ok, s_ok, g_ok = [sem(n) for n in ("la_ok", "a_ok", "a2_ok", "s_ok", "g_ok")]
        lru_end = sem("lru_end")
        kvt_tr, kvt_up, kvt_up_a, kv_out = sem("kvt_tr"), sem("kvt_up"), sem("kvt_up_a"), sem("kv_out")
        qx_ok = sem("qx_ok")
        sc_mm, mx_ok, ex_ok, pn_ok, pt_mm, pt_ok, o_mm, o_up = [sem(n) for n in ("sc_mm", "mx_ok", "ex_ok", "pn_ok", "pt_mm", "pt_ok", "o_mm", "o_up")]
        kv_in = [sem(f"kv_in{n}") for n in range(4)]
        kt_mm, kt_dve, kt_act, qs_mm = sem("kt_mm"), sem("kt_dve"), sem("kt_act"), sem("qs_mm")
        s_bias, s_ex, s_pn, s_ptm, s_ptu, s_o, s_ou = [sem(n) for n in ("s_bias", "s_ex", "s_pn", "s_ptm", "s_ptu", "s_o", "s_ou")]
        cv_y, cv_s = sem("cv_y"), sem("cv_s")
        dt_a, dt_e, dt_u, dt_l, cs_ok, ec_ok, row_ok = [sem(n) for n in ("dt_a", "dt_e", "dt_u", "dt_l", "cs_ok", "ec_ok", "row_ok")]
        tk_mm, tk_up = sem("tk_mm"), sem("tk_up")
        g_mm, g_up, g_up_a, st_mm, st_up = [sem(n) for n in ("g_mm", "g_up", "g_up_a", "st_mm", "st_up")]
        h0_in_s, h0_tr, h0_up, hd_ok = [sem("h0_in_even"), sem("h0_in_odd")], sem("h0_tr"), sem("h0_up"), sem("hd_ok")
        bc_mm, eb_ok, cs_mm, e_ok, m_ok, yt_mm, y_ok = [sem(n) for n in ("bc_mm", "eb_ok", "cs_mm", "e_ok", "m_ok", "yt_mm", "y_ok")]
        ss_mm, ss_ok, ss_out = sem("ss_mm"), sem("ss_ok"), sem("ss_out")
        fs_mm, fs_up, fs_out = sem("fs_mm"), sem("fs_up"), sem("fs_out")
        z_gate, z_sqd, z_sum, z_rt, z_ok = [sem(n) for n in ("z_gate", "z_sqd", "z_sum", "z_rt", "z_ok")]
        tl_mm, tl_up, tl_out = sem("tl_mm"), sem("tl_up"), sem("tl_out")
        rt_mm, rt_d, rt_e, rt_m, ct_mm, rt_ok = [sem(n) for n in ("rt_mm", "rt_d", "rt_e", "rt_m", "ct_mm", "rt_ok")]
        xt_mm, xt_hi, xt_lo = sem("xt_mm"), sem("xt_hi"), sem("xt_lo")
        w_hi, w_lo, w_used = sem("w_hi"), sem("w_lo"), sem("w_used")
        hot_ok, ga_mm, ga_hi, ga_lo = sem("hot_ok"), sem("ga_mm"), sem("ga_hi"), sem("ga_lo")
        e_silu, e_bank, e_h, d_ok = sem("e_silu"), sem("e_bank"), sem("e_h"), sem("d_ok")
        ty_mm, ty_hi, ty_lo, sc_y, sc_ok = sem("ty_mm"), sem("ty_hi"), sem("ty_lo"), sem("sc_y"), sem("sc_ok")
        th_mm, th_ok, sg_mm, sg_ok = sem("th_mm"), sem("th_ok"), sem("sg_mm"), sem("sg_ok")
        out_mm, out_up, out_st = sem("out_mm"), sem("out_up"), sem("out_st")

        block = ctx.enter_context(nc.Block())

        def cols(w, k0, nk, c0):
            return w[k0 * P:(k0 + nk) * P, :].rearrange("(k p) n -> p k n", p=P)[:, :, ds(c0, CW)]

        @block.sync
        def _(sp):
            for c in range(NCH):
                sp.dma_start(xin[:, c, :], I["x_prompt"][0, c * P:(c + 1) * P, :]).then_inc(in_x, 16)
            sp.dma_start(xin[0:NS, NCH, :], I["x_sample"].rearrange("b t d -> (b t) d")).then_inc(in_x, 16)

            def load(c, i, parts):
                slot = c % SLOTS
                sp.wait_ge(used, c + 1 + SLOTS * i)
                for dst, src in parts(ring[:, slot]):
                    sp.dma_start(dst, src).then_inc(loaded[slot], 16)

            def pair(w, k0, nk, c0):
                h = nk // 2
                return lambda s: [(s[:, 0:h, :], cols(w, k0, h, c0)), (s[:, h:nk, :], cols(w, k0 + h, nk - h, c0))]

            def up(w1, w3, c0):
                def tile(w):
                    return w.rearrange("(k p) n -> p k n", p=P)[:, :, ds(c0, P)]
                return lambda s: [(s[:, 0:KD, 0:P], tile(w1)), (s[:, 0:KD, P:CW], tile(w3))]

            w = I["w_in_even"][0]
            with sp.Fori(0, 2) as i:
                for j in range(SLOTS):
                    load(C_L1 + j, i, pair(w, 0, KD, (i * SLOTS + j) * CW))
            for j in range(8, 10):
                load(C_L1 + j, 0, pair(w, 0, KD, j * CW))

            sp.wait_ge(in_pages, 16)
            sp.wait_ge(lru_end, 1)
            for pr in range(DEC_B // 2):
                for which, cache in ((0, I["cache_k"]), (1, I["cache_v"])):
                    for q in range(4):
                        if which == 1:
                            sp.wait_ge(kt_mm, 4 * (4 * pr + q + 1))
                        elif pr > 0:
                            sp.wait_ge(s_o, 2 * (pr - 1) + q // 2 + 1)
                        for pg in range(QUAD):
                            at_page = (2 * pr + q // 2) * NPAGES + (q % 2) * QUAD + pg
                            page = sp.value_load(pages[0:1, at_page:at_page + 1], min_val=0, max_val=NPOOL - 1)
                            sp.dma_start(kv[q][:, pg, :], cache[0][page].rearrange("t h d -> t (h d)")).then_inc(kv_in[q], 16)
            w = I["w_out_even"][0]
            for j in range(KD // 2):
                load(C_L2 + j, 0, pair(w, 0, KD, j * CW))
            w1, w3 = I["ffn_w1"][0], I["ffn_w3"][0]
            with sp.Fori(0, FT // SLOTS) as i:
                for j in range(SLOTS):
                    load(C_L3 + j, i, up(w1, w3, (i * SLOTS + j) * P))
            for j in range(FT // SLOTS * SLOTS, FT):
                load(C_L3 + j, 0, up(w1, w3, j * P))
            w = I["ffn_w2"][0]
            for j in range(KD // 2):
                for h in range(2):
                    load(C_L4 + 2 * j + h, 0, pair(w, KMAX * h, KMAX, j * CW))
            w = I["ssd_w_in"][0]
            with sp.Fori(0, XBC // 2 // SLOTS) as i:
                for j in range(SLOTS):
                    load(C_XBC + j, i, pair(w, 0, KD, (i * SLOTS + j) * CW + 2048))
            load(C_DT, 0, lambda s: [
                (s[:, 4 * h:4 * h + 4, 0:SH],
                 w[4 * h * P:(4 * h + 4) * P, 2048 + SCONV:SIN].rearrange("(k p) n -> p k n", p=P)) for h in range(2)])
            with sp.Fori(0, XT // 2 // SLOTS) as i:
                for j in range(SLOTS):
                    if j == 2:
                        sp.wait_ge(ss_out, 16 * XT)
                        sp.wait_ge(yt_mm, XT)
                    load(C_Z + j, i, pair(w, 0, KD, (i * SLOTS + j) * CW))
            w = I["ssd_w_out"][0]
            for j in range(KD // 2):
                for h in range(2):
                    load(C_L6 + 2 * j + h, 0, pair(w, 8 * h, 8, j * CW))
            sp.wait_ge(used, SLOTS + C_MOE)
            sp.sem_inc(w_lo, 2 * RAW)
            sp.wait_ge(rt_ok, 1)
            rounds = sp.value_load(n_rounds[0:1, 0:1], min_val=1, max_val=RMAX)

            def moe_chunk(r, e, m):
                sp.wait_ge(w_lo, 2 * (PER_E * r + m) + 2)
                w1, w3, w2 = (I[n][0][e] for n in ("moe_w1", "moe_w3", "moe_w2"))
                parts = up(w1, w3, m * P) if m < FET else pair(w2, 0, FET, (m - FET) * CW)
                for dst, src in reversed(parts(ring[:, m % RAW])):
                    sp.dma_start(dst, src).then_inc(moe_loaded[m % RAW], 16)
            e0 = sp.value_load(expert_of[0:1, 0:1], min_val=0, max_val=NE - 1)
            for m in range(2):
                moe_chunk(0, e0, m)
            with sp.Fori(0, rounds) as r:
                e = sp.value_load(expert_of[0:1, ds(r, 1)], min_val=0, max_val=NE - 1)
                for m in range(2, PER_E):
                    moe_chunk(r, e, m)
                e = sp.value_load(expert_of[0:1, ds(r + 1, 1)], min_val=0, max_val=NE - 1)
                for m in range(2):
                    moe_chunk(r + 1, e, m)

        @block.gpsimd
        def _(pool):
            def rowsof(ap, n):
                return ap.rearrange("o (t p) -> (o t) p", p=P)
            ld = pool.dma_start
            ld(par_in[:, 0, :], I["ssd_conv_w"][0].rearrange("w (t p) -> (w t) p", p=P)).then_inc(in_par, 16)
            for lo, name in ((0, "ssd_conv_b"), (32, "ssd_norm_g"), (48, "ln_mix_g"), (64, "ln_mix_b"),
                             (80, "ln_ffn_g"), (96, "ln_ffn_b")):
                src = rowsof(I[name], 0)
                ld(par_in[lo:lo + src.shape[0], 1, :], src).then_inc(in_par, 16)
            ld(par_in[0:16, 2, :], I["lru_conv_w"][0].rearrange("w (t p) -> (w t) p", p=P)).then_inc(in_par, 16)
            ld(par_in[16:20, 2, :], rowsof(I["lru_conv_b"], 0)).then_inc(in_par, 16)
            for lo, name in ((20, "lru_b_a"), (24, "lru_b_x"), (28, "lru_lambda")):
                ld(par_in[lo:lo + 4, 2, :], I[name][0].rearrange("(t h) d -> t (h d)", h=2)).then_inc(in_par, 16)
            ld(h0_in[0:DEC_B, :], I["state_lru_h"][0]).then_inc(in_hist, 16)
            ld(lhist_in[0:DEC_B * HIST, :], I["state_lru_conv"][0].rearrange("b t d -> (b t) d")).then_inc(in_hist, 16)
            ld(shist_in[0:DEC_B * HIST, :], I["state_ssd_conv"][0].rearrange("b t d -> (b t) d")).then_inc(in_hist, 16)
            ld(pages[0:1, :], I["page_table"].rearrange("b (o n) -> o (b n)", o=1)).then_inc(in_pages, 16)
            ld(router[:], I["moe_router"][0].rearrange("(k p) e -> p k e", p=P)).then_inc(in_router, 16)
            for n, name in enumerate(("ssd_dt_bias", "ssd_a_log", "ssd_d")):
                ld(dt_par[:, n:n + 1], I[name].rearrange("o h -> h o")).then_inc(in_small, 16)

            link = Chain(pool, pool_c)
            pool.memset(ident[:], 0.0)
            pool.memset(ones[:], 1.0)
            pool.memset(qk_mask[:], 0.0)
            pool.memset(sl_mask[:], 0.0)
            pool.memset(seq_mask[:], 0.0)
            pool.memset(seq_maskT[:], 0.0)
            pool.memset(expand[:], 0.0)
            pool.memset(of_seq[:], 1.0)
            pool.memset(run_row[:], 1.0)
            pool.memset(tri[:], 0.0)
            pool.memset(before[:], 1.0)
            pool.iota(iota_i[:], pattern=[[1, CAP]], base=0, channel_multiplier=0)
            pool.memset(eps[:, 0:1], LN_EPS)
            pool.memset(eps[:, 1:2], RMS_EPS)
            link(pool.memset(gate_w[:], 0.0))
            for hh in range(2):
                for n, name in enumerate(("lru_w_a", "lru_w_x")):
                    src = I[name][0].rearrange("(t h) d e -> h d t e", h=2)[hh]
                    ld(gate_w[64 * hh:64 * hh + 64, n, :, 64 * hh:64 * hh + 64], src).then_inc(in_gatew, 16)
            sel = pool.affine_select
            sel(out=ident[:], in_=ident[:], compare_op=ALU.not_equal, fill=1.0, base=0, pattern=[[-1, P]], channel_multiplier=1)
            sel(out=qk_mask[:], in_=qk_mask[:], compare_op=ALU.is_ge, fill=NEG, base=0, pattern=[[-1, P]], channel_multiplier=1)
            sel(out=sl_mask[:], in_=sl_mask[:], compare_op=ALU.is_ge, fill=NEG, base=0, pattern=[[1, P]], channel_multiplier=-1)
            sel(out=before[:], in_=before[:], compare_op=ALU.is_ge, fill=0.0, base=-1, pattern=[[1, P]], channel_multiplier=-1)
            sm = seq_mask[:].rearrange("p (b t) -> p b t", t=DEC_T)
            smt = seq_maskT[:].rearrange("p (b t) -> p b t", t=DEC_T)
            sel(out=sm, in_=sm, compare_op=ALU.is_ge, fill=NEG, base=0, pattern=[[DEC_T, DEC_B], [1, DEC_T]], channel_multiplier=-1)
            sel(out=smt, in_=smt, compare_op=ALU.is_ge, fill=NEG, base=0, pattern=[[-DEC_T, DEC_B], [-1, DEC_T]], channel_multiplier=1)
            sel(out=of_seq[:], in_=of_seq[:], compare_op=ALU.is_ge, fill=0.0, base=0, pattern=[[-DEC_T, DEC_B]], channel_multiplier=1)
            for pr in range(4):
                v = expand[:, pr, :].rearrange("p (b h q) -> p b h q", b=2, h=HEADS)
                sel(out=v, in_=v, compare_op=ALU.not_equal, fill=1.0, base=-2 * DEC_T * pr,
                    pattern=[[-DEC_T, 2], [0, HEADS], [-1, DEC_T]], channel_multiplier=1)
            for e in range(1, NE):
                pool.memset(tri[:, e, 0:e], 1.0)
            pool.memset(run_row[:, 0:SEQ:P], 0.0)
            link(pool.memset(run_row[:, SEQ:T:DEC_T], 0.0))
            sel(out=sm, in_=sm, compare_op=ALU.is_ge, fill=NEG, base=0, pattern=[[-DEC_T, DEC_B], [0, DEC_T]], channel_multiplier=1)
            sel(out=smt, in_=smt, compare_op=ALU.is_ge, fill=NEG, base=DEC_T - 1, pattern=[[DEC_T, DEC_B], [0, DEC_T]], channel_multiplier=-1)
            sel(out=of_seq[:], in_=of_seq[:], compare_op=ALU.is_ge, fill=0.0, base=DEC_T - 1, pattern=[[DEC_T, DEC_B]],
                channel_multiplier=-1).then_inc(const_ok, 1)

            st = pool.dma_start
            pool.wait_ge(kvt_up, 8)
            pool.wait_ge(kvt_up_a, 8)
            for t_, pn, sn in ((k_tok, "k_prompt", "k_sample"), (v_tok, "v_prompt", "v_sample")):
                dst = O[pn][0, 0].rearrange("(c p) h d -> p c (h d)", p=P)
                st(dst, t_[:, 0:NCH, :]).then_inc(kv_out, 16)
                st(O[sn][0].rearrange("b t h d -> (b t) (h d)"), t_[0:NS, NCH, :]).then_inc(kv_out, 16)
            def h0_load(t):
                pool.dma_start(h0n[t % 2], I["state_ssm"][0].rearrange("b (t h) p n -> t (h p) b n", h=2)[t]).then_inc(h0_in_s[t % 2], 16)
            pool.wait_ge(row_ok, 1)
            h0_load(0)
            h0_load(1)
            pool.wait_ge(tk_up, 1)
            for t in range(XT):
                pool.wait_ge(h0_tr, t + 1)
                h = h0n[t % 2]
                pool.tensor_tensor(h, h, dec_s[:, t, :].unsqueeze(2).broadcast_to([P, DEC_B, P]), ALU.mult).then_inc(hd_ok, 1)
                if t % 2 == 0:
                    g = t // 2
                    pool.wait_ge(fs_up, g + 1)
                    st(O["ssm_prompt"][0, 0].rearrange("(g t h) p n -> g (h p) t n", h=2, t=2)[g], st_out[:, g % 2]).then_inc(fs_out, 16)
                pool.wait_ge(ss_ok, t + 1)
                st(O["ssm_sample"][0].rearrange("b (t h) p n -> t (h p) b n", h=2)[t], h).then_inc(ss_out, 16)
                if t + 2 < XT:
                    pool.wait_ge(ss_out, 16 * (t + 1))
                    h0_load(t + 2)
            pool.wait_ge(tl_up, 9)
            st(O["ssd_conv_prompt"][0, 0], tail_s[0:HIST, :]).then_inc(tl_out, 16)
            st(O["ssd_conv_sample"][0].rearrange("b t d -> (b t) d"), tail_s[HIST:HIST + DEC_B * HIST, :]).then_inc(tl_out, 16)
            st(O["lru_h_prompt"][0], tail_l[0:1, :]).then_inc(tl_out, 16)
            st(O["lru_h_sample"][0], tail_l[1:9, :]).then_inc(tl_out, 16)
            st(O["lru_conv_prompt"][0, 0], tail_l[9:12, :]).then_inc(tl_out, 16)
            st(O["lru_conv_sample"][0].rearrange("b t d -> (b t) d"), tail_l[12:36, :]).then_inc(tl_out, 16)
            for c in range(NCH + 1):
                pool.wait_ge(out_up, 2 * (c + 1))
                if c < NCH:
                    st(O["y_prompt"][0, c * P:(c + 1) * P, :], y_out[:, c, :]).then_inc(out_st, 16)
                else:
                    st(O["y_sample"].rearrange("b t d -> (b t) d"), y_out[0:NS, c, :]).then_inc(out_st, 16)
            pool.wait_ge(kv_out, 64)
            pool.wait_ge(ss_out, 16 * XT)
            pool.wait_ge(fs_out, 16 * SG)
            pool.wait_ge(tl_out, 96)
            pool.wait_ge(out_st, 16 * 5)

        def of_samples(a):
            return a[:, SEQ + HIST:].rearrange("p (b t) -> p b t", t=HIST + DEC_T)[:, :, 0:DEC_T]

        CHUNKS = [(P, c * P) for c in range(NCH)] + [(NS, SEQ)]

        @block.tensor
        def _(pe):
            mmul, tr = pe.matmul, pe.transpose
            pe.sem_inc(used, SLOTS)

            def unit(stage, n, bank, parts, X, M=P):
                pe.wait_ge(free[stage], n + 1)
                if stage == "l1":
                    pe.wait_ge(free_act1, n + 1)
                total = sum(p[4] for p in parts)
                for s, v, _, _, _ in parts:
                    pe.wait_ge(s, v)
                tiles = 1 if M < P else 2
                for q, (_, _, slot, k0, nk) in enumerate(parts):
                    for j in range(tiles):
                        for k in range(nk):
                            for h in range(2):
                                last = mmul(ps[0:M, bank + 2 * j + h, 0:HALF], slot[:, k, j * P:j * P + M],
                                            X[:, k0 + k, HALF * h:HALF * (h + 1)],
                                            start=(k0 + k == 0), stop=(k0 + k == total - 1))
                    last.then_inc(used, 1)

            def part(c, i=0, k0=0, nk=KD):
                return (loaded[c % SLOTS], 32 * (c // SLOTS + 1 + i), ring[:, c % SLOTS], k0, nk)

            def linear(stage, c0, units, X):
                turns = units // SLOTS
                with pe.Fori(0, turns) as i:
                    for j in range(SLOTS):
                        unit(stage, SLOTS * i + j, 4 * (j % 2), [part(c0 + j, i)], X)
                for j in range(turns * SLOTS, units):
                    unit(stage, j, 4 * (j % 2), [part(c0 + j)], X)

            def layer_norm(n):
                pe.wait_ge(ln_ready, n + 1)
                for k in range(KD):
                    for h in range(2):
                        last = mmul(ps[:, h, 0:HALF], ones[:], xT[:, k, HALF * h:HALF * (h + 1)], start=(k == 0), stop=(k == KD - 1))
                last.then_inc(ln_mu, 1)
                for k in range(KD):
                    pe.wait_ge(ln_sq, KD * n + k + 1)
                    for h in range(2):
                        last = mmul(ps[:, 2 + h, 0:HALF], ones[:], sq[:, k, HALF * h:HALF * (h + 1)], start=(k == 0), stop=(k == KD - 1))
                last.then_inc(ln_var, 1)
                pe.wait_ge(ln_out, KD * (n + 1))

            pe.wait_ge(const_ok, 1)
            pe.wait_ge(in_x, 80)
            for k in range(KD):
                if k >= 4:
                    pe.wait_ge(x_up, k - 3)
                b = 2 * (k % 4)
                for c, (n, _) in enumerate(CHUNKS):
                    last = tr(ps[:, b + c // 4, (c % 4) * P:(c % 4) * P + n], xin[0:n, c, k * P:(k + 1) * P], ident[0:n, 0:n])
                last.then_inc(x_tr, 1)
            pe.wait_ge(x_up, KD)
            pe.wait_ge(in_par, 16 * 12)
            pe.wait_ge(in_hist, 48)
            for n, r in enumerate((P, 112, 32)):
                last = tr(ps[:, 0, n * P:n * P + r], par_in[0:r, n, :], ident[0:r, 0:r])
            for t in range(LT):
                tr(ps[:, 1, t * DEC_B:(t + 1) * DEC_B], h0_in[0:DEC_B, t * P:(t + 1) * P], ident[0:DEC_B, 0:DEC_B])
                tr(ps[:, 1, 64 + t * 24:64 + (t + 1) * 24], lhist_in[0:24, t * P:(t + 1) * P], ident[0:24, 0:24])
            for t in range(XBC):
                last = tr(ps[:, 2 + t // 16, (t % 16) * 24:(t % 16 + 1) * 24], shist_in[0:24, t * P:(t + 1) * P], ident[0:24, 0:24])
            last.then_inc(p_tr, 1)

            linear("l1", C_L1, 10, xT)
            pe.wait_ge(free["l1"], 12)
            pe.wait_ge(free_act1, 12)
            pe.wait_ge(uc_ok, 1)
            pe.wait_ge(in_gatew, 64)
            for gate, done in ((0, gr_mm), (1, gi_mm)):
                if gate:
                    pe.wait_ge(gr_ok, LT)
                for t in range(LT):
                    for h in range(2):
                        last = mmul(ps[:, 2 * t + h, 0:HALF], gate_w[:, gate, t, :], uc[:, t, HALF * h:HALF * (h + 1)], start=True, stop=True)
                    last.then_inc(done, 1)
            pe.wait_ge(gi_ok, LT)

            pe.wait_ge(lru_end, 1)
            for n in range(8):
                if n >= 4:
                    pe.wait_ge(kvt_up, n - 3)
                    pe.wait_ge(kvt_up_a, n - 3)
                b = 2 * (n % 4)
                for c, (m, c0) in enumerate(CHUNKS):
                    last = tr(ps[0:m, b + c // 4, (c % 4) * P:(c % 4 + 1) * P], proj[:, 4 + n, c0:c0 + m], ident[:])
                last.then_inc(kvt_tr, 1)
            pe.wait_ge(kvt_up, 8)
            pe.wait_ge(kvt_up_a, 8)

            NQ = HEADS * NCH

            def scores(n):
                h, qt = n // NCH, n % NCH
                r = 64 * (h % 2)
                if n >= 2:
                    pe.wait_ge(ex_ok, n - 1)
                w = (qt + 1) * P
                mmul(ps[:, n % 2, 0:w], proj[r:r + 64, h // 2, qt * P:(qt + 1) * P], proj[r:r + 64, 4 + h // 2, 0:w], start=True, stop=False)
                mmul(ps[:, n % 2, w - P:w], ident[:], qk_mask[:], start=False, stop=True).then_inc(sc_mm, 1)

            scores(0)
            for n in range(NQ):
                h, qt = n // NCH, n % NCH
                if n + 1 < NQ:
                    scores(n + 1)
                pe.wait_ge(pn_ok, n + 1)
                if n >= 2:
                    pe.wait_ge(pt_ok, n - 1)
                for c in range(qt + 1):
                    last = tr(ps[:, 2 + n % 2, c * P:(c + 1) * P], pp[:, n % 2, c * P:(c + 1) * P], ident[:])
                last.then_inc(pt_mm, 1)
                pe.wait_ge(pt_ok, n + 1)
                if n % 8 == 0 and n >= 16:
                    pe.wait_ge(o_up, n // 8 - 1)
                r, b = 64 * (h % 2), 4 + (h // 2) % 2
                for c in range(qt + 1):
                    last = mmul(ps[r:r + 64, b, qt * P:(qt + 1) * P], v_tok[:, c, h * HD:(h + 1) * HD], ppt[:, n % 2, c * P:(c + 1) * P],
                                start=(c == 0), stop=(c == qt))
                last.then_inc(o_mm, 1)
            pe.wait_ge(o_up, 4)
            pe.wait_ge(qx_ok, 1)

            for pr in range(DEC_B // 2):
                for q in range(4):
                    b2, n = q // 2, 4 * pr + q
                    pe.wait_ge(kv_in[q], 16 * QUAD * (2 * pr + 1))
                    for t in range(AT):
                        m = 4 * n + t
                        if m >= 4:
                            pe.wait_ge(kt_dve if t % 2 == 0 else kt_act, 2 * (n - 1) + t // 2 + 1)
                        for pg in range(QUAD):
                            last = tr(ps[:, t, pg * P:(pg + 1) * P], kv[q][:, pg, t * P:(t + 1) * P], ident[:])
                        last.then_inc(kt_mm, 1)
                    pe.wait_ge(kt_dve, 2 * n + 2)
                    pe.wait_ge(kt_act, 2 * n + 2)
                    if q == 0 and pr > 0:
                        pe.wait_ge(s_ex, pr)
                        pe.wait_ge(s_ptu, 3 * pr)
                    for t in range(AT):
                        last = mmul(ps[64 * b2:64 * b2 + 64, 4 + q % 2, :], qx[:, t, 2 * pr + b2, :], kt[n % 3][:, t, :],
                                    start=(t == 0), stop=(t == AT - 1))
                    if q % 2 == 1:
                        for t in range(AT):
                            mmul(ps[64 * b2:64 * b2 + 64, 6, 0:NS], qx[:, t, 2 * pr + b2, :], ks_T[:, t, :], start=(t == 0), stop=False)
                        last = mmul(ps[64 * b2:64 * b2 + 64, 6, 0:NS], expand[:, pr, 64 * b2:64 * b2 + 64], seq_maskT[:], start=False, stop=True)
                    last.then_inc(qs_mm, 1)
                pe.wait_ge(s_pn, pr + 1)
                for rnd, b in ((0, 7), (1, 6), (2, 7)):
                    if rnd == 0 and pr > 0:
                        pe.wait_ge(s_ou, 2 * pr)
                    if rnd == 2:
                        pe.wait_ge(s_ptu, 3 * pr + 1)
                    for c in range(4 * rnd, min(4 * rnd + 4, 9)):
                        n = P if c < 8 else NS
                        last = tr(ps[0:n, b, (c % 4) * P:(c % 4 + 1) * P], p_s[:, c * P:c * P + n], ident[:])
                    last.then_inc(s_ptm, 1)
                pe.wait_ge(s_ptu, 3 * pr + 3)
                for b2 in range(2):
                    for h in range(2):
                        pe.wait_ge(kv_in[2 * b2 + h], 16 * QUAD * (2 * pr + 2))
                    for t in range(AT):
                        o = ps[:, 7, (4 * b2 + t) * 16:(4 * b2 + t + 1) * 16]
                        r = 64 * b2 + 16 * t
                        for c in range(NPAGES):
                            mmul(o, kv[2 * b2 + c // QUAD][:, c % QUAD, t * P:(t + 1) * P], p_sT[:, c, r:r + 16], start=(c == 0), stop=False)
                        last = mmul(o, v_tok[0:NS, NCH, t * P:(t + 1) * P], p_sT[0:NS, 8, r:r + 16], start=False, stop=True)
                    last.then_inc(s_o, 1)
            pe.wait_ge(s_ou, 8)

            for j in range(KD // 2):
                unit("l2", j, 4 * (j % 2), [part(C_L2 + j)], cat)
            layer_norm(0)
            linear("l3", C_L3, FT, xT)
            pe.wait_ge(free["l3"], FT + 2)
            for j in range(KD // 2):
                unit("l4", j, 4 * (j % 2), [part(C_L4 + 2 * j, 0, 0, KMAX), part(C_L4 + 2 * j + 1, 0, KMAX, KMAX)], hid)
            layer_norm(1)

            linear("xb", C_XBC, XBC // 2, xT)
            unit("dt", 0, 0, [part(C_DT)], xT, M=SH)
            pe.wait_ge(row_ok, 1)
            for n, src in enumerate((DTR, CSR, WDR)):
                for c, (m, c0) in enumerate(CHUNKS):
                    last = tr(ps[0:m, 2 + n, c * SH:(c + 1) * SH], rows[0:SH, src, c0:c0 + m], ident[0:SH, 0:SH])
            mmul(ps[:, 5, 0:SH * NCH], ones[0:SH, :], tmpr[0:SH, 1, 0:SH * NCH], start=True, stop=True)
            for t in range(XT):
                for hh in range(2):
                    sel = ident[0:SH, 2 * t + hh:2 * t + hh + 1].broadcast_to([SH, 64])
                    mmul(ps[64 * hh:64 * hh + 64, 6, t * 8:t * 8 + 8], sel, rows[0:SH, ECR, SEQ + DEC_T - 1:T:DEC_T], start=True, stop=True)
                    last = mmul(ps[64 * hh:64 * hh + 64, 6, 128 + t:129 + t], sel, dt_par[:, 2:3], start=True, stop=True)
            last.then_inc(tk_mm, 1)

            def cs_bare(t):
                for hh in range(2):
                    h = 2 * t + hh
                    sel = ident_r[0:SH, h:h + 1].broadcast_to([SH, P])
                    mmul(ps[:, 4 + hh, :], sel, cs_h[0:SH, :], start=True, stop=False)
                    mmul(ps[:, 4 + hh, :], sel, cs_l[0:SH, :], start=False, stop=True).then_inc(bc_mm, 1)

            def cs_mask(t):
                for hh in range(2):
                    pe.wait_ge(eb_ok, 2 * t + hh + 1)
                    mmul(ps[:, 4 + hh, :], ident_r[:], sl_mask_r[:].unsqueeze(1).broadcast_to([P, NCH, P]), start=False, stop=True,
                         skip_group_check=True).then_inc(cs_mm, 1)

            def cs_samples(t):
                for hh in range(2):
                    h = 2 * t + hh
                    mmul(ps[:, 3, 64 + 64 * hh:128 + 64 * hh], ident[0:SH, h:h + 1].broadcast_to([SH, P]), rows[0:SH, CSR, SEQ:T], start=True, stop=True)
                    o = ps[0:NS, 3, 192 + 64 * hh:256 + 64 * hh]
                    mmul(o, ident[0:SH, h:h + 1].broadcast_to([SH, NS]), rows[0:SH, CSR, SEQ:T], start=True, stop=False)
                    last = mmul(o, ident[0:NS, 0:NS], seq_mask[:], start=False, stop=True)
                last.then_inc(cs_mm, 1)

            def h0_turn(t):
                pe.wait_ge(h0_in_s[t % 2], 16 * (t // 2 + 1))
                for b in range(DEC_B):
                    last = tr(ps[:, 6 + b // 4, (b % 4) * P:(b % 4 + 1) * P], h0n[t % 2][:, b, :], ident[:])
                last.then_inc(h0_tr, 1)

            pe.wait_ge(tk_up, 1)
            cs_bare(0)
            cs_mask(0)
            for g in range(SG):
                Bt, Ct = xbc[:, XT + g, :], xbc[:, XT + BC + g, :]
                for c in range(NCH):
                    mmul(ps[:, 0, c * P:(c + 1) * P], Bt[:, c * P:(c + 1) * P], Ct[:, c * P:(c + 1) * P], start=True, stop=True)
                mmul(ps[0:NS, 1, 0:NS], Bt[:, SEQ:T], Ct[:, SEQ:T], start=True, stop=True)
                if g:
                    pe.wait_ge(y_ok, 2 * g)
                    pe.wait_ge(ss_ok, 2 * g)
                for c in range(NCH):
                    tr(ps[:, 2, c * P:(c + 1) * P], Bt[:, c * P:(c + 1) * P], ident[:])
                    for j in range(2):
                        tr(ps[:, 3 + 3 * j, c * P:(c + 1) * P], xbc[:, 2 * g + j, c * P:(c + 1) * P], ident[:])
                tr(ps[0:NS, 1, P:2 * P], Bt[:, SEQ:T], ident[:])
                for j in range(2):
                    last = tr(ps[0:NS, 1, (2 + j) * P:(3 + j) * P], xbc[:, 2 * g + j, SEQ:T], ident[:])
                last.then_inc(g_mm, 1)
                pe.wait_ge(g_up, g + 1)
                pe.wait_ge(g_up_a, g + 1)
                for c in range(NCH):
                    last = mmul(ps[:, 6 + c // 2, (c % 2) * 256:(c % 2 + 1) * 256], b_tok[:, c, :], x_w[:, c, :], start=True, stop=True)
                last.then_inc(st_mm, 1)
                cs_samples(2 * g)
                pe.wait_ge(st_up, g + 1)
                h0_turn(2 * g)
                for j in range(2):
                    last = tr(ps[:, 2, j * P:(j + 1) * P], state[:, NCH - 1, j * P:(j + 1) * P], ident[:])
                last.then_inc(fs_mm, 1)
                pe.wait_ge(fs_up, g + 1)
                for j in range(2):
                    t = 2 * g + j
                    for hh in range(2):
                        pe.wait_ge(m_ok, 3 * t + hh + 1)
                        hc = (2 * j + hh) * 64
                        for c in range(NCH):
                            o = ps[64 * hh:64 * hh + 64, 2, c * P:(c + 1) * P]
                            mmul(o, x_dt[:, c, hc:hc + 64], m_buf[:, hh, c * P:(c + 1) * P], start=True, stop=(c == 0))
                            if c:
                                mmul(o, state[:, c - 1, hc:hc + 64], ce[:, hh, c * P:(c + 1) * P], start=False, stop=True)
                    pe.wait_ge(m_ok, 3 * t + 3)
                    pe.wait_ge(h0_up, t + 1)
                    for hh in range(2):
                        hc = (2 * j + hh) * 64
                        r = slice(64 * hh, 64 * hh + 64)
                        mmul(ps[r, 3, 0:NS], x_dt[0:NS, NCH, hc:hc + 64], m_buf[0:NS, hh, SEQ:T], start=True, stop=True)
                        for b in range(DEC_B):
                            last = mmul(ps[r, 3, 8 * b:8 * b + 8], h0t[:, b, r], ce[:, hh, SEQ + 8 * b:SEQ + 8 * b + 8], start=False,
                                        stop=True, skip_group_check=True)
                    last.then_inc(yt_mm, 1)
                    if t + 1 < XT:
                        cs_bare(t + 1)
                    for hf in range(2):
                        last = mmul(ps[:, 6 + hf, :], x_w[0:NS, NCH, j * P:(j + 1) * P], b_seq[0:NS, 4 * hf:4 * hf + 4, :].rearrange("p b n -> p (b n)"), start=True, stop=True)
                    last.then_inc(ss_mm, 1)
                    if t + 1 < XT:
                        cs_mask(t + 1)
                    if j == 0:
                        pe.wait_ge(y_ok, t + 1)
                        cs_samples(t + 1)
                        pe.wait_ge(ss_ok, t + 1)
                        h0_turn(t + 1)
            pe.wait_ge(y_ok, XT)
            pe.wait_ge(ss_ok, XT)

            def z_unit(i, j):
                n = SLOTS * i + j
                unit("z", n, 0, [part(C_Z + j, i)], xT)
                pe.wait_ge(z_sqd, n + 1)
                pe.wait_ge(z_rt, n + 1)
                for k in range(2):
                    for h in range(2):
                        last = mmul(ps[:, 4 + h, 0:HALF], ones[:], z_q[:, k, HALF * h:HALF * (h + 1)], start=(k == 0), stop=(k == 1))
                last.then_inc(z_sum, 1)
            with pe.Fori(0, XT // 2 // SLOTS) as i:
                for j in range(SLOTS):
                    z_unit(i, j)
            pe.wait_ge(z_ok, XT // 2 + 1)
            for j in range(KD // 2):
                unit("l6", j, 4 * (j % 2), [part(C_L6 + 2 * j, 0, 0, 8), part(C_L6 + 2 * j + 1, 0, 8, 8)], xbc)
            layer_norm(2)
            for n in range(9):
                if n >= 2:
                    pe.wait_ge(tl_up, n - 1)
                for q in range(4):
                    t = 4 * n + q
                    if n < 8:
                        last = tr(ps[0:27, n % 2, q * P:(q + 1) * P], ssd_tail[:, t, :], ident[:])
                    else:
                        last = tr(ps[0:36, n % 2, q * P:(q + 1) * P], lru_tail[:, q, :], ident[:])
                last.then_inc(tl_mm, 1)
            pe.wait_ge(tl_up, 9)
            pe.wait_ge(in_router, 16)
            for c, (m, c0) in enumerate(CHUNKS):
                for k in range(KD):
                    last = mmul(ps[0:m, 4, c * NE:(c + 1) * NE], xT[:, k, c0:c0 + m], router[:, k, :], start=(k == 0), stop=(k == KD - 1))
            last.then_inc(rt_mm, 1)
            for n in range(10):
                m, c0 = CHUNKS[n // 2]
                if n >= 4:
                    pe.wait_ge(xt_lo, n - 3)
                for k in range(4):
                    last = tr(ps[0:m, n % 4, k * P:(k + 1) * P], xT[:, 4 * (n % 2) + k, c0:c0 + m], ident[:])
                last.then_inc(xt_mm, 1)
            pe.wait_ge(rt_m, 1)
            M = g_w[:, 10:50]
            mmul(ps[:, 5, 0:40], before[:], M, start=True, stop=False, skip_group_check=True)
            for c in range(NCH):
                mmul(ps[:, 5, (c + 1) * NE:40], ones[:], M[:, c * NE:(c + 1) * NE].unsqueeze(1).broadcast_to([P, NCH - c, NE]),
                     start=False, stop=(c == NCH - 1), skip_group_check=True)
            for c in range(5):
                last = mmul(ps[:, 6, 0:NE], ones[:], M[:, c * NE:(c + 1) * NE], start=(c == 0), stop=(c == 4))
            last.then_inc(ct_mm, 1)

            def gather(r):
                pe.wait_ge(hot_ok, r + 1)
                for s in range(4):
                    if s >= 2:
                        pe.wait_ge(ga_hi, 4 * r + s - 1)
                        pe.wait_ge(ga_lo, 4 * r + s - 1)
                    for src, b in ((xt_h, 3), (xt_l, 4)):
                        for q in range(2):
                            k = 2 * s + q
                            for c, (m, _) in enumerate(CHUNKS):
                                last = mmul(ps[:, b + 2 * (s % 2), q * CAP:(q + 1) * CAP], src[0:m, c, k * P:(k + 1) * P], hot[0:m, c, :],
                                            start=(c == 0), stop=(c == NCH))
                    last.then_inc(ga_mm, 1)

            def turn(r):
                pe.wait_ge(sc_ok, KD * r + 1)
                pe.wait_ge(ga_hi, 4 * r + 4)
                pe.wait_ge(ga_lo, 4 * r + 4)
                for u, (m, s0) in enumerate(((P, 0), (NS, P))):
                    for c, (n, c0) in enumerate(CHUNKS):
                        last = tr(ps[0:m, 3 + 2 * u + c // 4, (c % 4) * P:(c % 4) * P + n], hot[0:n, c, s0:s0 + m].bitcast(F32), ident[0:n, 0:n])
                last.then_inc(th_mm, 1)
                for u, (m, s0) in enumerate(((P, 0), (NS, P))):
                    for c, (n, c0) in enumerate(CHUNKS):
                        last = mmul(ps[0:m, 7, u:u + 1], hot[0:n, c, s0:s0 + m].bitcast(F32), gate_now[0:n, c:c + 1], start=(c == 0), stop=(c == NCH))
                last.then_inc(sg_mm, 1)
                pe.wait_ge(th_ok, r + 1)
                pe.wait_ge(sg_ok, r + 1)

            rounds = None
            pe.wait_ge(rt_ok, 1)
            rounds = pe.value_load(n_rounds[0:1, 0:1], min_val=1, max_val=RMAX)
            gather(0)
            turn(0)
            with pe.Fori(0, rounds) as r:
                for v in range(PER_E):
                    up = v < FET
                    if v < 3 or v == 14:
                        pe.wait_ge(d_ok, 4 * r + (v + 2 if v < 3 else 5))
                    else:
                        pe.wait_ge(e_bank, FET * r + v - 2)
                    if v == FET:
                        gather(r + 1)
                        pe.wait_ge(e_h, FET * r + FET)
                    K, x_h, x_l = (KD, xg_h, xg_l) if up else (FET, h_h, h_l)
                    if v == 0:
                        pe.wait_ge(ga_hi, 4 * r + 4)
                        pe.wait_ge(ga_lo, 4 * r + 4)
                    for j in range(2):
                        u = 2 * v + j
                        pe.wait_ge(w_lo, 2 * RAW + 1 + u + TILES * r)
                        o = ps[:, v % 3, j * CAP:(j + 1) * CAP]
                        for n, (w, x) in enumerate(((w_h, x_h), (w_l, x_h), (w_h, x_l))):
                            for k in range(K):
                                last = mmul(o, w[:, u % RAW, k, :], x[:, k, :], start=(n == 0 and k == 0), stop=(n == 2 and k == K - 1))
                        last.then_inc(w_used, 1)
                pe.wait_ge(d_ok, 4 * r + 8)
                pe.wait_ge(ga_hi, 4 * r + 8)
                pe.wait_ge(ga_lo, 4 * r + 8)
                for u, (m, s0) in enumerate(((P, 0), (NS, P))):
                    for k in range(KD):
                        last = tr(ps[0:m, 3 + 2 * u + k // 4, (k % 4) * P:(k % 4 + 1) * P], yg[:, k, s0:s0 + m], ident[:])
                    last.then_inc(ty_mm, 1)
                pe.wait_ge(ty_lo, 2 * r + 2)
                for k in range(KD):
                    if k >= 2:
                        pe.wait_ge(sc_ok, KD * r + k)
                    b = 3 + 2 * (k % 2)
                    for h in range(2):
                        cs_ = slice(HALF * h, HALF * (h + 1))
                        n = 0
                        for y in (yt_h, yt_l):
                            for u, m in ((0, P), (1, NS)):
                                last = mmul(ps[:, b + h, 0:HALF], y[0:m, u, k * P:(k + 1) * P], hotT[0:m, u, cs_], start=(n == 0), stop=(n == 3))
                                n += 1
                    last.then_inc(sc_y, 1)
                turn(r + 1)
            layer_norm(3)
            for c, (m, c0) in enumerate(CHUNKS):
                for hf in range(2):
                    n = 2 * c + hf
                    if n >= 4:
                        pe.wait_ge(out_up, n - 3)
                    for k in range(4):
                        last = tr(ps[0:m, n % 4, k * P:(k + 1) * P], xT[:, 4 * hf + k, c0:c0 + m], ident[:])
                    last.then_inc(out_mm, 1)

        @block.scalar
        def _(act):
            f = act.activation
            link = Chain(act, act_c)

            def banks(b):
                return ps[:, b:b + 2, 0:HALF]

            def halves(v):
                return v.rearrange("p (h n) -> p h n", h=2)

            def layer_norm(n):
                for k in range(KD):
                    act.wait_ge(ln_c, KD * n + k + 1)
                    f(sq[:, k, :], xT[:, k, :], ACT.Square).then_inc(ln_sq, 1)
                act.wait_ge(ln_var, n + 1)
                f(halves(std), banks(2), ACT.Sqrt, bias=eps[:, 0:1], scale=1.0 / D).then_inc(ln_std, 1)
                for k in range(KD):
                    act.wait_ge(ln_n, KD * n + k + 1)
                    f(xT[:, k, :], xT[:, k, :], ACT.Identity, bias=ln_b[n][:, k:k + 1], scale=ln_g[n][:, k:k + 1]).then_inc(ln_out, 1)

            act.wait_ge(const_ok, 1)
            act.wait_ge(p_up, 1)
            act.sem_inc(free_act1, 2)

            def l1(n, j):
                act.wait_ge(used, done("l1", n))
                f(halves(proj[:, ds(2 * n + 1, 1), :].rearrange("p o n -> p (o n)")), banks(4 * (j % 2) + 2), ACT.Copy).then_inc(free_act1, 1)
            with act.Fori(0, 2) as i:
                for j in range(SLOTS):
                    l1(SLOTS * i + j, j)
            for j in range(2):
                l1(8 + j, j)

            act.wait_ge(lam_e, 1)
            f(stat[:, 8:12], stat[:, 4:8], ACT.Exp, scale=-1.0).then_inc(lam_e, 1)
            act.wait_ge(lam_u, 1)
            f(stat[:, 16:20], stat[:, 12:16], ACT.Ln).then_inc(lam_l, 1)
            for t in range(LT):
                act.wait_ge(gr_mm, t + 1)
                f(halves(lru_a[:, t * T:(t + 1) * T]), banks(2 * t), ACT.Sigmoid, bias=b_gate[0][:, t:t + 1]).then_inc(gr_ok, 1)
            for t in range(LT):
                act.wait_ge(gi_mm, t + 1)
                f(halves(lru_i[:, t * T:(t + 1) * T]), banks(2 * t), ACT.Sigmoid, bias=b_gate[1][:, t:t + 1]).then_inc(gi_ok, 1)
            act.wait_ge(la_ok, 1)
            link(f(lru_t[:], lru_a[:], ACT.Tanh, scale=-1.0))
            f(lru_a[:], lru_a[:], ACT.Exp).then_inc(a_ok, 1)
            f(proj[:, 16:20, :], proj[:, 16:20, :], ACT.Gelu_apprx_tanh).then_inc(g_ok, 1)
            act.wait_ge(a2_ok, 1)
            f(lru_t[:], lru_t[:], ACT.Sqrt).then_inc(s_ok, 1)

            act.wait_ge(lru_end, 1)
            for n in range(8):
                act.wait_ge(kvt_tr, n + 1)
                dst = (k_tok if n < 4 else v_tok)
                f(dst[0:NS, NCH, (n % 4) * P:(n % 4 + 1) * P], ps[0:NS, 2 * (n % 4) + 1, 0:P], ACT.Copy).then_inc(kvt_up_a, 1)

            NQ = HEADS * NCH
            for n in range(NQ + 1):
                if n < NQ:
                    w = (n % NCH + 1) * P
                    act.wait_ge(mx_ok, n + 1)
                    if n >= 2:
                        act.wait_ge(pt_mm, n - 1)
                    f(pp[:, n % 2, 0:w], ps[:, n % 2, 0:w], ACT.Exp, bias=stat[:, 34 + n % 2:35 + n % 2], scale=HD ** -0.5,
                      accum_out=stat[:, 36 + n % 2:37 + n % 2]).then_inc(ex_ok, 1)
                if n >= 1:
                    m = n - 1
                    w = (m % NCH + 1) * P
                    act.wait_ge(pt_mm, m + 1)
                    if m >= 2:
                        act.wait_ge(o_mm, m - 1)
                    f(ppt[:, m % 2, 0:w], ps[:, 2 + m % 2, 0:w], ACT.Copy).then_inc(pt_ok, 1)

            for pr in range(DEC_B // 2):
                for q in range(4):
                    n = 4 * pr + q
                    if n >= 3:
                        act.wait_ge(qs_mm, n - 2)
                    for t in (1, 3):
                        act.wait_ge(kt_mm, 4 * n + t + 1)
                        f(kt[n % 3][:, t, :], ps[:, t, :], ACT.Copy).then_inc(kt_act, 1)
                act.wait_ge(s_bias, pr + 1)
                if pr:
                    act.wait_ge(s_ptm, 3 * pr)
                for n in range(NBLK):
                    f(p_s[:, BLK * n:BLK * (n + 1)], ps[:, 4 + n // 2, (n % 2) * BLK:(n % 2 + 1) * BLK], ACT.Exp,
                      bias=stat[:, 40 + n:41 + n], scale=HD ** -0.5, accum_out=stat[:, 48 + n:49 + n])
                f(p_s[:, NBLK * BLK:], ps[:, 6, 0:NS], ACT.Exp, bias=stat[:, 44:45], scale=HD ** -0.5,
                  accum_out=stat[:, 52:53]).then_inc(s_ex, 1)
                if pr:
                    act.wait_ge(s_o, 2 * pr)
                for rnd, b in ((0, 7), (1, 6)):
                    act.wait_ge(s_ptm, 3 * pr + rnd + 1)
                    f(p_sT[:, 4 * rnd:4 * rnd + 4, :].rearrange("p c n -> p (c n)"), ps[:, b, :], ACT.Copy).then_inc(s_ptu, 1)
                act.wait_ge(s_ptm, 3 * pr + 3)
                f(p_sT[0:NS, 8, :], ps[0:NS, 7, 0:P], ACT.Copy).then_inc(s_ptu, 1)

            act.wait_ge(kv_out, 64)
            layer_norm(0)

            def silu3(n, j):
                act.wait_ge(used, done("l3", n))
                f(halves(hid[:, ds(n, 1), :].rearrange("p o n -> p (o n)")), banks(4 * (j % 2)), ACT.Silu).then_inc(silu_ok["l3"], 1)
            with act.Fori(0, FT // SLOTS) as i:
                for j in range(SLOTS):
                    silu3(SLOTS * i + j, j)
            for j in range(2):
                silu3(FT // SLOTS * SLOTS + j, j)
            layer_norm(1)

            act.sem_inc(free["xb"], 2)
            act.sem_inc(cv_s, 1)

            def raw_out(n, j):
                act.wait_ge(used, done("xb", n))
                act.wait_ge(cv_y, n + 1)
                b, s = 4 * (j % 2), 2 * (j % 2)
                f(raw[:, s:s + 2, HIST:HIST + HALF], ps[:, b:b + 4:2, 0:HALF], ACT.Copy)
                f(raw[:, s:s + 2, HIST + HALF:HIST + SEQ], ps[:, b + 1:b + 4:2, 0:SEQ - HALF], ACT.Copy)
                for q in range(2):
                    smp = raw[:, s + q, HIST + SEQ:].rearrange("p (b t) -> p b t", t=HIST + DEC_T)
                    last = f(smp[:, :, HIST:], ps[:, b + 1 + 2 * q, SEQ - HALF:HALF].rearrange("p (b t) -> p b t", t=DEC_T), ACT.Copy)
                last.then_inc(free["xb"], 1)

            def conv_silu(n):
                act.wait_ge(cv_y, n + 3)
                f(xbc[:, ds(2 * n, 2), 0:SEQ], acc[:, :, 0:SEQ], ACT.Silu)
                for q in range(2):
                    last = f(xbc[:, ds(2 * n + q, 1), SEQ:T].rearrange("p o (b t) -> p (o b) t", t=DEC_T), of_samples(acc[:, q, :]), ACT.Silu)
                last.then_inc(cv_s, 1)
            with act.Fori(0, XBC // 2 // SLOTS) as i:
                for j in range(SLOTS):
                    raw_out(SLOTS * i + j, j)
                    conv_silu(SLOTS * i + j)

            act.wait_ge(dt_a, 1)
            f(tmpr[0:SH, 2, :], tmpr[0:SH, 1, :], ACT.Exp, scale=-1.0)
            f(dt_par[:, 3:4], dt_par[:, 1:2], ACT.Exp).then_inc(dt_e, 1)
            act.wait_ge(dt_u, 1)
            f(tmpr[0:SH, 1, :], tmpr[0:SH, 3, :], ACT.Ln).then_inc(dt_l, 1)
            act.wait_ge(cs_ok, 1)
            f(rows[0:SH, ECR, :], rows[0:SH, CSR, :], ACT.Exp)
            f(tmpr[0:SH, 0, :], tmpr[0:SH, 0, :], ACT.Exp).then_inc(ec_ok, 1)

            def exps(t):
                for hh in range(2):
                    act.wait_ge(bc_mm, 2 * t + hh + 1)
                    f(ebc[:, hh, 0:SEQ], ps[:, 4 + hh, :], ACT.Exp).then_inc(eb_ok, 1)
                for hh in range(2):
                    h = 2 * t + hh
                    act.wait_ge(cs_mm, 3 * t + hh + 1)
                    for c in range(NCH):
                        i = f(e_buf[:, hh, c * P:(c + 1) * P], ps[:, 4 + hh, c * P:(c + 1) * P], ACT.Exp, bias=tok[:, 1, c * SH + h:c * SH + h + 1])
                    i.then_inc(e_ok, 1)

            def exps_samples(t):
                act.wait_ge(cs_mm, 3 * t + 3)
                f(ebc[:, :, SEQ:T], ps[:, 3, 64:192].rearrange("p (u n) -> p u n", u=2), ACT.Exp)
                for hh in range(2):
                    h = 2 * t + hh
                    i = f(e_buf[0:NS, hh, SEQ:T], ps[0:NS, 3, 192 + 64 * hh:256 + 64 * hh], ACT.Exp,
                          bias=tok[0:NS, 1, NCH * SH + h:NCH * SH + h + 1])
                i.then_inc(e_ok, 1)

            act.wait_ge(tk_up, 1)
            exps(0)
            for g in range(SG):
                act.wait_ge(g_mm, g + 1)
                f(b_tok[:, 0:NCH, :].rearrange("p c n -> p (c n)"), ps[:, 2, :], ACT.Copy).then_inc(g_up_a, 1)
                for j in range(2):
                    t = 2 * g + j
                    exps_samples(t)
                    act.wait_ge(h0_tr, t + 1)
                    f(h0t[:].rearrange("p (u b) n -> p u (b n)", u=2), ps[:, 6:8, :], ACT.Copy).then_inc(h0_up, 1)
                    if j == 0:
                        act.wait_ge(fs_mm, g + 1)
                        if g >= 2:
                            act.wait_ge(fs_out, 16 * (g - 1))
                        f(st_out[:, g % 2].rearrange("p a n -> p (a n)"), ps[:, 2, 0:2 * P], ACT.Copy).then_inc(fs_up, 1)
                    if t + 1 < XT:
                        act.wait_ge(m_ok, 3 * t + 3)
                        exps(t + 1)

            act.sem_inc(free["z"], 1)
            act.sem_inc(z_rt, 1)

            def z_unit(i, j):
                n = SLOTS * i + j
                act.wait_ge(used, done("z", n))
                act.wait_ge(z_gate, n + 1)
                f(z_s[:].rearrange("p k (h n) -> p (k h) n", h=2), ps[:, 0:4, 0:HALF], ACT.Silu).then_inc(free["z"], 1)
                act.wait_ge(z_gate, n + 2)
                f(z_q[:], xbc[:, ds(2 * n, 2), :], ACT.Square).then_inc(z_sqd, 1)
                act.wait_ge(z_sum, n + 1)
                act.wait_ge(z_ok, n + 1)
                f(halves(z_r), banks(4), ACT.Sqrt, bias=eps[:, 1:2], scale=1.0 / (2 * P)).then_inc(z_rt, 1)
            with act.Fori(0, XT // 2 // SLOTS) as i:
                for j in range(SLOTS):
                    z_unit(i, j)
            layer_norm(2)
            act.wait_ge(rt_d, 1)
            f(g_w[:, 0:5], g_w[:, 5:10], ACT.Exp).then_inc(rt_e, 1)
            act.wait_ge(tl_out, 96)
            for n in range(10):
                m = CHUNKS[n // 2][0]
                act.wait_ge(xt_mm, n + 1)
                f(xt_h[0:m, n // 2, 512 * (n % 2):512 * (n % 2) + 512], ps[0:m, n % 4, :], ACT.Copy).then_inc(xt_hi, 1)

            act.wait_ge(rt_ok, 1)
            rounds = act.value_load(n_rounds[0:1, 0:1], min_val=1, max_val=RMAX)

            def w_round(r, u):
                m, j = u // 2, u % 2
                K = KD if m < FET else FET
                if j == 0 or u == 3:
                    act.wait_ge(moe_loaded[m % RAW], 32 * (5 * r + m // RAW + 1))
                act.wait_ge(w_used, TILES * r + u + 1)
                f(w_h[:, u % RAW, 0:K, :], ring[:, m % RAW, 0:K, j * P:(j + 1) * P], ACT.Copy).then_inc(w_hi, 1)

            def gather_lo(r):
                for s in range(4):
                    act.wait_ge(ga_mm, 4 * r + s + 1)
                    f(xg_l[:, 2 * s:2 * s + 2, :].rearrange("p k n -> p (k n)"), ps[:, 4 + 2 * (s % 2), 0:2 * CAP], ACT.Copy).then_inc(ga_lo, 1)

            act.sem_inc(w_used, RAW)
            act.sem_inc(d_ok, 4)
            for u in range(RAW):
                w_round(0, u)
            gather_lo(0)
            with act.Fori(0, rounds) as r:
                for v in range(PER_E):
                    for u in (2 * v + 3, 2 * v + 4):
                        w_round(r + u // TILES, u % TILES)
                    act.wait_ge(w_used, RAW + 2 * v + 2 + TILES * r)
                    if v < FET:
                        act.wait_ge(e_bank, FET * r + v + 1)
                        f(h_s[:, v % 2, :], ps[:, v % 3, 0:CAP], ACT.Silu).then_inc(e_silu, 1)
                    else:
                        w = 2 * (v - FET)
                        f(yg[:, w:w + 2, :].rearrange("p k n -> p (k n)"), ps[:, v % 3, 0:2 * CAP], ACT.Copy).then_inc(d_ok, 1)
                    if v == FET - 1:
                        gather_lo(r + 1)
                for u, m in ((0, P), (1, NS)):
                    act.wait_ge(ty_mm, 2 * r + u + 1)
                    f(yt_h[0:m, u, :].rearrange("p (g n) -> p g n", g=2), ps[0:m, 3 + 2 * u:5 + 2 * u, :], ACT.Copy, scale=slot_gate[0:m, u:u + 1]).then_inc(ty_hi, 1)
            layer_norm(3)

        @block.vector
        def _(dve):
            link = Chain(dve, dve_c)
            tt, tsc, stt, cp = dve.tensor_tensor, dve.tensor_scalar, dve.scalar_tensor_tensor, dve.tensor_copy

            def banks(b):
                return ps[:, b:b + 2, 0:HALF]

            def halves(v):
                return v.rearrange("p (h n) -> p h n", h=2)

            def layer_norm(n):
                dve.wait_ge(ln_mu, n + 1)
                mu = banks(0)
                link(tsc(halves(std), mu, 1.0 / D, None, ALU.mult))
                for k in range(KD):
                    tt(xT[:, k, :], xT[:, k, :], std[:], ALU.subtract).then_inc(ln_c, 1)
                dve.wait_ge(ln_std, n + 1)
                link(dve.reciprocal(rstd[:], std[:]))
                for k in range(KD):
                    tt(xT[:, k, :], xT[:, k, :], rstd[:], ALU.mult).then_inc(ln_n, 1)

            def residual(stage, n, bank, last=None):
                dve.wait_ge(used, done(stage, n))
                for q in range(2):
                    i = stt(halves(xT[:, 2 * n + q, :]), halves(xT[:, 2 * n + q, :]), ALPHA, banks(bank + 2 * q), ALU.mult, ALU.add)
                i.then_inc(last or free[stage], 1)

            for k in range(KD):
                dve.wait_ge(x_tr, k + 1)
                b = 2 * (k % 4)
                cp(xT[:, k, 0:SEQ], ps[:, b, :])
                cp(xT[:, k, SEQ:T], ps[:, b + 1, 0:NS]).then_inc(x_up, 1)
            dve.wait_ge(p_tr, 1)
            cp(par[:, 0, :], ps[:, 0, 0:P])
            cp(par[:, 1, 0:112], ps[:, 0, P:P + 112])
            cp(par[:, 2, 0:32], ps[:, 0, 2 * P:2 * P + 32])
            cp(lru_h0[:].rearrange("p t b -> p (t b)"), ps[:, 1, 0:LT * DEC_B])
            cp(lru_hist[:].rearrange("p t n -> p (t n)"), ps[:, 1, 64:64 + LT * 24])
            for u in range(2):
                last = cp(ssd_hist[:, 16 * u:16 * u + 16, :].rearrange("p t n -> p (t n)"), ps[:, 2 + u, 0:384])
            last.then_inc(p_up, 1)
            dve.wait_ge(p_up, 1)
            dve.sem_inc(free["l1"], 2)

            def l1(n, j):
                dve.wait_ge(used, done("l1", n))
                cp(halves(proj[:, ds(2 * n, 1), :].rearrange("p o n -> p (o n)")), banks(4 * (j % 2))).then_inc(free["l1"], 1)
            with dve.Fori(0, 2) as i:
                for j in range(SLOTS):
                    l1(SLOTS * i + j, j)
            for j in range(2):
                l1(8 + j, j)

            dve.wait_ge(free_act1, 12)
            dve.wait_ge(free["l1"], 12)
            padded = u_pad[:, :, HIST + SEQ:].rearrange("p t (b n) -> p t b n", b=DEC_B)
            dve.memset(u_pad[:, :, 0:HIST], 0.0)
            cp(u_pad[:, :, HIST:HIST + SEQ], proj[:, 12:16, 0:SEQ])
            for t in range(LT):
                cp(padded[:, t, :, 0:HIST], lru_hist[:, t, :].rearrange("p (b n) -> p b n", b=DEC_B))
                cp(padded[:, t, :, HIST:], proj[:, 12 + t, SEQ:T].rearrange("p (b n) -> p b n", b=DEC_B))
                cp(lru_tail[:, t, 12:36].rearrange("p (b n) -> p b n", b=DEC_B),
                   proj[:, 12 + t, SEQ:T].rearrange("p (b n) -> p b n", b=DEC_B)[:, :, DEC_T - HIST:])
            link(cp(lru_tail[:, :, 9:12], proj[:, 12:16, SEQ - HIST:SEQ]))
            N = PADT - HIST
            for t in range(LT):
                link(tsc(u_acc[:, 0:N], u_pad[:, t, 3:3 + N], conv_w_l[:, 3, t:t + 1], conv_b_l[:, t:t + 1], ALU.mult, ALU.add))
                for w in (2, 1):
                    link(stt(u_acc[:, 0:N], u_pad[:, t, w:w + N], conv_w_l[:, w, t:t + 1], u_acc[:, 0:N], ALU.mult, ALU.add))
                link(stt(u_acc[:, 0:N], u_pad[:, t, 0:N], conv_w_l[:, 0, t:t + 1], u_acc[:, 0:N], ALU.mult, ALU.add))
                cp(uc[:, t, 0:SEQ], u_acc[:, 0:SEQ])
                link(cp(uc[:, t, SEQ:T].rearrange("p (b n) -> p b n", b=DEC_B), of_samples(u_acc[:])))
            dve.sem_inc(uc_ok, 1)
            c4 = lambda n: stat[:, 4 * n:4 * n + 4]
            stt(c4(1), lam, -1.0, lam, ALU.mult, ALU.max).then_inc(lam_e, 1)
            dve.wait_ge(lam_e, 2)
            link(tsc(c4(3), c4(2), 1.0, None, ALU.add))
            link(tsc(c4(5), c4(3), -1.0, None, ALU.add))
            dve.sem_inc(lam_u, 1)
            link(tsc(c4(6), c4(5), 0.0, None, ALU.is_equal))
            link(tt(c4(5), c4(5), c4(6), ALU.add))
            link(dve.reciprocal(c4(5), c4(5)))
            dve.wait_ge(lam_l, 1)
            link(tt(c4(4), c4(4), c4(6), ALU.add))
            link(tt(c4(4), c4(4), c4(2), ALU.mult))
            link(tt(c4(4), c4(4), c4(5), ALU.mult))
            link(tsc(c4(7), lam, -1.0, 0.0, ALU.mult, ALU.max))
            link(tt(c4(7), c4(7), c4(4), ALU.add))
            link(tsc(c4(7), c4(7), -8.0, None, ALU.mult))
            for t in range(LT):
                dve.wait_ge(gr_ok, t + 1)
                last = tsc(lru_a[:, t * T:(t + 1) * T], lru_a[:, t * T:(t + 1) * T], stat[:, 28 + t:29 + t], None, ALU.mult)
            last.then_inc(la_ok, 1)
            dve.wait_ge(gi_ok, LT)
            link(tt(lru_i[:], lru_i[:], uc[:].rearrange("p t n -> p (t n)"), ALU.mult))
            dve.wait_ge(a_ok, 1)
            a2 = u_pad[:].rearrange("p t n -> p (t n)")[:, 0:LT * T]
            link(tt(a2, lru_a[:], lru_a[:], ALU.mult))
            stt(lru_t[:], a2, 1.0, lru_t[:], ALU.add, ALU.mult).then_inc(a2_ok, 1)
            dve.wait_ge(s_ok, 1)
            link(tt(lru_i[:], lru_i[:], lru_t[:], ALU.mult))
            a3 = lru_a[:].rearrange("p (t n) -> p t n", t=LT)
            b3 = lru_i[:].rearrange("p (t n) -> p t n", t=LT)
            a0, b0 = a3[:, :, SEQ:T:DEC_T], b3[:, :, SEQ:T:DEC_T]
            h1 = stat[:, 64:96].rearrange("p (t b) -> p t b", t=LT)
            link(tt(h1, a0, lru_h0[:], ALU.mult))
            tt(b0, b0, h1, ALU.add)
            link(dve.memset(a0, 0.0))
            link(dve.memset(a3[:, :, 0:1], 0.0))
            ucf = uc[:].rearrange("p t n -> p (t n)")
            link(dve.tensor_tensor_scan(ucf, lru_a[:], lru_i[:], 0.0, ALU.mult, ALU.add))
            cp(lru_tail[:, :, 0:1], uc[:, :, SEQ - 1:SEQ])
            cp(lru_tail[:, :, 1:9], uc[:, :, SEQ + DEC_T - 1:T:DEC_T])
            dve.wait_ge(g_ok, 1)
            tt(cat[:, AT:, :], uc[:], proj[:, 16:20, :], ALU.mult).then_inc(lru_end, 1)
            dve.wait_ge(lru_end, 1)

            for n in range(8):
                dve.wait_ge(kvt_tr, n + 1)
                dst = (k_tok if n < 4 else v_tok)
                cp(dst[:, 0:NCH, (n % 4) * P:(n % 4 + 1) * P], ps[:, 2 * (n % 4), :].rearrange("p (c d) -> p c d", c=NCH)).then_inc(kvt_up, 1)
            link(dve.memset(qx[:], 0.0))
            for t in range(AT):
                for hh in range(2):
                    r = 64 * hh
                    cp(qx[r:r + 64, t, :, 16 * t + 8 * hh:16 * t + 8 * hh + 8],
                       proj[r:r + 64, t, SEQ:T].rearrange("p (b n) -> p b n", b=DEC_B))
            cp(ks_T[:], proj[:, 4:8, SEQ:T]).then_inc(qx_ok, 1)

            NQ = HEADS * NCH

            def o_out(u):
                dve.wait_ge(o_mm, 8 * u + 8)
                cp(cat[:, u, 0:SEQ], ps[:, 4 + u % 2, :]).then_inc(o_up, 1)
            for n in range(NQ + 1):
                if n < NQ:
                    w = (n % NCH + 1) * P
                    dve.wait_ge(sc_mm, n + 1)
                    mx, neg = stat[:, 32 + n % 2:33 + n % 2], stat[:, 34 + n % 2:35 + n % 2]
                    link(dve.tensor_reduce(mx, ps[:, n % 2, 0:w], AX, ALU.max))
                    tsc(neg, mx, -(HD ** -0.5), None, ALU.mult).then_inc(mx_ok, 1)
                if n >= 1:
                    m = n - 1
                    w = (m % NCH + 1) * P
                    dve.wait_ge(ex_ok, m + 1)
                    rc = stat[:, 38 + m % 2:39 + m % 2]
                    link(dve.reciprocal(rc, stat[:, 36 + m % 2:37 + m % 2]))
                    tsc(pp[:, m % 2, 0:w], pp[:, m % 2, 0:w], rc, None, ALU.mult).then_inc(pn_ok, 1)
                if n >= 2 and (n - 2) % 8 == 7:
                    o_out((n - 2) // 8)
            o_out(3)

            for pr in range(DEC_B // 2):
                for q in range(4):
                    n = 4 * pr + q
                    if n >= 3:
                        dve.wait_ge(qs_mm, n - 2)
                    for t in (0, 2):
                        dve.wait_ge(kt_mm, 4 * n + t + 1)
                        cp(kt[n % 3][:, t, :], ps[:, t, :]).then_inc(kt_dve, 1)
                dve.wait_ge(qs_mm, 4 * pr + 4)
                if pr:
                    dve.wait_ge(s_pn, pr)
                S = ps[:, 4:6, :].rearrange("p u (n k) -> p (u n) k", k=BLK)
                bs, bm = stat[:, 56:60], stat[:, 60:65]
                dve.tensor_reduce(bs, S, AX, ALU.add)
                dve.tensor_reduce(bm[:, 0:NBLK], S, AX, ALU.max)
                link(dve.tensor_reduce(bm[:, NBLK:], ps[:, 6, 0:NS], AX, ALU.max))
                gt = stat[:, 96:112].rearrange("p (a b) -> p a b", a=NBLK)
                eq = stat[:, 112:128].rearrange("p (a b) -> p a b", a=NBLK)
                mine, other = bs.unsqueeze(2).broadcast_to([P, NBLK, NBLK]), bs.unsqueeze(1).broadcast_to([P, NBLK, NBLK])
                tt(gt, other, mine, ALU.is_gt)
                link(tt(eq, other, mine, ALU.is_equal))
                link(tt(eq, eq, tri[:, 0:NBLK, 0:NBLK], ALU.mult))
                link(tt(gt, gt, eq, ALU.add))
                rank = stat[:, 128:132]
                link(dve.tensor_reduce(rank, gt, AX, ALU.add))
                pen = stat[:, 132:136]
                link(tsc(pen, rank, float(NBLK - 1), NEG, ALU.is_ge, ALU.mult))
                link(tt(bm[:, 0:NBLK], bm[:, 0:NBLK], pen, ALU.add))
                link(dve.tensor_reduce(stat[:, 136:137], bm, AX, ALU.max))
                link(tsc(stat[:, 44:45], stat[:, 136:137], -(HD ** -0.5), None, ALU.mult))
                tsc(stat[:, 40:44], pen, stat[:, 44:45], None, ALU.add).then_inc(s_bias, 1)
                dve.wait_ge(s_ex, pr + 1)
                link(dve.tensor_reduce(stat[:, 137:138], stat[:, 48:53], AX, ALU.add))
                link(dve.reciprocal(stat[:, 138:139], stat[:, 137:138]))
                tsc(p_s[:], p_s[:], stat[:, 138:139], None, ALU.mult).then_inc(s_pn, 1)
                dve.wait_ge(s_o, 2 * pr + 2)
                for hh in range(2):
                    r = 64 * hh
                    for b2 in range(2):
                        c0 = SEQ + DEC_T * (2 * pr + b2)
                        i = cp(cat[r:r + 64, 0:AT, c0:c0 + DEC_T],
                               ps[r:r + 64, 7, 64 * b2:64 * b2 + 64].rearrange("p (t n) -> p t n", t=AT)[:, :, 8 * hh:8 * hh + 8])
                    i.then_inc(s_ou, 1)

            dve.wait_ge(s_ou, 8)
            dve.sem_inc(free["l2"], 2)
            for j in range(KD // 2):
                residual("l2", j, 4 * (j % 2), ln_ready if j == 3 else None)
            layer_norm(0)
            dve.wait_ge(ln_out, KD)
            dve.sem_inc(free["l3"], 2)

            def mul3(n, j):
                dve.wait_ge(silu_ok["l3"], n + 1)
                v = halves(hid[:, ds(n, 1), :].rearrange("p o n -> p (o n)"))
                tt(v, v, banks(4 * (j % 2) + 2), ALU.mult).then_inc(free["l3"], 1)
            with dve.Fori(0, FT // SLOTS) as i:
                for j in range(SLOTS):
                    mul3(SLOTS * i + j, j)
            for j in range(2):
                mul3(FT // SLOTS * SLOTS + j, j)
            dve.sem_inc(free["l4"], 2)
            for j in range(KD // 2):
                residual("l4", j, 4 * (j % 2), ln_ready if j == 3 else None)
            layer_norm(1)

            link(dve.memset(raw[:, :, 0:HIST], 0.0))
            dve.sem_inc(cv_y, 2)

            def conv(n, j):
                dve.wait_ge(free["xb"], n + 3)
                s = 2 * (j % 2)
                for q in range(2):
                    smp = raw[:, s + q, HIST + SEQ:].rearrange("p (b t) -> p b t", b=DEC_B)
                    cp(smp[:, :, 0:HIST], ssd_hist[:, ds(2 * n + q, 1), :].rearrange("p o (b t) -> p (o b) t", b=DEC_B))
                    cp(ssd_tail[:, ds(2 * n + q, 1), HIST:].rearrange("p o (b t) -> p (o b) t", b=DEC_B), smp[:, :, DEC_T:])
                link(cp(ssd_tail[:, ds(2 * n, 2), 0:HIST], raw[:, s:s + 2, SEQ:SEQ + HIST]))
                dve.wait_ge(cv_s, n + 1)
                for w in (3, 2, 1, 0):
                    for q in range(2):
                        x = raw[:, s + q, w:w + N]
                        cw = conv_w_s[:, w, ds(2 * n + q, 1)]
                        if w == 3:
                            i = tsc(acc[:, q, 0:N], x, cw, conv_b_s[:, ds(2 * n + q, 1)], ALU.mult, ALU.add)
                        else:
                            i = stt(acc[:, q, 0:N], x, cw, acc[:, q, 0:N], ALU.mult, ALU.add)
                    if w:
                        link(i)
                i.then_inc(cv_y, 1)
            with dve.Fori(0, XBC // 2 // SLOTS) as i:
                link.enter(i, 4 * SLOTS)
                for j in range(SLOTS):
                    conv(SLOTS * i + j, j)
            link.leave(XBC // 2 // SLOTS)

            dve.sem_inc(free["dt"], 1)
            dve.wait_ge(used, done("dt", 0))
            dve.wait_ge(cv_s, XBC // 2 + 1)
            dve.wait_ge(in_small, 48)
            R = lambda n: tmpr[0:SH, n, :]
            W = lambda n: rows[0:SH, n, :]
            link(tsc(halves(R(0)), ps[0:SH, 0:2, 0:HALF], dt_par[:, 0:1], None, ALU.add))
            stt(R(1), R(0), -1.0, R(0), ALU.mult, ALU.max).then_inc(dt_a, 1)
            dve.wait_ge(dt_e, 1)
            link(tsc(dt_par[:, 3:4], dt_par[:, 3:4], -1.0, None, ALU.mult))
            link(tsc(R(3), R(2), 1.0, None, ALU.add))
            tsc(R(4), R(3), -1.0, None, ALU.add).then_inc(dt_u, 1)
            dve.wait_ge(dt_l, 1)
            link(tsc(R(3), R(4), 0.0, None, ALU.is_equal))
            link(tt(R(4), R(4), R(3), ALU.add))
            link(dve.reciprocal(R(4), R(4)))
            link(tt(R(1), R(1), R(3), ALU.add))
            link(tt(R(1), R(1), R(2), ALU.mult))
            link(tt(R(1), R(1), R(4), ALU.mult))
            link(stt(W(DTR), R(0), 0.0, R(1), ALU.max, ALU.add))
            link(tsc(R(0), W(DTR), dt_par[:, 3:4], None, ALU.mult))
            link(dve.tensor_tensor_scan(W(CSR), run_row[:], R(0), 0.0, ALU.mult, ALU.add))
            csp = W(CSR)[:, 0:SEQ].rearrange("p (c n) -> p c n", c=NCH)
            css = W(CSR)[:, SEQ:T].rearrange("p (c n) -> p c n", c=DEC_B)
            tt(R(0)[:, 0:SEQ].rearrange("p (c n) -> p c n", c=NCH), csp[:, :, P - 1:P].broadcast_to([SH, NCH, P]), csp, ALU.subtract)
            tt(R(0)[:, SEQ:T].rearrange("p (c n) -> p c n", c=DEC_B), css[:, :, DEC_T - 1:DEC_T].broadcast_to([SH, DEC_B, DEC_T]), css,
               ALU.subtract).then_inc(cs_ok, 1)
            dve.wait_ge(ec_ok, 1)
            tt(R(1)[:, 0:SH * NCH].rearrange("p (h c) -> p h c", h=SH), ident[0:SH, 0:SH].unsqueeze(2).broadcast_to([SH, SH, NCH]),
               W(ECR)[:, P - 1:SEQ:P].unsqueeze(1).broadcast_to([SH, SH, NCH]), ALU.mult)
            cp(ident_r[:], ident[:])
            cp(sl_mask_r[:], sl_mask[:])
            link(cp(cs_h[0:SH, :], W(CSR)[:, 0:SEQ]))
            tt(cs_l[0:SH, :], W(CSR)[:, 0:SEQ], cs_h[0:SH, :].bitcast(F32), ALU.subtract)
            tt(W(WDR), R(0), W(DTR), ALU.mult).then_inc(row_ok, 1)
            dve.wait_ge(tk_mm, 1)
            for n, sc in enumerate((1.0, -1.0, 1.0)):
                tsc(tok[:, n, 0:NCH * SH], ps[:, 2 + n, 0:NCH * SH], sc, None, ALU.mult)
                tsc(tok[0:NS, n, NCH * SH:], ps[0:NS, 2 + n, NCH * SH:5 * SH], sc, None, ALU.mult)
            cp(dec_p[:], ps[:, 5, 0:SH * NCH])
            cp(dec_s[:].rearrange("p t b -> p (t b)"), ps[:, 6, 0:P])
            cp(d_exp, ps[:, 6, P:P + XT]).then_inc(tk_up, 1)
            dve.wait_ge(tk_up, 1)

            for g in range(SG):
                dve.wait_ge(g_mm, g + 1)
                for dst, which in ((x_dt, 0), (x_w, 2)):
                    fac = tok[:, which, 0:NCH * SH].rearrange("p (c h) -> p c h", c=NCH)
                    for j in range(2):
                        h = 4 * g + 2 * j
                        tt(dst[:, 0:NCH, j * P:(j + 1) * P].rearrange("p c (h n) -> p c h n", h=2),
                           ps[:, 3 + 3 * j, :].rearrange("p (c h n) -> p c h n", c=NCH, h=2),
                           fac[:, :, h:h + 2].unsqueeze(3).broadcast_to([P, NCH, 2, 64]), ALU.mult)
                    i = tt(dst[0:NS, NCH, :].rearrange("p (h n) -> p h n", h=4), ps[0:NS, 1, 256:512].rearrange("p (h n) -> p h n", h=4),
                           tok[0:NS, which, NCH * SH + 4 * g:NCH * SH + 4 * g + 4].unsqueeze(2).broadcast_to([NS, 4, 64]), ALU.mult)
                tt(b_seq[0:NS], ps[0:NS, 1, P:2 * P].unsqueeze(1).broadcast_to([NS, DEC_B, P]),
                   of_seq[:].unsqueeze(2).broadcast_to([NS, DEC_B, P]), ALU.mult).then_inc(g_up, 1)
                dve.wait_ge(st_mm, g + 1)
                dec = dec_p[:].rearrange("p (h c) -> p h c", h=SH)
                link(cp(state[:, 0, :], ps[:, 6, 0:256]))
                for c in range(1, NCH):
                    v = state[:, c, :].rearrange("p (h n) -> p h n", h=4)
                    link(tt(v, state[:, c - 1, :].rearrange("p (h n) -> p h n", h=4), dec[:, 4 * g:4 * g + 4, c:c + 1].broadcast_to([P, 4, 64]), ALU.mult))
                    link(tt(state[:, c, :], state[:, c, :], ps[:, 6 + c // 2, (c % 2) * 256:(c % 2 + 1) * 256], ALU.add))
                dve.sem_inc(st_up, 1)
                for j in range(2):
                    t = 2 * g + j
                    Ct = xbc[:, XT + BC + g, :]
                    if t:
                        dve.wait_ge(yt_mm, t)
                    for hh in range(2):
                        dve.wait_ge(e_ok, 3 * t + hh + 1)
                        tt(ce[:, hh, P:SEQ], Ct[:, P:SEQ], ebc[:, hh, P:SEQ], ALU.mult)
                        tt(m_buf[:, hh, 0:SEQ], ps[:, 0, :], e_buf[:, hh, 0:SEQ], ALU.mult).then_inc(m_ok, 1)
                    dve.wait_ge(e_ok, 3 * t + 3)
                    tt(ce[:, :, SEQ:T], Ct[:, SEQ:T].unsqueeze(1).broadcast_to([P, 2, NS]), ebc[:, :, SEQ:T], ALU.mult)
                    tt(m_buf[0:NS, :, SEQ:T], ps[0:NS, 1, 0:NS].unsqueeze(1).broadcast_to([NS, 2, NS]), e_buf[0:NS, :, SEQ:T], ALU.mult).then_inc(m_ok, 1)
                    dve.wait_ge(yt_mm, t + 1)
                    stt(xbc[:, t, SEQ:T], xbc[:, t, SEQ:T], d_exp[:, t:t + 1], ps[:, 3, 0:NS], ALU.mult, ALU.add)
                    stt(xbc[:, t, 0:SEQ], xbc[:, t, 0:SEQ], d_exp[:, t:t + 1], ps[:, 2, :], ALU.mult, ALU.add).then_inc(y_ok, 1)
                    dve.wait_ge(ss_mm, t + 1)
                    dve.wait_ge(hd_ok, t + 1)
                    v = h0n[t % 2].rearrange("p (u b) n -> p u (b n)", u=2)
                    tt(v, v, ps[:, 6:8, :], ALU.add).then_inc(ss_ok, 1)

            dve.sem_inc(z_gate, 1)
            dve.sem_inc(z_ok, 1)

            def z_unit(i, j):
                n = SLOTS * i + j
                v = xbc[:, ds(2 * n, 2), :]
                dve.wait_ge(free["z"], n + 2)
                tt(v, v, z_s[:], ALU.mult).then_inc(z_gate, 1)
                dve.wait_ge(z_rt, n + 2)
                link(dve.reciprocal(z_i[:], z_r[:]))
                for q in range(2):
                    y = xbc[:, ds(2 * n + q, 1), :].rearrange("p o n -> p (o n)")
                    last = stt(y, y, norm_g[:, ds(2 * n + q, 1)], z_i[:], ALU.mult, ALU.mult)
                last.then_inc(z_ok, 1)
            with dve.Fori(0, XT // 2 // SLOTS) as i:
                link.enter(i, SLOTS)
                for j in range(SLOTS):
                    z_unit(i, j)
            link.leave(XT // 2 // SLOTS)
            dve.wait_ge(z_ok, XT // 2 + 1)
            dve.sem_inc(free["l6"], 2)
            for j in range(KD // 2):
                residual("l6", j, 4 * (j % 2), ln_ready if j == 3 else None)
            layer_norm(2)
            dve.wait_ge(ss_out, 16 * XT)
            dve.wait_ge(fs_out, 16 * SG)
            for n in range(9):
                dve.wait_ge(tl_mm, n + 1)
                if n < 8:
                    cp(tail_s[0:27, n * 512:(n + 1) * 512], ps[0:27, n % 2, :]).then_inc(tl_up, 1)
                else:
                    cp(tail_l[0:36, :], ps[0:36, n % 2, :]).then_inc(tl_up, 1)

            dve.wait_ge(tl_out, 96)
            lg, gts = stat[:, 40:80], stat[:, 0:40]
            link(dve.memset(lg, 0.0))
            dve.wait_ge(rt_mm, 1)
            cp(lg[:, 0:32], ps[:, 4, 0:32])
            link(cp(lg[0:NS, 32:40], ps[0:NS, 4, 32:40]))
            l3 = lg.rearrange("p (c e) -> p c e", c=5)
            gg = g_w[:, 10:90].rearrange("p (u n) -> p u n", u=2)
            gt = g_w[:, 100:140].rearrange("p (c e) -> p c e", c=5)
            rank = g_w[:, 140:180].rearrange("p (c e) -> p c e", c=5)
            sel = g_w[:, 180:220].rearrange("p (c e) -> p c e", c=5)
            link(dve.memset(rank, 0.0))
            for o in range(NE):
                other = l3[:, :, o:o + 1].broadcast_to([P, 5, NE])
                link(tt(gt, other, l3, ALU.is_gt))
                link(tt(rank, rank, gt, ALU.add))
                if o < NE - 1:
                    n = NE - 1 - o
                    link(tt(gt[:, :, 0:n], l3[:, :, o:o + 1].broadcast_to([P, 5, n]), l3[:, :, o + 1:], ALU.is_equal))
                    link(tt(rank[:, :, o + 1:], rank[:, :, o + 1:], gt[:, :, 0:n], ALU.add))
            best = [g_w[:, 220:225], g_w[:, 225:230]]
            for r in range(2):
                link(tsc(sel, rank, float(r), None, ALU.is_equal))
                link(tt(sel, sel, l3, ALU.mult))
                link(dve.tensor_reduce(best[r], sel, AX, ALU.add))
            tt(g_w[:, 5:10], best[1], best[0], ALU.subtract).then_inc(rt_d, 1)
            dve.wait_ge(rt_e, 1)
            link(tsc(best[0], g_w[:, 0:5], 1.0, None, ALU.add))
            link(dve.reciprocal(best[0], best[0]))
            link(tt(best[1], best[0], g_w[:, 0:5], ALU.mult))
            G = gts.rearrange("p (c e) -> p c e", c=5)
            Mf = g_w[:, 10:50]
            M = Mf.rearrange("p (c e) -> p c e", c=5)
            link(tsc(Mf, g_w[:, 140:180], 1.5, None, ALU.is_lt))
            dve.memset(Mf[NS:P, 32:40], 0.0).then_inc(rt_m, 1)
            for r in range(2):
                link(tsc(sel, rank, float(r), None, ALU.is_equal))
                link(tt(sel, sel, best[r].unsqueeze(2).broadcast_to([P, 5, NE]), ALU.mult))
                if r == 0:
                    link(cp(G, sel))
            link(tt(G, G, sel, ALU.add))
            link(cp(iota, iota_i[:]))
            for n in range(10):
                m = CHUNKS[n // 2][0]
                dve.wait_ge(xt_hi, n + 1)
                c = slice(512 * (n % 2), 512 * (n % 2) + 512)
                tt(xt_l[0:m, n // 2, c], ps[0:m, n % 4, :], xt_h[0:m, n // 2, c].bitcast(F32), ALU.subtract).then_inc(xt_lo, 1)
            dve.wait_ge(xt_mm, 10)
            for k in range(KD):
                last = tsc(xT[:, k, :], xT[:, k, :], ALPHA, None, ALU.mult)
            link(last)
            dve.wait_ge(ct_mm, 1)
            Q, cnt, nr, incl, excl = g_w[:, 60:100], g_w[:, 230:238], g_w[:, 238:246], g_w[:, 246:254], g_w[:, 254:262]
            tmp8 = g_w[:, 262:270]
            link(stt(Q, ps[:, 5, 0:40], BIG, Mf, ALU.add, ALU.mult))
            link(cp(cnt, ps[:, 6, 0:NE]))
            link(tsc(nr, cnt, 0.5, None, ALU.is_gt))
            for m in (1, 2):
                link(tsc(tmp8, cnt, CAP * m + 0.5, None, ALU.is_gt))
                link(tt(nr, nr, tmp8, ALU.add))
            link(dve.tensor_tensor_scan(incl, ones[:, 0:NE], nr, 0.0, ALU.mult, ALU.add))
            link(tt(excl, incl, nr, ALU.subtract))
            NR = RMAX + 2
            rounds3 = [P, NR, NE]
            inr = g_w[:, 270:270 + NR * NE].rearrange("p (r e) -> p r e", e=NE)
            off = g_w[:, 400:400 + NR * NE].rearrange("p (r e) -> p r e", e=NE)
            sub = g_w[:, 530:530 + NR]
            big = g_w[:, 600:600 + NR * 5 * NE].rearrange("p (r c e) -> p r c e", c=5, e=NE)
            r_of = iota[:, 0:NR].unsqueeze(2).broadcast_to(rounds3)
            link(tt(off, r_of, excl.unsqueeze(1).broadcast_to(rounds3), ALU.subtract))
            link(tt(inr, r_of, incl.unsqueeze(1).broadcast_to(rounds3), ALU.is_lt))
            link(stt(inr, off, 0.0, inr, ALU.is_ge, ALU.mult))
            off2 = g_w[:, 1210:1210 + NR * NE].rearrange("p (r e) -> p r e", e=NE)
            link(tt(off2, inr, iota[:, 0:NE].unsqueeze(1).broadcast_to(rounds3), ALU.mult))
            link(dve.tensor_reduce(g_w[:, 550:550 + NR], off2, AX, ALU.add))
            link(cp(expert_of[0:1, 0:NR], g_w[0:1, 550:550 + NR]))
            link(cp(n_rounds[:], incl[0:1, NE - 1:NE]))
            link(tt(off, off, inr, ALU.mult))
            link(dve.tensor_reduce(sub, off, AX, ALU.add))
            link(tsc(sub, sub, float(CAP), BIG, ALU.mult, ALU.add))
            rounds4 = [P, NR, 5, NE]
            for src, dst in ((Q, slot_of), (gts, gate_of)):
                link(tt(big, src.rearrange("p (c e) -> p c e", c=5).unsqueeze(1).broadcast_to(rounds4), inr.unsqueeze(2).broadcast_to(rounds4), ALU.mult))
                link(dve.tensor_reduce(dst[:], big, AX, ALU.add))
            link(tt(slot_of[:], slot_of[:], sub.unsqueeze(2).broadcast_to([P, NR, 5]), ALU.subtract))
            dve.sem_inc(rt_ok, 1)

            rounds = dve.value_load(n_rounds[0:1, 0:1], min_val=1, max_val=RMAX)

            def w_rest(r, u):
                m, j = u // 2, u % 2
                K = KD if m < FET else FET
                dve.wait_ge(w_hi, TILES * r + u + 1)
                tt(w_l[:, u % RAW, 0:K, :], ring[:, m % RAW, 0:K, j * P:(j + 1) * P], w_h[:, u % RAW, 0:K, :].bitcast(F32), ALU.subtract).then_inc(w_lo, 1)

            def one_hot(r):
                i = cp(gate_now, gate_of[:, ds(r, 1), :].rearrange("p o c -> p (o c)"))
                for c in range(5):
                    i = tsc(hot[:, c, :], iota, slot_of[:, ds(r, 1), c:c + 1].rearrange("p o c -> p (o c)"), None, ALU.is_equal)
                i.then_inc(hot_ok, 1)

            def gather_hi(r):
                for s in range(4):
                    dve.wait_ge(ga_mm, 4 * r + s + 1)
                    cp(xg_h[:, 2 * s:2 * s + 2, :].rearrange("p k n -> p (k n)"), ps[:, 3 + 2 * (s % 2), 0:2 * CAP]).then_inc(ga_hi, 1)

            def turned(r):
                dve.wait_ge(th_mm, r + 1)
                for u, m in ((0, P), (1, NS)):
                    cp(hotT[0:m, u, 0:SEQ], ps[0:m, 3 + 2 * u, :])
                    i = cp(hotT[0:m, u, SEQ:T], ps[0:m, 4 + 2 * u, 0:NS])
                i.then_inc(th_ok, 1)
                dve.wait_ge(sg_mm, r + 1)
                cp(slot_gate[:, 0:1], ps[:, 7, 0:1])
                cp(slot_gate[0:NS, 1:2], ps[0:NS, 7, 1:2]).then_inc(sg_ok, 1)

            dve.sem_inc(e_bank, 2)
            dve.sem_inc(sc_ok, 1)
            one_hot(0)
            for u in range(RAW):
                w_rest(0, u)
            gather_hi(0)
            turned(0)
            with dve.Fori(0, rounds) as r:
                link.enter(r, FET)
                for v in range(PER_E):
                    for u in (2 * v + 3, 2 * v + 4):
                        w_rest(r + u // TILES, u % TILES)
                    if v < FET:
                        dve.wait_ge(e_silu, FET * r + v + 1)
                        hm = h_m[:, v % 2, :]
                        i = tt(hm, h_s[:, v % 2, :], ps[:, v % 3, CAP:2 * CAP], ALU.mult)
                        i.then_inc(e_bank, 1)
                        dve.wait_ge(e_bank, 2 + FET * r + v + 1)
                        link(cp(h_h[:, v, :], hm))
                        tt(h_l[:, v, :], hm, h_h[:, v, :].bitcast(F32), ALU.subtract).then_inc(e_h, 1)
                    if v == FET - 3:
                        one_hot(r + 1)
                    if v == FET - 1:
                        gather_hi(r + 1)
                for u, m in ((0, P), (1, NS)):
                    dve.wait_ge(ty_hi, 2 * r + u + 1)
                    stt(yt_l[0:m, u, :].rearrange("p (g n) -> p g n", g=2), ps[0:m, 3 + 2 * u:5 + 2 * u, :], slot_gate[0:m, u:u + 1],
                        yt_h[0:m, u, :].bitcast(F32).rearrange("p (g n) -> p g n", g=2), ALU.mult, ALU.subtract).then_inc(ty_lo, 1)
                for k in range(KD):
                    dve.wait_ge(sc_y, KD * r + k + 1)
                    tt(halves(xT[:, k, :]), halves(xT[:, k, :]), banks(3 + 2 * (k % 2)), ALU.add).then_inc(sc_ok, 1)
                turned(r + 1)
            dve.sem_inc(ln_ready, 1)
            layer_norm(3)
            for n in range(10):
                dve.wait_ge(out_mm, n + 1)
                m = CHUNKS[n // 2][0]
                cp(y_out[0:m, n // 2, 512 * (n % 2):512 * (n % 2) + 512], ps[0:m, n % 4, :]).then_inc(out_up, 1)


_INS = ["x_prompt", "x_sample", "cache_k", "cache_v", "page_table", "state_lru_h", "state_lru_conv", "state_ssm",
        "state_ssd_conv", "w_in_even", "lru_conv_w", "lru_conv_b", "lru_w_a", "lru_b_a", "lru_w_x", "lru_b_x", "lru_lambda",
        "w_out_even", "ssd_w_in", "ssd_conv_w", "ssd_conv_b", "ssd_dt_bias", "ssd_a_log", "ssd_d", "ssd_norm_g", "ssd_w_out",
        "ffn_w1", "ffn_w3", "ffn_w2", "moe_router", "moe_w1", "moe_w3", "moe_w2", "ln_mix_g", "ln_mix_b", "ln_ffn_g", "ln_ffn_b"]
_OUTS = [("y_prompt", (1, SEQ, D)), ("y_sample", (DEC_B, DEC_T, D)),
         ("k_prompt", (1, 1, SEQ, HEADS, HD)), ("v_prompt", (1, 1, SEQ, HEADS, HD)),
         ("k_sample", (1, DEC_B, DEC_T, HEADS, HD)), ("v_sample", (1, DEC_B, DEC_T, HEADS, HD)),
         ("lru_h_prompt", (1, 1, 512)), ("lru_h_sample", (1, DEC_B, 512)),
         ("lru_conv_prompt", (1, 1, HIST, 512)), ("lru_conv_sample", (1, DEC_B, HIST, 512)),
         ("ssm_prompt", (1, 1, SH, 64, SN)), ("ssm_sample", (1, DEC_B, SH, 64, SN)),
         ("ssd_conv_prompt", (1, 1, HIST, SCONV)), ("ssd_conv_sample", (1, DEC_B, HIST, SCONV))]


def kernel(**inputs):
    import concourse.bacc as bacc
    from concourse.bass_utils import run_bass_kernel_spmd

    nc = bacc.Bacc("TRN2", target_bir_lowering=False, num_devices=1)
    arrays, I, O = {}, {}, {}
    for name in _INS:
        a = np.ascontiguousarray(inputs[name])
        arrays["in_" + name] = a
        I[name] = nc.dram_tensor("in_" + name, a.shape, mybir.dt.from_np(a.dtype), kind="ExternalInput").ap()
    for name, shape in _OUTS:
        O[name] = nc.dram_tensor("out_" + name, shape, F32, kind="ExternalOutput").ap()
    build(nc, I, O)
    r = run_bass_kernel_spmd(nc, [arrays], core_ids=[0])
    return tuple(r.results[0]["out_" + name] for name, _ in _OUTS)
```

```python
from contextlib import ExitStack

import numpy as np

import concourse.bass as bass
from concourse import mybir

F32 = mybir.dt.float32
F32R = mybir.dt.float32r
I32 = mybir.dt.int32
ALU = mybir.AluOpType
ACT = mybir.ActivationFunctionType
AX = mybir.AxisListType.X
ds = bass.ds

P = 128
D = 1024
KD = D // P
SEQ, DEC_B, DEC_T = 512, 8, 8
NS = DEC_B * DEC_T
T = SEQ + NS
HALF = T // 2
NCH = SEQ // P
CONV_W = 4
HIST = CONV_W - 1
PADT = HIST + SEQ + DEC_B * (HIST + DEC_T)
HEADS, HD = 8, 64
AW = HEADS * HD
AT = AW // P
LT = 512 // P
PAGE, NPAGES, NPOOL = 128, 8, 80
QUAD = 4
BLK = 256
NBLK = NPAGES * PAGE // BLK
FF = 2816
SG, SH, SN = 8, 32, 128
XT, BC = 2048 // P, 8
XBC = XT + 2 * BC
SCONV = XBC * P
SIN = 2048 + SCONV + SH
NE, FE, FET = 8, 1408, 1408 // P
ALPHA = float(4 ** 0.25)
LN_EPS, RMS_EPS = 1e-5, 1e-6
NEG = -1e30
SLOTS = 4
KMAX = 11
CW = 2 * P
RAW = 3
CAP = 192
RMAX = 13
BIG = 4096.0

C_L1 = 0
L1_ORDER = (6, 7, 8, 9, 0, 1, 2, 3, 4, 5)
L1_GATES = 6
C_L2 = C_L1 + 10
C_XBC = C_L2 + KD // 2
C_DT = C_XBC + XBC // 2
C_Z = C_DT + 1
C_L6 = C_Z + XT // 2
C_MOE = C_L6 + KD
PER_E = FET + KD // 2
TILES = 2 * PER_E
FROUNDS = FF // FE
assert FROUNDS * FE == FF
XU = XBC // 2


class Chain:

    def __init__(self, eng, sem):
        self.eng, self.sem, self.n, self.turn = eng, sem, 0, 0

    def __call__(self, ins):
        ins.then_inc(self.sem, 1)
        self.n += 1
        self.eng.wait_ge(self.sem, self.n + self.turn)

    def enter(self, i, per):
        self.per, self.n0, self.turn = per, self.n, i * per

    def leave(self, turns):
        assert self.n - self.n0 == self.per
        self.n, self.turn = self.n0 + turns * self.per, 0


def build(nc, I, O):
    ctx = ExitStack()
    with ctx:
        def sb(name, shape, dt=F32):
            return ctx.enter_context(nc.sbuf_tensor(name, shape, dt))

        def sem(name):
            return ctx.enter_context(nc.semaphore(name))

        ring = sb("ring", [P, SLOTS, KMAX, CW])
        ring_base = nc.sbuf_base - 4 * SLOTS * KMAX * CW
        xT = sb("xT", [P, KD, T])
        par = sb("par", [P, 3, P])
        lru_h0 = sb("lru_h0", [P, LT, DEC_B])
        lru_hist = sb("lru_hist", [P, LT, DEC_B * HIST])
        ssd_hist = sb("ssd_hist", [P, XBC, DEC_B * HIST])
        ssd_tail = sb("ssd_tail", [P, XBC, HIST + DEC_B * HIST])
        lru_tail = sb("lru_tail", [P, LT, 36])
        ident = sb("ident", [P, P])
        ones = sb("ones", [P, P])
        qk_mask = sb("qk_mask", [P, P])
        sl_mask = sb("sl_mask", [P, P])
        seq_mask = sb("seq_mask", [NS, NS])
        seq_maskT = sb("seq_maskT", [NS, NS])
        expand = sb("expand", [NS, 4, P])
        of_seq = sb("of_seq", [NS, DEC_B])
        run_row = sb("run_row", [SH, T])
        tri = sb("tri", [P, 8, 8])
        gate_w = sb("gate_w", [P, 2, LT, P])
        router = sb("router", [P, KD, NE])
        dt_par = sb("dt_par", [SH, 4])
        eps = sb("eps", [P, 2])
        pages = sb("pages", [1, DEC_B * NPAGES], I32)
        stat = sb("stat", [P, 160])
        before = sb("before", [P, P])
        iota_i = sb("iota_i", [P, CAP], I32)
        expert_of = sb("expert_of", [1, 16], I32)
        n_rounds = sb("n_rounds", [1, 1], I32)
        ARENA = nc.sbuf_bytes_remaining // 4 - 16
        arena = sb("arena", [P, ARENA])
        arena_base = nc.sbuf_base - 4 * ARENA
        ps = ctx.enter_context(nc.psum_tensor("ps", [P, 8, 512], F32))

        def at(off, *dims):
            n = int(np.prod(dims))
            assert off + n <= ARENA, (off, dims, ARENA)
            v = arena[:, off:off + n]
            if len(dims) == 2:
                return v.rearrange("p (a b) -> p a b", a=dims[0])
            if len(dims) == 3:
                return v.rearrange("p (a b c) -> p a b c", a=dims[0], b=dims[1])
            return v

        def spare(slot, off, *dims):
            off += slot * KMAX * CW
            v = ring.rearrange("p s k n -> p (s k n)")[:, off:off + int(np.prod(dims))]
            if len(dims) == 2:
                return v.rearrange("p (a b) -> p a b", a=dims[0])
            if len(dims) == 3:
                return v.rearrange("p (a b c) -> p a b c", a=dims[0], b=dims[1])
            return v

        def split_spare(name, slot, off, *dims):
            return nc.alloc_sbuf_tensor_at(name, [P, *dims], F32R, offset=ring_base + 4 * (slot * KMAX * CW + off))

        def split_at(name, off, *dims):
            return nc.alloc_sbuf_tensor_at(name, [P, *dims], F32R, offset=arena_base + 4 * off)

        proj = at(0, 20, T)
        cat = at(11520, 8, T)
        xin = at(16128, 5, D)
        shist_in = at(21248, SCONV)
        par_in = at(25344, 3, P)
        h0_in = at(25728, 512)
        lhist_in = at(26240, 512)
        u_pad = at(16128, LT, PADT)
        uc = at(18540, LT, T)
        u_acc = at(28356, PADT)
        lru_a = at(21444, LT * T)
        lru_t = at(23748, LT * T)
        lru_i = at(26052, LT * T)
        qx = at(6912, AT, DEC_B, NS)
        k_tok = at(8960, 5, AW)
        v_tok = at(16128, 5, AW)
        v_pages = [at(18688 + 2048 * n, QUAD, AW) for n in range(4)]
        pp = at(26880, 2, 512)
        ppt = at(27904, 2, 512)
        ks_T = at(28928, AT, NS)
        kt = [at(2048 * n, AT, QUAD * PAGE) for n in range(3)]
        p_s = at(29184, NPAGES * PAGE + NS)
        k_pages = [spare(q, 0, QUAD, AW) for q in range(4)]
        o_s = at(26880, AW)
        p_sT = at(30272, 9, P)
        xf_h, xf_l = split_at("xf_h", 0, KD, T), split_at("xf_l", 4608, KD, T)
        hid_h, hid_l = split_at("hid_h", 9216, FET, T), split_at("hid_l", 15552, FET, T)
        fw_h, fw_l = split_at("fw_h", 21888, RAW, KMAX, P), split_at("fw_l", 26112, RAW, KMAX, P)
        f_s, f_m = at(30336, T), at(30912, T)
        ln_mem = [(at(b, KD, T), at(b + 4608, T), at(b + 5184, T)) for b in (15552, 0, 15552, 15552)]
        xbc = at(0, XBC, T)
        xs_h, xs_l = split_at("xs_h", 18432, KD, T), split_at("xs_l", 23040, KD, T)
        raw = at(27648, 4, PADT)
        acc = at(27648 + 4 * PADT, 2, PADT)
        x_raw = [spare(0, 2048 * n, KD, CW) for n in range(2)]
        SLOT = KMAX * CW
        in_dt = split_spare("in_dt", C_DT % SLOTS, 0, KD, CW)
        xw_h = [split_spare("xw_h0", 0, 4096, KD, P), split_spare("xw_h1", 3, 0, KD, P)]
        xw_l = [split_spare("xw_l0", 3, 1024, KD, P), in_dt[:, :, P:CW]]
        assert C_DT % SLOTS == 2 and 4096 + KD * P <= 2 * SLOT
        rows = at(18432, 4, T)
        DTR, CSR, ECR, WDR = range(4)
        tmpr = at(21472, 5, T)
        tok = at(20736, 3, 5 * SH)
        dec_p = at(21216, SH * NCH)
        dec_s = at(21344, XT, DEC_B)
        b_tok = at(21472, 5, P)
        x_dt = at(22112, 5, 256)
        x_w = at(23392, 5, 256)
        state = at(24672, NCH, 256)
        b_seq = at(25696, DEC_B, P)
        SPARE = [(C_Z + 2) % SLOTS, (C_Z + 3) % SLOTS]
        h0n = [spare(SPARE[0], 1024 * n, DEC_B, P) for n in range(2)]
        ident_r = split_spare("ident_r", SPARE[0], 2048, P)
        sl_mask_r = split_spare("sl_mask_r", SPARE[0], 2176, P)
        cs_h, cs_l = split_spare("cs_h", SPARE[1], 0, SEQ), split_spare("cs_l", SPARE[0], 2304, SEQ)
        ebc = spare(SPARE[1], 512, 2, T)
        ce = spare(SPARE[1], 1664, 2, T)
        st_out = at(26720, 2, 2, P)
        h0t = at(27744, DEC_B, P)
        e_buf = at(28768, 2, T)
        m_buf = at(29920, 2, T)
        d_exp = stat[:, 0:XT]
        z_s = at(18432, 2, T)
        z_q = at(19584, 2, T)
        z_r = at(20736, T)
        z_i = at(21312, T)
        xt_h, xt_l = split_at("xt_h", 0, 5, D), split_at("xt_l", 5120, 5, D)
        xg_h, xg_l = split_at("xg_h", 10240, KD, CAP), split_at("xg_l", 11776, KD, CAP)
        h_h, h_l = split_at("h_h", 13312, FET, CAP), split_at("h_l", 15424, FET, CAP)
        yt_h, yt_l = split_at("yt_h", 13312, 2, D), split_at("yt_l", 15360, 2, D)
        w_h, w_l = split_at("w_h", 17536, RAW, KMAX, P), split_at("w_l", 21760, RAW, KMAX, P)
        hot = split_at("hot", 25984, 5, CAP)
        hotT = split_at("hotT", 26944, 2, T)
        yg = at(28096, KD, CAP)
        h_s = at(29632, 2, CAP)
        h_m = at(30016, 2, CAP)
        slot_of = at(30400, RMAX + 2, 5)
        gate_of = at(30480, RMAX + 2, 5)
        iota = at(30560, CAP)
        gate_now = at(30760, 5)
        slot_gate = at(30768, 2)
        g_w = at(24128, 1856)
        tail_s = at(26000, SCONV)
        tail_l = at(30096, 512)
        y_out = at(0, 5, D)

        conv_w_s = par[:, 0, :].rearrange("p (w t) -> p w t", w=CONV_W)
        conv_b_s = par[:, 1, 0:32]
        norm_g = par[:, 1, 32:48]
        ln_g = [par[:, 1, 48:56], par[:, 1, 80:88], par[:, 1, 56:64], par[:, 1, 88:96]]
        ln_b = [par[:, 1, 64:72], par[:, 1, 96:104], par[:, 1, 72:80], par[:, 1, 104:112]]
        conv_w_l = par[:, 2, 0:16].rearrange("p (w t) -> p w t", w=CONV_W)
        conv_b_l = par[:, 2, 16:20]
        b_gate = [par[:, 2, 20:24], par[:, 2, 24:28]]
        lam = par[:, 2, 28:32]

        loaded = [sem(f"loaded{s}") for s in range(SLOTS)]
        moe_loaded = [sem(f"moe_loaded{s}") for s in range(RAW)]
        used = sem("used")
        in_x, in_par, in_hist = sem("in_x"), sem("in_par"), sem("in_hist")
        in_gatew, in_small, in_pages = sem("in_gatew"), sem("in_small"), sem("in_pages")
        const_ok, pool_c, dve_c, act_c = sem("const_ok"), sem("pool_c"), sem("dve_c"), sem("act_c")
        x_tr, x_up = sem("x_tr"), sem("x_up")
        p_tr, p_up = sem("p_tr"), sem("p_up")
        stages = ["l1", "l2", "xb", "dt", "z", "l6"]
        first = dict(l1=C_L1, l2=C_L2, xb=C_XBC, dt=C_DT, z=C_Z, l6=C_L6)
        per_unit = dict(l6=2)

        def done(stage, n):
            return SLOTS + first[stage] + per_unit.get(stage, 1) * (n + 1)

        free = {s: sem(f"free_{s}") for s in stages}
        free_act1 = sem("free_act1")
        f_bank, f_silu, f_hid, x_lo = sem("f_bank"), sem("f_silu"), sem("f_hid"), sem("x_lo")
        ln_ready = sem("ln_ready")
        ln_mu, ln_c, ln_sq, ln_var, ln_std, ln_n, ln_out = [sem(f"ln_{n}") for n in ("mu", "c", "sq", "var", "std", "n", "out")]
        uc_ok, gr_mm, gr_ok, gi_mm, gi_ok = [sem(n) for n in ("uc_ok", "gr_mm", "gr_ok", "gi_mm", "gi_ok")]
        lam_e, lam_u, lam_l = sem("lam_e"), sem("lam_u"), sem("lam_l")
        la_ok, a_ok, a2_ok, s_ok, g_ok = [sem(n) for n in ("la_ok", "a_ok", "a2_ok", "s_ok", "g_ok")]
        lru_end = sem("lru_end")
        kvt_tr, kvt_up, kvt_up_a, kv_out = sem("kvt_tr"), sem("kvt_up"), sem("kvt_up_a"), sem("kv_out")
        qx_ok = sem("qx_ok")
        sc_mm, mx_ok, ex_ok, pn_ok, pt_mm, pt_ok, o_mm, o_up = [sem(n) for n in ("sc_mm", "mx_ok", "ex_ok", "pn_ok", "pt_mm", "pt_ok", "o_mm", "o_up")]
        v_in = [sem(f"v_in{n}") for n in range(2)]
        k_in = [sem(f"k_in{n}") for n in range(4)]
        kt_mm, kt_dve, kt_act, qs_mm = sem("kt_mm"), sem("kt_dve"), sem("kt_act"), sem("qs_mm")
        s_bias, s_ex, s_pn, s_ptm, s_ptu, s_o, s_oc, s_ot, s_ou = [sem(n) for n in ("s_bias", "s_ex", "s_pn", "s_ptm", "s_ptu", "s_o", "s_oc", "s_ot", "s_ou")]
        cv_y, cv_s = sem("cv_y"), sem("cv_s")
        dt_a, dt_e, dt_u, dt_l, cs_ok, ec_ok, row_ok = [sem(n) for n in ("dt_a", "dt_e", "dt_u", "dt_l", "cs_ok", "ec_ok", "row_ok")]
        tk_mm, tk_up = sem("tk_mm"), sem("tk_up")
        g_mm, g_up, g_up_a, st_mm, st_up = [sem(n) for n in ("g_mm", "g_up", "g_up_a", "st_mm", "st_up")]
        h0_in_s, h0_tr, h0_up, hd_ok = [sem("h0_in_even"), sem("h0_in_odd")], sem("h0_tr"), sem("h0_up"), sem("hd_ok")
        bc_mm, eb_ok, cs_mm, e_ok, m_ok, yt_mm, y_ok = [sem(n) for n in ("bc_mm", "eb_ok", "cs_mm", "e_ok", "m_ok", "yt_mm", "y_ok")]
        ss_mm, ss_ok, ss_out = sem("ss_mm"), sem("ss_ok"), sem("ss_out")
        fs_mm, fs_up, fs_out = sem("fs_mm"), sem("fs_up"), sem("fs_out")
        z_gate, z_sqd, z_sum, z_rt, z_ok = [sem(n) for n in ("z_gate", "z_sqd", "z_sum", "z_rt", "z_ok")]
        row_mm, row_up, tl_out = sem("row_mm"), sem("row_up"), sem("tl_out")
        rt_mm, rt_d, rt_e, rt_m, ct_mm, rt_ok = [sem(n) for n in ("rt_mm", "rt_d", "rt_e", "rt_m", "ct_mm", "rt_ok")]
        xt_mm, xt_hi, xt_lo = sem("xt_mm"), sem("xt_hi"), sem("xt_lo")
        w_hi, w_lo, w_used = sem("w_hi"), sem("w_lo"), sem("w_used")
        hot_ok, ga_mm, ga_hi, ga_lo = sem("hot_ok"), sem("ga_mm"), sem("ga_hi"), sem("ga_lo")
        e_silu, e_bank, e_h, d_ok = sem("e_silu"), sem("e_bank"), sem("e_h"), sem("d_ok")
        ty_mm, ty_hi, ty_lo, sc_y, sc_ok = sem("ty_mm"), sem("ty_hi"), sem("ty_lo"), sem("sc_y"), sem("sc_ok")
        th_mm, th_ok = sem("th_mm"), sem("th_ok")
        out_st = sem("out_st")

        block = ctx.enter_context(nc.Block())

        def cols(w, k0, nk, c0):
            return w[k0 * P:(k0 + nk) * P, :].rearrange("(k p) n -> p k n", p=P)[:, :, ds(c0, CW)]

        @block.sync
        def _(sp):
            for c in range(NCH):
                sp.dma_start(xin[:, c, :], I["x_prompt"][0, c * P:(c + 1) * P, :]).then_inc(in_x, 16)
            sp.dma_start(xin[0:NS, NCH, :], I["x_sample"].rearrange("b t d -> (b t) d")).then_inc(in_x, 16)

            def load(c, i, parts):
                slot = c % SLOTS
                sp.wait_ge(used, c + 1 + SLOTS * i)
                for dst, src in parts(ring[:, slot]):
                    sp.dma_start(dst, src).then_inc(loaded[slot], 16)

            def pair(w, k0, nk, c0):
                h = nk // 2
                return lambda s: [(s[:, 0:h, :], cols(w, k0, h, c0)), (s[:, h:nk, :], cols(w, k0 + h, nk - h, c0))]

            def up(w1, w3, c0):
                def tile(w):
                    return w.rearrange("(k p) n -> p k n", p=P)[:, :, ds(c0, P)]
                return lambda s: [(s[:, 0:KD, 0:P], tile(w1)), (s[:, 0:KD, P:CW], tile(w3))]

            w = I["w_in_even"][0]
            for n, u in enumerate(L1_ORDER):
                load(C_L1 + n, 0, pair(w, 0, KD, u * CW))

            sp.wait_ge(in_pages, 16)
            sp.wait_ge(used, SLOTS + C_L2)
            for pr in range(DEC_B // 2):
                for which, cache in ((0, I["cache_k"]), (1, I["cache_v"])):
                    for q in range(4):
                        if which == 0 and pr > 0:
                            sp.wait_ge(kt_mm, 4 * (4 * (pr - 1) + q + 1))
                        if which == 1 and pr == 0 and q == 0:
                            sp.wait_ge(lru_end, 1)
                        if which == 1 and pr > 0:
                            sp.wait_ge(s_o, 2 * (pr - 1) + q // 2 + 1)
                        for pg in range(QUAD):
                            at_page = (2 * pr + q // 2) * NPAGES + (q % 2) * QUAD + pg
                            page = sp.value_load(pages[0:1, at_page:at_page + 1], min_val=0, max_val=NPOOL - 1)
                            dst, here = ((k_pages, k_in[q]), (v_pages, v_in[q // 2]))[which]
                            sp.dma_start(dst[q][:, pg, :], cache[0][page].rearrange("t h d -> t (h d)")).then_inc(here, 16)
            sp.wait_ge(kt_mm, 4 * 16)
            w = I["w_out_even"][0]
            for j in range(KD // 2):
                load(C_L2 + j, 0, pair(w, 0, KD, j * CW))
            sp.sem_inc(w_lo, 2 * RAW)
            for r in range(FROUNDS):
                for m in range(PER_E):
                    n = PER_E * r + m
                    if n < RAW:
                        sp.wait_ge(used, SLOTS + next(c for c in range(C_L2, C_XBC) if c % SLOTS == n) + 1)
                    sp.wait_ge(w_lo, 2 * n + 2)
                    parts = (up(I["ffn_w1"][0], I["ffn_w3"][0], (FET * r + m) * P) if m < FET
                             else pair(I["ffn_w2"][0], FET * r, FET, (m - FET) * CW))
                    for dst, src in reversed(parts(ring[:, m % RAW])):
                        sp.dma_start(dst, src).then_inc(moe_loaded[m % RAW], 16)
            sp.wait_ge(w_lo, 2 * RAW + TILES * FROUNDS)
            w = I["ssd_w_in"][0]
            with sp.Fori(0, XU // SLOTS) as i:
                for j in range(SLOTS):
                    n = SLOTS * i + j
                    sp.wait_ge(w_lo, 2 * RAW + TILES * FROUNDS + 2 * n - 2)
                    for dst, src in pair(w, 0, KD, n * CW + 2048)(x_raw[j % 2]):
                        sp.dma_start(dst, src).then_inc(loaded[(C_XBC + j) % SLOTS], 16)
            load(C_DT, 0, lambda s: [
                (s[:, 4 * h:4 * h + 4, 0:SH],
                 w[4 * h * P:(4 * h + 4) * P, 2048 + SCONV:SIN].rearrange("(k p) n -> p k n", p=P)) for h in range(2)])
            sp.wait_ge(used, SLOTS + C_DT)
            with sp.Fori(0, XT // 2 // SLOTS) as i:
                for j in range(SLOTS):
                    if j == 2:
                        sp.wait_ge(ss_out, 16 * XT)
                        sp.wait_ge(yt_mm, XT)
                    load(C_Z + j, i, pair(w, 0, KD, (i * SLOTS + j) * CW))
            w = I["ssd_w_out"][0]
            for j in range(KD // 2):
                for h in range(2):
                    load(C_L6 + 2 * j + h, 0, pair(w, 8 * h, 8, j * CW))
            sp.wait_ge(used, SLOTS + C_MOE)
            sp.wait_ge(rt_ok, 1)
            rounds = sp.value_load(n_rounds[0:1, 0:1], min_val=1, max_val=RMAX)

            def moe_chunk(r, e, m):
                sp.wait_ge(w_lo, 2 * (PER_E * (r + FROUNDS) + m + XU) + 2)
                w1, w3, w2 = (I[n][0][e] for n in ("moe_w1", "moe_w3", "moe_w2"))
                parts = up(w1, w3, m * P) if m < FET else pair(w2, 0, FET, (m - FET) * CW)
                for dst, src in reversed(parts(ring[:, m % RAW])):
                    sp.dma_start(dst, src).then_inc(moe_loaded[m % RAW], 16)
            e0 = sp.value_load(expert_of[0:1, 0:1], min_val=0, max_val=NE - 1)
            for m in range(2):
                moe_chunk(0, e0, m)
            with sp.Fori(0, rounds) as r:
                e = sp.value_load(expert_of[0:1, ds(r, 1)], min_val=0, max_val=NE - 1)
                for m in range(2, PER_E):
                    moe_chunk(r, e, m)
                e = sp.value_load(expert_of[0:1, ds(r + 1, 1)], min_val=0, max_val=NE - 1)
                for m in range(2):
                    moe_chunk(r + 1, e, m)

        @block.gpsimd
        def _(pool):
            link = Chain(pool, pool_c)
            pool.memset(ident[:], 0.0)
            pool.memset(ones[:], 1.0)
            pool.memset(qk_mask[:], 0.0)
            pool.memset(sl_mask[:], 0.0)
            pool.memset(seq_mask[:], 0.0)
            pool.memset(seq_maskT[:], 0.0)
            pool.memset(expand[:], 0.0)
            pool.memset(of_seq[:], 1.0)
            pool.memset(run_row[:], 1.0)
            pool.memset(tri[:], 0.0)
            pool.memset(before[:], 1.0)
            pool.iota(iota_i[:], pattern=[[1, CAP]], base=0, channel_multiplier=0)
            pool.memset(eps[:, 0:1], LN_EPS)
            pool.memset(eps[:, 1:2], RMS_EPS)
            link(pool.memset(gate_w[:], 0.0))
            sel = pool.affine_select
            sel(out=ident[:], in_=ident[:], compare_op=ALU.not_equal, fill=1.0, base=0, pattern=[[-1, P]], channel_multiplier=1)
            sel(out=qk_mask[:], in_=qk_mask[:], compare_op=ALU.is_ge, fill=NEG, base=0, pattern=[[-1, P]], channel_multiplier=1)
            sel(out=sl_mask[:], in_=sl_mask[:], compare_op=ALU.is_ge, fill=NEG, base=0, pattern=[[1, P]], channel_multiplier=-1)
            sel(out=before[:], in_=before[:], compare_op=ALU.is_ge, fill=0.0, base=-1, pattern=[[1, P]], channel_multiplier=-1)
            sm = seq_mask[:].rearrange("p (b t) -> p b t", t=DEC_T)
            smt = seq_maskT[:].rearrange("p (b t) -> p b t", t=DEC_T)
            sel(out=sm, in_=sm, compare_op=ALU.is_ge, fill=NEG, base=0, pattern=[[DEC_T, DEC_B], [1, DEC_T]], channel_multiplier=-1)
            sel(out=smt, in_=smt, compare_op=ALU.is_ge, fill=NEG, base=0, pattern=[[-DEC_T, DEC_B], [-1, DEC_T]], channel_multiplier=1)
            sel(out=of_seq[:], in_=of_seq[:], compare_op=ALU.is_ge, fill=0.0, base=0, pattern=[[-DEC_T, DEC_B]], channel_multiplier=1)
            for pr in range(4):
                v = expand[:, pr, :].rearrange("p (b h q) -> p b h q", b=2, h=HEADS)
                sel(out=v, in_=v, compare_op=ALU.not_equal, fill=1.0, base=-2 * DEC_T * pr,
                    pattern=[[-DEC_T, 2], [0, HEADS], [-1, DEC_T]], channel_multiplier=1)
            for e in range(1, NE):
                pool.memset(tri[:, e, 0:e], 1.0)
            pool.memset(run_row[:, 0:SEQ:P], 0.0)
            link(pool.memset(run_row[:, SEQ:T:DEC_T], 0.0))
            sel(out=sm, in_=sm, compare_op=ALU.is_ge, fill=NEG, base=0, pattern=[[-DEC_T, DEC_B], [0, DEC_T]], channel_multiplier=1)
            sel(out=smt, in_=smt, compare_op=ALU.is_ge, fill=NEG, base=DEC_T - 1, pattern=[[DEC_T, DEC_B], [0, DEC_T]], channel_multiplier=-1)
            sel(out=of_seq[:], in_=of_seq[:], compare_op=ALU.is_ge, fill=0.0, base=DEC_T - 1, pattern=[[DEC_T, DEC_B]],
                channel_multiplier=-1).then_inc(const_ok, 1)

            ld = pool.dma_start
            ld(pages[0:1, :], I["page_table"].rearrange("b (o n) -> o (b n)", o=1)).then_inc(in_pages, 16)
            ld(router[:], I["moe_router"][0].rearrange("(k p) e -> p k e", p=P)).then_inc(in_small, 16)
            for n, name in enumerate(("ssd_dt_bias", "ssd_a_log", "ssd_d")):
                ld(dt_par[:, n:n + 1], I[name].rearrange("o h -> h o")).then_inc(in_small, 16)
            for hh in range(2):
                for n, name in enumerate(("lru_w_a", "lru_w_x")):
                    src = I[name][0].rearrange("(t h) d e -> h d t e", h=2)[hh]
                    pool.dma_start(gate_w[64 * hh:64 * hh + 64, n, :, 64 * hh:64 * hh + 64], src).then_inc(in_gatew, 16)

            st = pool.dma_start
            pool.wait_ge(kvt_up, 8)
            pool.wait_ge(kvt_up_a, 8)
            for t_, pn, sn in ((k_tok, "k_prompt", "k_sample"), (v_tok, "v_prompt", "v_sample")):
                dst = O[pn][0, 0].rearrange("(c p) h d -> p c (h d)", p=P)
                st(dst, t_[:, 0:NCH, :]).then_inc(kv_out, 16)
                st(O[sn][0].rearrange("b t h d -> (b t) (h d)"), t_[0:NS, NCH, :]).then_inc(kv_out, 16)
            def h0_load(t):
                pool.dma_start(h0n[t % 2], I["state_ssm"][0].rearrange("b (t h) p n -> t (h p) b n", h=2)[t]).then_inc(h0_in_s[t % 2], 16)
            pool.wait_ge(row_ok, 1)
            h0_load(0)
            h0_load(1)
            pool.wait_ge(tk_up, 1)
            for t in range(XT):
                pool.wait_ge(h0_tr, t + 1)
                h = h0n[t % 2]
                pool.tensor_tensor(h, h, dec_s[:, t, :].unsqueeze(2).broadcast_to([P, DEC_B, P]), ALU.mult).then_inc(hd_ok, 1)
                if t % 2 == 0:
                    g = t // 2
                    pool.wait_ge(fs_up, g + 1)
                    st(O["ssm_prompt"][0, 0].rearrange("(g t h) p n -> g (h p) t n", h=2, t=2)[g], st_out[:, g % 2]).then_inc(fs_out, 16)
                pool.wait_ge(ss_ok, t + 1)
                st(O["ssm_sample"][0].rearrange("b (t h) p n -> t (h p) b n", h=2)[t], h).then_inc(ss_out, 16)
                if t + 2 < XT:
                    pool.wait_ge(ss_out, 16 * (t + 1))
                    h0_load(t + 2)
            pool.wait_ge(row_up, 9)
            st(O["ssd_conv_prompt"][0, 0], tail_s[0:HIST, :]).then_inc(tl_out, 16)
            st(O["ssd_conv_sample"][0].rearrange("b t d -> (b t) d"), tail_s[HIST:HIST + DEC_B * HIST, :]).then_inc(tl_out, 16)
            st(O["lru_h_prompt"][0], tail_l[0:1, :]).then_inc(tl_out, 16)
            st(O["lru_h_sample"][0], tail_l[1:9, :]).then_inc(tl_out, 16)
            st(O["lru_conv_prompt"][0, 0], tail_l[9:12, :]).then_inc(tl_out, 16)
            st(O["lru_conv_sample"][0].rearrange("b t d -> (b t) d"), tail_l[12:36, :]).then_inc(tl_out, 16)
            for c in range(NCH + 1):
                pool.wait_ge(row_up, 9 + 2 * (c + 1))
                if c < NCH:
                    st(O["y_prompt"][0, c * P:(c + 1) * P, :], y_out[:, c, :]).then_inc(out_st, 16)
                else:
                    st(O["y_sample"].rearrange("b t d -> (b t) d"), y_out[0:NS, c, :]).then_inc(out_st, 16)
            pool.wait_ge(kv_out, 64)
            pool.wait_ge(ss_out, 16 * XT)
            pool.wait_ge(fs_out, 16 * SG)
            pool.wait_ge(tl_out, 96)
            pool.wait_ge(out_st, 16 * 5)

        def of_samples(a):
            return a[:, SEQ + HIST:].rearrange("p (b t) -> p b t", t=HIST + DEC_T)[:, :, 0:DEC_T]

        CHUNKS = [(P, c * P) for c in range(NCH)] + [(NS, SEQ)]

        @block.tensor
        def _(pe):
            mmul, tr = pe.matmul, pe.transpose
            pe.sem_inc(used, SLOTS)

            def unit(stage, n, bank, parts, X, M=P):
                pe.wait_ge(free[stage], n + 1)
                if stage == "l1":
                    pe.wait_ge(free_act1, n + 1)
                total = sum(p[4] for p in parts)
                for s, v, _, _, _ in parts:
                    pe.wait_ge(s, v)
                tiles = 1 if M < P else 2
                for q, (_, _, slot, k0, nk) in enumerate(parts):
                    for j in range(tiles):
                        for k in range(nk):
                            for h in range(2):
                                last = mmul(ps[0:M, bank + 2 * j + h, 0:HALF], slot[:, k, j * P:j * P + M],
                                            X[:, k0 + k, HALF * h:HALF * (h + 1)],
                                            start=(k0 + k == 0), stop=(k0 + k == total - 1))
                    last.then_inc(used, 1)

            def part(c, i=0, k0=0, nk=KD):
                return (loaded[c % SLOTS], 32 * (c // SLOTS + 1 + i), ring[:, c % SLOTS], k0, nk)

            def layer_norm(n):
                sq = ln_mem[n][0]
                pe.wait_ge(ln_ready, n + 1)
                for k in range(KD):
                    for h in range(2):
                        last = mmul(ps[:, h, 0:HALF], ones[:], xT[:, k, HALF * h:HALF * (h + 1)], start=(k == 0), stop=(k == KD - 1))
                last.then_inc(ln_mu, 1)
                for k in range(KD):
                    pe.wait_ge(ln_sq, KD * n + k + 1)
                    for h in range(2):
                        last = mmul(ps[:, 2 + h, 0:HALF], ones[:], sq[:, k, HALF * h:HALF * (h + 1)], start=(k == 0), stop=(k == KD - 1))
                last.then_inc(ln_var, 1)
                if n >= 2:
                    pe.wait_ge(ln_out, KD * (n + 1))

            pe.wait_ge(const_ok, 1)
            pe.wait_ge(in_x, 80)
            for k in range(KD):
                if k >= 4:
                    pe.wait_ge(x_up, k - 3)
                b = 2 * (k % 4)
                for c, (n, _) in enumerate(CHUNKS):
                    last = tr(ps[:, b + c // 4, (c % 4) * P:(c % 4) * P + n], xin[0:n, c, k * P:(k + 1) * P], ident[0:n, 0:n])
                last.then_inc(x_tr, 1)
            pe.wait_ge(x_up, KD)
            pe.wait_ge(in_par, 16 * 12)
            pe.wait_ge(in_hist, 48)
            for n, r in enumerate((P, 112, 32)):
                last = tr(ps[:, 0, n * P:n * P + r], par_in[0:r, n, :], ident[0:r, 0:r])
            for t in range(LT):
                tr(ps[:, 1, t * DEC_B:(t + 1) * DEC_B], h0_in[0:DEC_B, t * P:(t + 1) * P], ident[0:DEC_B, 0:DEC_B])
                tr(ps[:, 1, 64 + t * 24:64 + (t + 1) * 24], lhist_in[0:24, t * P:(t + 1) * P], ident[0:24, 0:24])
            for t in range(XBC):
                last = tr(ps[:, 2 + t // 16, (t % 16) * 24:(t % 16 + 1) * 24], shist_in[0:24, t * P:(t + 1) * P], ident[0:24, 0:24])
            last.then_inc(p_tr, 1)

            for n in range(L1_GATES):
                unit("l1", n, 4 * (n % 2), [part(C_L1 + n)], xT)
            pe.wait_ge(free["l1"], 2 + L1_GATES)
            pe.wait_ge(free_act1, 2 + L1_GATES)
            pe.wait_ge(uc_ok, 1)
            pe.wait_ge(in_gatew, 64)
            for gate, done in ((0, gr_mm), (1, gi_mm)):
                if gate:
                    pe.wait_ge(gr_ok, LT)
                for t in range(LT):
                    for h in range(2):
                        last = mmul(ps[:, 2 * t + h, 0:HALF], gate_w[:, gate, t, :], uc[:, t, HALF * h:HALF * (h + 1)], start=True, stop=True)
                    last.then_inc(done, 1)
            pe.wait_ge(gi_ok, LT)
            for n in range(L1_GATES, 10):
                unit("l1", n, 4 * (n % 2), [part(C_L1 + n)], xT)
            pe.wait_ge(free["l1"], 12)
            pe.wait_ge(free_act1, 12)

            pe.wait_ge(lru_end, 1)
            for n in range(8):
                if n >= 4:
                    pe.wait_ge(kvt_up, n - 3)
                    pe.wait_ge(kvt_up_a, n - 3)
                b = 2 * (n % 4)
                for c, (m, c0) in enumerate(CHUNKS):
                    last = tr(ps[0:m, b + c // 4, (c % 4) * P:(c % 4 + 1) * P], proj[:, 4 + n, c0:c0 + m], ident[:])
                last.then_inc(kvt_tr, 1)
            pe.wait_ge(kvt_up, 8)
            pe.wait_ge(kvt_up_a, 8)

            NQ = HEADS * NCH

            def scores(n):
                h, qt = n // NCH, n % NCH
                r = 64 * (h % 2)
                if n >= 3:
                    pe.wait_ge(ex_ok, n - 2)
                w = (qt + 1) * P
                mmul(ps[:, n % 3, 0:w], proj[r:r + 64, h // 2, qt * P:(qt + 1) * P], proj[r:r + 64, 4 + h // 2, 0:w], start=True, stop=False)
                mmul(ps[:, n % 3, w - P:w], ident[:], qk_mask[:], start=False, stop=True).then_inc(sc_mm, 1)

            def weighted(n):
                h, qt = n // NCH, n % NCH
                pe.wait_ge(pt_ok, n + 1)
                if n % 8 == 0 and n >= 16:
                    pe.wait_ge(o_up, n // 8 - 1)
                r, b = 64 * (h % 2), 4 + (h // 2) % 2
                for c in range(qt + 1):
                    last = mmul(ps[r:r + 64, b, qt * P:(qt + 1) * P], v_tok[:, c, h * HD:(h + 1) * HD], ppt[:, n % 2, c * P:(c + 1) * P],
                                start=(c == 0), stop=(c == qt))
                last.then_inc(o_mm, 1)

            scores(0)
            scores(1)
            for n in range(NQ):
                if n + 2 < NQ:
                    scores(n + 2)
                pe.wait_ge(pn_ok, n + 1)
                if n >= 2:
                    pe.wait_ge(pt_ok, n - 1)
                for c in range(n % NCH + 1):
                    last = tr(ps[:, 6 + n % 2, c * P:(c + 1) * P], pp[:, n % 2, c * P:(c + 1) * P], ident[:])
                last.then_inc(pt_mm, 1)
                if n:
                    weighted(n - 1)
            weighted(NQ - 1)
            pe.wait_ge(o_up, 4)
            pe.wait_ge(qx_ok, 1)

            NQUAD = 2 * DEC_B

            def keys(n):
                pe.wait_ge(k_in[n % 4], 16 * QUAD * (n // 4 + 1))
                for t in range(AT):
                    if n:
                        pe.wait_ge(kt_dve if n % 2 == 0 else kt_act, 4 * ((n - 1) // 2) + t + 1)
                    for pg in range(QUAD):
                        last = tr(ps[:, t, pg * P:(pg + 1) * P], k_pages[n % 4][:, pg, t * P:(t + 1) * P], ident[:])
                    last.then_inc(kt_mm, 1)

            def quad_scores(n):
                pr, q = n // 4, n % 4
                b2 = q // 2
                pe.wait_ge(kt_act if n % 2 == 0 else kt_dve, 4 * (n // 2) + 4)
                for t in range(AT):
                    last = mmul(ps[64 * b2:64 * b2 + 64, 4 + q % 2, :], qx[:, t, 2 * pr + b2, :], kt[n % 3][:, t, :],
                                start=(t == 0), stop=(t == AT - 1))
                if q % 2 == 1:
                    for t in range(AT):
                        mmul(ps[64 * b2:64 * b2 + 64, 6, 0:NS], qx[:, t, 2 * pr + b2, :], ks_T[:, t, :], start=(t == 0), stop=False)
                    last = mmul(ps[64 * b2:64 * b2 + 64, 6, 0:NS], expand[:, pr, 64 * b2:64 * b2 + 64], seq_maskT[:], start=False, stop=True)
                last.then_inc(qs_mm, 1)

            def turn_back(pr):
                pe.wait_ge(s_oc, pr + 1)
                for t in range(AT):
                    last = tr(ps[:, 6, t * P:(t + 1) * P], o_s[:, t * P:(t + 1) * P], ident[:])
                last.then_inc(s_ot, 1)

            keys(0)
            keys(1)
            for pr in range(DEC_B // 2):
                quad_scores(4 * pr)
                if pr:
                    turn_back(pr - 1)
                keys(4 * pr + 2)
                if pr:
                    pe.wait_ge(s_ou, pr)
                quad_scores(4 * pr + 1)
                keys(4 * pr + 3)
                quad_scores(4 * pr + 2)
                quad_scores(4 * pr + 3)
                if pr < DEC_B // 2 - 1:
                    keys(4 * pr + 4)
                    keys(4 * pr + 5)
                pe.wait_ge(s_pn, pr + 1)
                for rnd, b in ((0, 7), (1, 6), (2, 7)):
                    if rnd == 2:
                        pe.wait_ge(s_ptu, 3 * pr + 1)
                    for c in range(4 * rnd, min(4 * rnd + 4, 9)):
                        n = P if c < 8 else NS
                        last = tr(ps[0:n, b, (c % 4) * P:(c % 4 + 1) * P], p_s[:, c * P:c * P + n], ident[:])
                    last.then_inc(s_ptm, 1)
                pe.wait_ge(s_ptu, 3 * pr + 3)
                for b2 in range(2):
                    pe.wait_ge(v_in[b2], 32 * QUAD * (pr + 1))
                    o = ps[64 * b2:64 * b2 + 64, 7, :]
                    for c in range(NPAGES):
                        mmul(o, p_sT[:, c, 64 * b2:64 * b2 + 64], v_pages[2 * b2 + c // QUAD][:, c % QUAD, :], start=(c == 0), stop=False)
                    mmul(o, p_sT[0:NS, 8, 64 * b2:64 * b2 + 64], v_tok[0:NS, NCH, :], start=False, stop=True).then_inc(s_o, 1)
            turn_back(DEC_B // 2 - 1)
            pe.wait_ge(s_ou, 4)

            for j in range(KD // 2):
                unit("l2", j, 4 * (j % 2), [part(C_L2 + j)], cat)
            layer_norm(0)
            for n in range(PER_E * FROUNDS):
                r, v = n // PER_E, n % PER_E
                if n >= 2:
                    pe.wait_ge(f_bank, n - 1)
                if v == FET:
                    pe.wait_ge(f_hid, FET * (r + 1))
                K, a_h, a_l = (KD, xf_h, xf_l) if v < FET else (FET, hid_h, hid_l)
                for j in range(2):
                    u = 2 * v + j
                    pe.wait_ge(w_lo, 2 * RAW + 1 + u + TILES * r)
                    for q, (w, a) in enumerate(((fw_h, a_h), (fw_l, a_h), (fw_h, a_l))):
                        for k in range(K):
                            if n == 0 and j == 0 and q == 0:
                                pe.wait_ge(x_lo, k + 1)
                            for h in range(2):
                                last = mmul(ps[:, 4 * (n % 2) + 2 * j + h, 0:HALF], w[:, u % RAW, k, :], a[:, k, HALF * h:HALF * (h + 1)],
                                            start=(q == 0 and k == 0), stop=(q == 2 and k == K - 1))
                    last.then_inc(w_used, 1)
            layer_norm(1)

            with pe.Fori(0, XU // SLOTS) as i:
                for j in range(SLOTS):
                    n = SLOTS * i + j
                    pe.wait_ge(free["xb"], n + 1)
                    for q in range(2):
                        pe.wait_ge(w_lo, 2 * RAW + TILES * FROUNDS + 2 * n + q + 1)
                        for part_, (w, a) in enumerate(((xw_h[q], xs_h), (xw_l[q], xs_h), (xw_h[q], xs_l))):
                            for k in range(KD):
                                if j == 0 and q == 0 and part_ == 0:
                                    pe.wait_ge(x_lo, KD + k + 1)
                                for h in range(2):
                                    last = mmul(ps[:, 4 * (j % 2) + 2 * q + h, 0:HALF], w[:, k, :], a[:, k, HALF * h:HALF * (h + 1)],
                                                start=(part_ == 0 and k == 0), stop=(part_ == 2 and k == KD - 1))
                        last.then_inc(w_used if q == 0 else used, 1)
            unit("dt", 0, 0, [part(C_DT)], xT, M=SH)
            pe.wait_ge(row_ok, 1)
            for n, src in enumerate((DTR, CSR, WDR)):
                for c, (m, c0) in enumerate(CHUNKS):
                    last = tr(ps[0:m, 2 + n, c * SH:(c + 1) * SH], rows[0:SH, src, c0:c0 + m], ident[0:SH, 0:SH])
            mmul(ps[:, 5, 0:SH * NCH], ones[0:SH, :], tmpr[0:SH, 1, 0:SH * NCH], start=True, stop=True)
            for t in range(XT):
                for hh in range(2):
                    sel = ident[0:SH, 2 * t + hh:2 * t + hh + 1].broadcast_to([SH, 64])
                    mmul(ps[64 * hh:64 * hh + 64, 6, t * 8:t * 8 + 8], sel, rows[0:SH, ECR, SEQ + DEC_T - 1:T:DEC_T], start=True, stop=True)
                    last = mmul(ps[64 * hh:64 * hh + 64, 6, 128 + t:129 + t], sel, dt_par[:, 2:3], start=True, stop=True)
            last.then_inc(tk_mm, 1)

            def cs_bare(t):
                for hh in range(2):
                    h = 2 * t + hh
                    sel = ident_r[0:SH, h:h + 1].broadcast_to([SH, P])
                    mmul(ps[:, 4 + hh, :], sel, cs_h[0:SH, :], start=True, stop=False)
                    mmul(ps[:, 4 + hh, :], sel, cs_l[0:SH, :], start=False, stop=True).then_inc(bc_mm, 1)

            def cs_mask(t):
                for hh in range(2):
                    pe.wait_ge(eb_ok, 2 * t + hh + 1)
                    mmul(ps[:, 4 + hh, :], ident_r[:], sl_mask_r[:].unsqueeze(1).broadcast_to([P, NCH, P]), start=False, stop=True,
                         skip_group_check=True).then_inc(cs_mm, 1)

            def cs_samples(t):
                for hh in range(2):
                    h = 2 * t + hh
                    mmul(ps[:, 3, 64 + 64 * hh:128 + 64 * hh], ident[0:SH, h:h + 1].broadcast_to([SH, P]), rows[0:SH, CSR, SEQ:T], start=True, stop=True)
                    o = ps[0:NS, 3, 192 + 64 * hh:256 + 64 * hh]
                    mmul(o, ident[0:SH, h:h + 1].broadcast_to([SH, NS]), rows[0:SH, CSR, SEQ:T], start=True, stop=False)
                    last = mmul(o, ident[0:NS, 0:NS], seq_mask[:], start=False, stop=True)
                last.then_inc(cs_mm, 1)

            def h0_turn(t):
                pe.wait_ge(h0_in_s[t % 2], 16 * (t // 2 + 1))
                for b in range(DEC_B):
                    last = tr(ps[:, 6 + b // 4, (b % 4) * P:(b % 4 + 1) * P], h0n[t % 2][:, b, :], ident[:])
                last.then_inc(h0_tr, 1)

            pe.wait_ge(tk_up, 1)
            cs_bare(0)
            cs_mask(0)
            for g in range(SG):
                Bt, Ct = xbc[:, XT + g, :], xbc[:, XT + BC + g, :]
                for c in range(NCH):
                    mmul(ps[:, 0, c * P:(c + 1) * P], Bt[:, c * P:(c + 1) * P], Ct[:, c * P:(c + 1) * P], start=True, stop=True)
                mmul(ps[0:NS, 1, 0:NS], Bt[:, SEQ:T], Ct[:, SEQ:T], start=True, stop=True)
                if g:
                    pe.wait_ge(y_ok, 2 * g)
                    pe.wait_ge(ss_ok, 2 * g)
                for c in range(NCH):
                    tr(ps[:, 2, c * P:(c + 1) * P], Bt[:, c * P:(c + 1) * P], ident[:])
                    for j in range(2):
                        tr(ps[:, 3 + 3 * j, c * P:(c + 1) * P], xbc[:, 2 * g + j, c * P:(c + 1) * P], ident[:])
                tr(ps[0:NS, 1, P:2 * P], Bt[:, SEQ:T], ident[:])
                for j in range(2):
                    last = tr(ps[0:NS, 1, (2 + j) * P:(3 + j) * P], xbc[:, 2 * g + j, SEQ:T], ident[:])
                last.then_inc(g_mm, 1)
                pe.wait_ge(g_up, g + 1)
                pe.wait_ge(g_up_a, g + 1)
                for c in range(NCH):
                    last = mmul(ps[:, 6 + c // 2, (c % 2) * 256:(c % 2 + 1) * 256], b_tok[:, c, :], x_w[:, c, :], start=True, stop=True)
                last.then_inc(st_mm, 1)
                pe.wait_ge(st_up, g + 1)
                h0_turn(2 * g)
                cs_samples(2 * g)
                for j in range(2):
                    last = tr(ps[:, 2, j * P:(j + 1) * P], state[:, NCH - 1, j * P:(j + 1) * P], ident[:])
                last.then_inc(fs_mm, 1)
                pe.wait_ge(fs_up, g + 1)
                for j in range(2):
                    t = 2 * g + j
                    for hh in range(2):
                        pe.wait_ge(m_ok, 3 * t + hh + 1)
                        hc = (2 * j + hh) * 64
                        for c in range(NCH):
                            o = ps[64 * hh:64 * hh + 64, 2, c * P:(c + 1) * P]
                            mmul(o, x_dt[:, c, hc:hc + 64], m_buf[:, hh, c * P:(c + 1) * P], start=True, stop=(c == 0))
                            if c:
                                mmul(o, state[:, c - 1, hc:hc + 64], ce[:, hh, c * P:(c + 1) * P], start=False, stop=True)
                    pe.wait_ge(m_ok, 3 * t + 3)
                    pe.wait_ge(h0_up, t + 1)
                    for hh in range(2):
                        hc = (2 * j + hh) * 64
                        r = slice(64 * hh, 64 * hh + 64)
                        mmul(ps[r, 3, 0:NS], x_dt[0:NS, NCH, hc:hc + 64], m_buf[0:NS, hh, SEQ:T], start=True, stop=True)
                        for b in range(DEC_B):
                            last = mmul(ps[r, 3, 8 * b:8 * b + 8], h0t[:, b, r], ce[:, hh, SEQ + 8 * b:SEQ + 8 * b + 8], start=False,
                                        stop=True, skip_group_check=True)
                    last.then_inc(yt_mm, 1)
                    if t + 1 < XT:
                        cs_bare(t + 1)
                    for hf in range(2):
                        last = mmul(ps[:, 6 + hf, :], x_w[0:NS, NCH, j * P:(j + 1) * P], b_seq[0:NS, 4 * hf:4 * hf + 4, :].rearrange("p b n -> p (b n)"), start=True, stop=True)
                    last.then_inc(ss_mm, 1)
                    if t + 1 < XT:
                        cs_mask(t + 1)
                    if j == 0:
                        pe.wait_ge(y_ok, t + 1)
                        cs_samples(t + 1)
                        pe.wait_ge(ss_ok, t + 1)
                        h0_turn(t + 1)
            pe.wait_ge(y_ok, XT)
            pe.wait_ge(ss_ok, XT)

            NZ = XT // 2

            def z_sums(n):
                pe.wait_ge(z_sqd, n + 1)
                if n:
                    pe.wait_ge(z_rt, n)
                for k in range(2):
                    for h in range(2):
                        last = mmul(ps[:, 4 + h, 0:HALF], ones[:], z_q[:, k, HALF * h:HALF * (h + 1)], start=(k == 0), stop=(k == 1))
                last.then_inc(z_sum, 1)
            for n in range(NZ):
                unit("z", n, 0, [part(C_Z + n)], xT)
                if n:
                    z_sums(n - 1)
            z_sums(NZ - 1)
            pe.wait_ge(z_ok, NZ)
            for j in range(KD // 2):
                unit("l6", j, 4 * (j % 2), [part(C_L6 + 2 * j, 0, 0, 8), part(C_L6 + 2 * j + 1, 0, 8, 8)], xbc)
            layer_norm(2)
            for n in range(9):
                if n >= 2:
                    pe.wait_ge(row_up, n - 1)
                for q in range(4):
                    t = 4 * n + q
                    if n < 8:
                        last = tr(ps[0:27, n % 2, q * P:(q + 1) * P], ssd_tail[:, t, :], ident[:])
                    else:
                        last = tr(ps[0:36, n % 2, q * P:(q + 1) * P], lru_tail[:, q, :], ident[:])
                last.then_inc(row_mm, 1)
            pe.wait_ge(row_up, 9)
            pe.wait_ge(in_small, 64)
            for c, (m, c0) in enumerate(CHUNKS):
                for k in range(KD):
                    last = mmul(ps[0:m, 4, c * NE:(c + 1) * NE], xT[:, k, c0:c0 + m], router[:, k, :], start=(k == 0), stop=(k == KD - 1))
            last.then_inc(rt_mm, 1)
            for n in range(10):
                m, c0 = CHUNKS[n // 2]
                if n >= 4:
                    pe.wait_ge(xt_lo, n - 3)
                for k in range(4):
                    last = tr(ps[0:m, n % 4, k * P:(k + 1) * P], xT[:, 4 * (n % 2) + k, c0:c0 + m], ident[:])
                last.then_inc(xt_mm, 1)
            pe.wait_ge(rt_m, 1)
            M = g_w[:, 10:50]
            mmul(ps[:, 5, 0:40], before[:], M, start=True, stop=False, skip_group_check=True)
            for c in range(NCH):
                mmul(ps[:, 5, (c + 1) * NE:40], ones[:], M[:, c * NE:(c + 1) * NE].unsqueeze(1).broadcast_to([P, NCH - c, NE]),
                     start=False, stop=(c == NCH - 1), skip_group_check=True)
            for c in range(5):
                last = mmul(ps[:, 6, 0:NE], ones[:], M[:, c * NE:(c + 1) * NE], start=(c == 0), stop=(c == 4))
            last.then_inc(ct_mm, 1)

            def gather(r):
                pe.wait_ge(hot_ok, r + 1)
                for s in range(4):
                    if s >= 2:
                        pe.wait_ge(ga_hi, 4 * r + s - 1)
                        pe.wait_ge(ga_lo, 4 * r + s - 1)
                    for src, b in ((xt_h, 3), (xt_l, 4)):
                        for q in range(2):
                            k = 2 * s + q
                            for c, (m, _) in enumerate(CHUNKS):
                                last = mmul(ps[:, b + 2 * (s % 2), q * CAP:(q + 1) * CAP], src[0:m, c, k * P:(k + 1) * P], hot[0:m, c, :],
                                            start=(c == 0), stop=(c == NCH))
                    last.then_inc(ga_mm, 1)

            def turn(r):
                pe.wait_ge(sc_ok, KD * r + 1)
                pe.wait_ge(ga_hi, 4 * r + 4)
                pe.wait_ge(ga_lo, 4 * r + 4)
                for u, (m, s0) in enumerate(((P, 0), (NS, P))):
                    for c, (n, c0) in enumerate(CHUNKS):
                        last = tr(ps[0:m, 3 + 2 * u + c // 4, (c % 4) * P:(c % 4) * P + n], hot[0:n, c, s0:s0 + m].bitcast(F32), ident[0:n, 0:n])
                last.then_inc(th_mm, 1)
                for u, (m, s0) in enumerate(((P, 0), (NS, P))):
                    for c, (n, c0) in enumerate(CHUNKS):
                        last = mmul(ps[0:m, 7, u:u + 1], hot[0:n, c, s0:s0 + m].bitcast(F32), gate_now[0:n, c:c + 1], start=(c == 0), stop=(c == NCH))
                last.then_inc(th_mm, 1)
                pe.wait_ge(th_ok, 2 * r + 2)

            rounds = None
            pe.wait_ge(rt_ok, 1)
            rounds = pe.value_load(n_rounds[0:1, 0:1], min_val=1, max_val=RMAX)
            gather(0)
            turn(0)
            with pe.Fori(0, rounds) as r:
                for v in range(PER_E):
                    up = v < FET
                    if v < 3 or v == 14:
                        pe.wait_ge(d_ok, 4 * r + (v + 2 if v < 3 else 5))
                    else:
                        pe.wait_ge(e_bank, FET * r + v - 2)
                    if v == FET:
                        gather(r + 1)
                        pe.wait_ge(e_h, FET * r + FET)
                    K, x_h, x_l = (KD, xg_h, xg_l) if up else (FET, h_h, h_l)
                    if v == 0:
                        pe.wait_ge(ga_hi, 4 * r + 4)
                        pe.wait_ge(ga_lo, 4 * r + 4)
                    for j in range(2):
                        u = 2 * v + j
                        pe.wait_ge(w_lo, 2 * RAW + 1 + u + TILES * (r + FROUNDS) + 2 * XU)
                        o = ps[:, v % 3, j * CAP:(j + 1) * CAP]
                        for n, (w, x) in enumerate(((w_h, x_h), (w_l, x_h), (w_h, x_l))):
                            for k in range(K):
                                last = mmul(o, w[:, u % RAW, k, :], x[:, k, :], start=(n == 0 and k == 0), stop=(n == 2 and k == K - 1))
                        last.then_inc(w_used, 1)
                pe.wait_ge(d_ok, 4 * r + 8)
                pe.wait_ge(ga_hi, 4 * r + 8)
                pe.wait_ge(ga_lo, 4 * r + 8)
                for u, (m, s0) in enumerate(((P, 0), (NS, P))):
                    for k in range(KD):
                        last = tr(ps[0:m, 3 + 2 * u + k // 4, (k % 4) * P:(k % 4 + 1) * P], yg[:, k, s0:s0 + m], ident[:])
                    last.then_inc(ty_mm, 1)
                pe.wait_ge(ty_lo, 2 * r + 2)
                for k in range(KD):
                    if k >= 2:
                        pe.wait_ge(sc_ok, KD * r + k)
                    b = 3 + 2 * (k % 2)
                    for h in range(2):
                        cs_ = slice(HALF * h, HALF * (h + 1))
                        n = 0
                        for y in (yt_h, yt_l):
                            for u, m in ((0, P), (1, NS)):
                                last = mmul(ps[:, b + h, 0:HALF], y[0:m, u, k * P:(k + 1) * P], hotT[0:m, u, cs_], start=(n == 0), stop=(n == 3))
                                n += 1
                    last.then_inc(sc_y, 1)
                turn(r + 1)
            layer_norm(3)
            for c, (m, c0) in enumerate(CHUNKS):
                for hf in range(2):
                    n = 2 * c + hf
                    if n >= 4:
                        pe.wait_ge(row_up, 9 + n - 3)
                    for k in range(4):
                        last = tr(ps[0:m, n % 4, k * P:(k + 1) * P], xT[:, 4 * hf + k, c0:c0 + m], ident[:])
                    last.then_inc(row_mm, 1)

        @block.scalar
        def _(act):
            f = act.activation
            link = Chain(act, act_c)

            def rowsof(ap, n):
                return ap.rearrange("o (t p) -> (o t) p", p=P)
            ld = act.dma_start
            ld(par_in[:, 0, :], I["ssd_conv_w"][0].rearrange("w (t p) -> (w t) p", p=P)).then_inc(in_par, 16)
            for lo, name in ((0, "ssd_conv_b"), (32, "ssd_norm_g"), (48, "ln_mix_g"), (64, "ln_mix_b"),
                             (80, "ln_ffn_g"), (96, "ln_ffn_b")):
                src = rowsof(I[name], 0)
                ld(par_in[lo:lo + src.shape[0], 1, :], src).then_inc(in_par, 16)
            ld(par_in[0:16, 2, :], I["lru_conv_w"][0].rearrange("w (t p) -> (w t) p", p=P)).then_inc(in_par, 16)
            ld(par_in[16:20, 2, :], rowsof(I["lru_conv_b"], 0)).then_inc(in_par, 16)
            for lo, name in ((20, "lru_b_a"), (24, "lru_b_x"), (28, "lru_lambda")):
                ld(par_in[lo:lo + 4, 2, :], I[name][0].rearrange("(t h) d -> t (h d)", h=2)).then_inc(in_par, 16)
            ld(h0_in[0:DEC_B, :], I["state_lru_h"][0]).then_inc(in_hist, 16)
            ld(lhist_in[0:DEC_B * HIST, :], I["state_lru_conv"][0].rearrange("b t d -> (b t) d")).then_inc(in_hist, 16)
            ld(shist_in[0:DEC_B * HIST, :], I["state_ssd_conv"][0].rearrange("b t d -> (b t) d")).then_inc(in_hist, 16)

            def banks(b):
                return ps[:, b:b + 2, 0:HALF]

            def halves(v):
                return v.rearrange("p (h n) -> p h n", h=2)

            def layer_norm(n):
                sq, std, _ = ln_mem[n]
                for k in range(KD):
                    act.wait_ge(ln_c, KD * n + k + 1)
                    f(sq[:, k, :], xT[:, k, :], ACT.Square).then_inc(ln_sq, 1)
                act.wait_ge(ln_var, n + 1)
                f(halves(std), banks(2), ACT.Sqrt, bias=eps[:, 0:1], scale=1.0 / D).then_inc(ln_std, 1)
                for k in range(KD):
                    act.wait_ge(ln_n, KD * n + k + 1)
                    if n < 2:
                        f((xf_h, xs_h)[n][:, k, :], xT[:, k, :], ACT.Identity, bias=ln_b[n][:, k:k + 1], scale=ln_g[n][:, k:k + 1])
                    f(xT[:, k, :], xT[:, k, :], ACT.Identity, bias=ln_b[n][:, k:k + 1], scale=ln_g[n][:, k:k + 1]).then_inc(ln_out, 1)

            act.wait_ge(const_ok, 1)
            act.wait_ge(p_up, 1)
            act.sem_inc(free_act1, 2)

            def l1(n):
                act.wait_ge(used, done("l1", n))
                f(halves(proj[:, 2 * L1_ORDER[n] + 1, :]), banks(4 * (n % 2) + 2), ACT.Copy).then_inc(free_act1, 1)
            for n in range(4):
                l1(n)

            act.wait_ge(lam_e, 1)
            f(stat[:, 8:12], stat[:, 4:8], ACT.Exp, scale=-1.0).then_inc(lam_e, 1)
            act.wait_ge(lam_u, 1)
            f(stat[:, 16:20], stat[:, 12:16], ACT.Ln).then_inc(lam_l, 1)
            for n in range(4, L1_GATES):
                l1(n)
            for t in range(LT):
                act.wait_ge(gr_mm, t + 1)
                f(halves(lru_a[:, t * T:(t + 1) * T]), banks(2 * t), ACT.Sigmoid, bias=b_gate[0][:, t:t + 1]).then_inc(gr_ok, 1)
            for t in range(LT):
                act.wait_ge(gi_mm, t + 1)
                f(halves(lru_i[:, t * T:(t + 1) * T]), banks(2 * t), ACT.Sigmoid, bias=b_gate[1][:, t:t + 1]).then_inc(gi_ok, 1)
            act.wait_ge(la_ok, 1)
            link(f(lru_t[:], lru_a[:], ACT.Tanh, scale=-1.0))
            f(lru_a[:], lru_a[:], ACT.Exp).then_inc(a_ok, 1)
            f(proj[:, 16:20, :], proj[:, 16:20, :], ACT.Gelu_apprx_tanh).then_inc(g_ok, 1)
            act.wait_ge(a2_ok, 1)
            f(lru_t[:], lru_t[:], ACT.Sqrt).then_inc(s_ok, 1)
            for n in range(L1_GATES, 10):
                l1(n)

            act.wait_ge(lru_end, 1)
            for n in range(8):
                act.wait_ge(kvt_tr, n + 1)
                dst = (k_tok if n < 4 else v_tok)
                f(dst[0:NS, NCH, (n % 4) * P:(n % 4 + 1) * P], ps[0:NS, 2 * (n % 4) + 1, 0:P], ACT.Copy).then_inc(kvt_up_a, 1)

            NQ = HEADS * NCH
            for n in range(NQ + 1):
                if n < NQ:
                    w = (n % NCH + 1) * P
                    act.wait_ge(mx_ok, n + 1)
                    if n >= 2:
                        act.wait_ge(pt_mm, n - 1)
                    f(pp[:, n % 2, 0:w], ps[:, n % 3, 0:w], ACT.Exp, bias=stat[:, 34 + n % 2:35 + n % 2], scale=HD ** -0.5,
                      accum_out=stat[:, 36 + n % 2:37 + n % 2]).then_inc(ex_ok, 1)
                if n >= 1:
                    m = n - 1
                    w = (m % NCH + 1) * P
                    act.wait_ge(pt_mm, m + 1)
                    if m >= 2:
                        act.wait_ge(o_mm, m - 1)
                    f(ppt[:, m % 2, 0:w], ps[:, 6 + m % 2, 0:w], ACT.Copy).then_inc(pt_ok, 1)

            def keys_out(n):
                if n >= 3:
                    act.wait_ge(qs_mm, n - 2)
                for t in range(AT):
                    act.wait_ge(kt_mm, 4 * n + t + 1)
                    f(kt[n % 3][:, t, :], ps[:, t, :], ACT.Copy).then_inc(kt_act, 1)

            keys_out(0)
            for pr in range(DEC_B // 2):
                keys_out(4 * pr + 2)
                if pr < DEC_B // 2 - 1:
                    keys_out(4 * pr + 4)
                act.wait_ge(s_bias, pr + 1)
                if pr:
                    act.wait_ge(s_ptm, 3 * pr)
                for n in range(NBLK):
                    f(p_s[:, BLK * n:BLK * (n + 1)], ps[:, 4 + n // 2, (n % 2) * BLK:(n % 2 + 1) * BLK], ACT.Exp,
                      bias=stat[:, 40 + n:41 + n], scale=HD ** -0.5, accum_out=stat[:, 48 + n:49 + n])
                f(p_s[:, NBLK * BLK:], ps[:, 6, 0:NS], ACT.Exp, bias=stat[:, 44:45], scale=HD ** -0.5,
                  accum_out=stat[:, 52:53]).then_inc(s_ex, 1)
                for rnd, b in ((0, 7), (1, 6)):
                    act.wait_ge(s_ptm, 3 * pr + rnd + 1)
                    f(p_sT[:, 4 * rnd:4 * rnd + 4, :].rearrange("p c n -> p (c n)"), ps[:, b, :], ACT.Copy).then_inc(s_ptu, 1)
                act.wait_ge(s_ptm, 3 * pr + 3)
                f(p_sT[0:NS, 8, :], ps[0:NS, 7, 0:P], ACT.Copy).then_inc(s_ptu, 1)
                act.wait_ge(s_o, 2 * pr + 2)
                f(o_s[:], ps[:, 7, :], ACT.Copy).then_inc(s_oc, 1)

            act.wait_ge(kv_out, 64)
            act.sem_inc(w_used, RAW)

            def f_round(n):
                u, m = n % TILES, n // 2
                K = KD if u // 2 < FET else FET
                if n % 2 == 0:
                    act.wait_ge(moe_loaded[m % RAW], 32 * (m // RAW + 1))
                act.wait_ge(w_used, n + 1)
                f(fw_h[:, n % RAW, 0:K, :], ring[:, m % RAW, 0:K, (n % 2) * P:(n % 2 + 1) * P], ACT.Copy).then_inc(w_hi, 1)

            act.wait_ge(s_o, 2 * (DEC_B // 2))
            for n in range(RAW):
                f_round(n)
            layer_norm(0)
            for n in range(PER_E * FROUNDS):
                for u in (2 * n + 3, 2 * n + 4):
                    if u < TILES * FROUNDS:
                        f_round(u)
                if n % PER_E < FET:
                    act.wait_ge(w_used, RAW + 2 * n + 2)
                    if n:
                        act.wait_ge(f_bank, n)
                    f(halves(f_s[:]), banks(4 * (n % 2)), ACT.Silu).then_inc(f_silu, 1)
            def x_round(n, q):
                if q == 0:
                    act.wait_ge(loaded[(C_XBC + n) % SLOTS], 32 * ((C_XBC + n) // SLOTS + 1))
                    act.wait_ge(w_used, RAW + TILES * FROUNDS + n)
                else:
                    act.wait_ge(used, SLOTS + C_XBC + n)
                f(xw_h[q][:], x_raw[n % 2][:, :, q * P:(q + 1) * P], ACT.Copy).then_inc(w_hi, 1)

            x_round(0, 0)
            x_round(0, 1)
            layer_norm(1)

            act.sem_inc(free["xb"], 2)
            act.sem_inc(cv_s, 1)

            def raw_out(n, j):
                act.wait_ge(used, done("xb", n))
                act.wait_ge(cv_y, n + 1)
                b, s = 4 * (j % 2), 2 * (j % 2)
                f(raw[:, s:s + 2, HIST:HIST + HALF], ps[:, b:b + 4:2, 0:HALF], ACT.Copy)
                f(raw[:, s:s + 2, HIST + HALF:HIST + SEQ], ps[:, b + 1:b + 4:2, 0:SEQ - HALF], ACT.Copy)
                for q in range(2):
                    smp = raw[:, s + q, HIST + SEQ:].rearrange("p (b t) -> p b t", t=HIST + DEC_T)
                    last = f(smp[:, :, HIST:], ps[:, b + 1 + 2 * q, SEQ - HALF:HALF].rearrange("p (b t) -> p b t", t=DEC_T), ACT.Copy)
                last.then_inc(free["xb"], 1)

            def conv_silu(n):
                act.wait_ge(cv_y, n + 3)
                f(xbc[:, 2 * n:2 * n + 2, 0:SEQ], acc[:, :, 0:SEQ], ACT.Silu)
                for q in range(2):
                    last = f(xbc[:, ds(2 * n + q, 1), SEQ:T].rearrange("p o (b t) -> p (o b) t", t=DEC_T), of_samples(acc[:, q, :]), ACT.Silu)
                last.then_inc(cv_s, 1)
            for n in range(XU):
                if n:
                    x_round(n, 1)
                if n + 1 < XU:
                    x_round(n + 1, 0)
                if n:
                    conv_silu(n - 1)
                raw_out(n, n)
            conv_silu(XU - 1)

            act.wait_ge(dt_a, 1)
            f(tmpr[0:SH, 2, :], tmpr[0:SH, 1, :], ACT.Exp, scale=-1.0)
            f(dt_par[:, 3:4], dt_par[:, 1:2], ACT.Exp).then_inc(dt_e, 1)
            act.wait_ge(dt_u, 1)
            f(tmpr[0:SH, 1, :], tmpr[0:SH, 3, :], ACT.Ln).then_inc(dt_l, 1)
            act.wait_ge(cs_ok, 1)
            f(rows[0:SH, ECR, :], rows[0:SH, CSR, :], ACT.Exp)
            f(tmpr[0:SH, 0, :], tmpr[0:SH, 0, :], ACT.Exp).then_inc(ec_ok, 1)

            def exps(t):
                for hh in range(2):
                    act.wait_ge(bc_mm, 2 * t + hh + 1)
                    f(ebc[:, hh, 0:SEQ], ps[:, 4 + hh, :], ACT.Exp).then_inc(eb_ok, 1)
                for hh in range(2):
                    h = 2 * t + hh
                    act.wait_ge(cs_mm, 3 * t + hh + 1)
                    for c in range(NCH):
                        i = f(e_buf[:, hh, c * P:(c + 1) * P], ps[:, 4 + hh, c * P:(c + 1) * P], ACT.Exp, bias=tok[:, 1, c * SH + h:c * SH + h + 1])
                    i.then_inc(e_ok, 1)

            def exps_samples(t):
                act.wait_ge(cs_mm, 3 * t + 3)
                f(ebc[:, :, SEQ:T], ps[:, 3, 64:192].rearrange("p (u n) -> p u n", u=2), ACT.Exp)
                for hh in range(2):
                    h = 2 * t + hh
                    i = f(e_buf[0:NS, hh, SEQ:T], ps[0:NS, 3, 192 + 64 * hh:256 + 64 * hh], ACT.Exp,
                          bias=tok[0:NS, 1, NCH * SH + h:NCH * SH + h + 1])
                i.then_inc(e_ok, 1)

            act.wait_ge(tk_up, 1)
            exps(0)
            for g in range(SG):
                act.wait_ge(g_mm, g + 1)
                f(b_tok[:, 0:NCH, :].rearrange("p c n -> p (c n)"), ps[:, 2, :], ACT.Copy).then_inc(g_up_a, 1)
                for j in range(2):
                    t = 2 * g + j
                    if j:
                        exps_samples(t)
                    act.wait_ge(h0_tr, t + 1)
                    f(h0t[:].rearrange("p (u b) n -> p u (b n)", u=2), ps[:, 6:8, :], ACT.Copy).then_inc(h0_up, 1)
                    if j == 0:
                        exps_samples(t)
                    if j == 0:
                        act.wait_ge(fs_mm, g + 1)
                        if g >= 2:
                            act.wait_ge(fs_out, 16 * (g - 1))
                        f(st_out[:, g % 2].rearrange("p a n -> p (a n)"), ps[:, 2, 0:2 * P], ACT.Copy).then_inc(fs_up, 1)
                    if t + 1 < XT:
                        act.wait_ge(m_ok, 3 * t + 3)
                        exps(t + 1)

            act.sem_inc(free["z"], 1)
            NZ = XT // 2

            def z_root(n):
                act.wait_ge(z_sum, n + 1)
                if n:
                    act.wait_ge(z_ok, n)
                f(halves(z_r), banks(4), ACT.Sqrt, bias=eps[:, 1:2], scale=1.0 / (2 * P)).then_inc(z_rt, 1)
            for n in range(NZ):
                act.wait_ge(used, done("z", n))
                if n:
                    act.wait_ge(z_gate, n)
                f(z_s[:].rearrange("p k (h n) -> p (k h) n", h=2), ps[:, 0:4, 0:HALF], ACT.Silu).then_inc(free["z"], 1)
                if n:
                    z_root(n - 1)
                act.wait_ge(z_gate, n + 1)
                f(z_q[:], xbc[:, 2 * n:2 * n + 2, :], ACT.Square).then_inc(z_sqd, 1)
            z_root(NZ - 1)
            layer_norm(2)
            act.wait_ge(rt_d, 1)
            f(g_w[:, 0:5], g_w[:, 5:10], ACT.Exp).then_inc(rt_e, 1)
            act.wait_ge(tl_out, 96)
            for n in range(10):
                m = CHUNKS[n // 2][0]
                act.wait_ge(xt_mm, n + 1)
                f(xt_h[0:m, n // 2, 512 * (n % 2):512 * (n % 2) + 512], ps[0:m, n % 4, :], ACT.Copy).then_inc(xt_hi, 1)

            act.wait_ge(rt_ok, 1)
            rounds = act.value_load(n_rounds[0:1, 0:1], min_val=1, max_val=RMAX)

            def w_round(r, u):
                m, j = u // 2, u % 2
                K = KD if m < FET else FET
                if j == 0 or u == 3:
                    act.wait_ge(moe_loaded[m % RAW], 32 * (5 * (r + FROUNDS) + m // RAW + 1))
                act.wait_ge(w_used, TILES * (r + FROUNDS) + XU + u + 1)
                f(w_h[:, u % RAW, 0:K, :], ring[:, m % RAW, 0:K, j * P:(j + 1) * P], ACT.Copy).then_inc(w_hi, 1)

            def gather_lo(r):
                for s in range(4):
                    act.wait_ge(ga_mm, 4 * r + s + 1)
                    f(xg_l[:, 2 * s:2 * s + 2, :].rearrange("p k n -> p (k n)"), ps[:, 4 + 2 * (s % 2), 0:2 * CAP], ACT.Copy).then_inc(ga_lo, 1)

            act.sem_inc(d_ok, 4)
            for u in range(RAW):
                w_round(0, u)
            gather_lo(0)
            with act.Fori(0, rounds) as r:
                for v in range(PER_E):
                    for u in (2 * v + 3, 2 * v + 4):
                        w_round(r + u // TILES, u % TILES)
                    act.wait_ge(w_used, RAW + 2 * v + 2 + TILES * (r + FROUNDS) + XU)
                    if v < FET:
                        act.wait_ge(e_bank, FET * r + v + 1)
                        f(h_s[:, v % 2, :], ps[:, v % 3, 0:CAP], ACT.Silu).then_inc(e_silu, 1)
                    else:
                        w = 2 * (v - FET)
                        f(yg[:, w:w + 2, :].rearrange("p k n -> p (k n)"), ps[:, v % 3, 0:2 * CAP], ACT.Copy).then_inc(d_ok, 1)
                    if v == FET - 1:
                        gather_lo(r + 1)
                for u, m in ((0, P), (1, NS)):
                    act.wait_ge(ty_mm, 2 * r + u + 1)
                    f(yt_h[0:m, u, :].rearrange("p (g n) -> p g n", g=2), ps[0:m, 3 + 2 * u:5 + 2 * u, :], ACT.Copy, scale=slot_gate[0:m, u:u + 1]).then_inc(ty_hi, 1)
            layer_norm(3)

        @block.vector
        def _(dve):
            link = Chain(dve, dve_c)
            tt, tsc, stt, cp = dve.tensor_tensor, dve.tensor_scalar, dve.scalar_tensor_tensor, dve.tensor_copy

            def banks(b):
                return ps[:, b:b + 2, 0:HALF]

            def halves(v):
                return v.rearrange("p (h n) -> p h n", h=2)

            def layer_norm(n):
                _, std, rstd = ln_mem[n]
                dve.wait_ge(ln_mu, n + 1)
                mu = banks(0)
                link(tsc(halves(std), mu, 1.0 / D, None, ALU.mult))
                for k in range(KD):
                    tt(xT[:, k, :], xT[:, k, :], std[:], ALU.subtract).then_inc(ln_c, 1)
                dve.wait_ge(ln_std, n + 1)
                link(dve.reciprocal(rstd[:], std[:]))
                for k in range(KD):
                    tt(xT[:, k, :], xT[:, k, :], rstd[:], ALU.mult).then_inc(ln_n, 1)

            def residual(stage, n, bank, last=None):
                dve.wait_ge(used, done(stage, n))
                for q in range(2):
                    i = stt(halves(xT[:, 2 * n + q, :]), halves(xT[:, 2 * n + q, :]), ALPHA, banks(bank + 2 * q), ALU.mult, ALU.add)
                i.then_inc(last or free[stage], 1)

            for k in range(KD):
                dve.wait_ge(x_tr, k + 1)
                b = 2 * (k % 4)
                cp(xT[:, k, 0:SEQ], ps[:, b, :])
                cp(xT[:, k, SEQ:T], ps[:, b + 1, 0:NS]).then_inc(x_up, 1)
            dve.wait_ge(p_tr, 1)
            cp(par[:, 0, :], ps[:, 0, 0:P])
            cp(par[:, 1, 0:112], ps[:, 0, P:P + 112])
            cp(par[:, 2, 0:32], ps[:, 0, 2 * P:2 * P + 32])
            cp(lru_h0[:].rearrange("p t b -> p (t b)"), ps[:, 1, 0:LT * DEC_B])
            cp(lru_hist[:].rearrange("p t n -> p (t n)"), ps[:, 1, 64:64 + LT * 24])
            for u in range(2):
                last = cp(ssd_hist[:, 16 * u:16 * u + 16, :].rearrange("p t n -> p (t n)"), ps[:, 2 + u, 0:384])
            last.then_inc(p_up, 1)
            dve.wait_ge(p_up, 1)
            dve.sem_inc(free["l1"], 2)

            def l1(n):
                dve.wait_ge(used, done("l1", n))
                cp(halves(proj[:, 2 * L1_ORDER[n], :]), banks(4 * (n % 2))).then_inc(free["l1"], 1)
            l1(0)
            l1(1)

            dve.wait_ge(free_act1, 4)
            dve.wait_ge(free["l1"], 4)
            padded = u_pad[:, :, HIST + SEQ:].rearrange("p t (b n) -> p t b n", b=DEC_B)
            dve.memset(u_pad[:, :, 0:HIST], 0.0)
            cp(u_pad[:, :, HIST:HIST + SEQ], proj[:, 12:16, 0:SEQ])
            for t in range(LT):
                cp(padded[:, t, :, 0:HIST], lru_hist[:, t, :].rearrange("p (b n) -> p b n", b=DEC_B))
                cp(padded[:, t, :, HIST:], proj[:, 12 + t, SEQ:T].rearrange("p (b n) -> p b n", b=DEC_B))
                cp(lru_tail[:, t, 12:36].rearrange("p (b n) -> p b n", b=DEC_B),
                   proj[:, 12 + t, SEQ:T].rearrange("p (b n) -> p b n", b=DEC_B)[:, :, DEC_T - HIST:])
            link(cp(lru_tail[:, :, 9:12], proj[:, 12:16, SEQ - HIST:SEQ]))
            N = PADT - HIST
            for t in range(LT):
                link(tsc(u_acc[:, 0:N], u_pad[:, t, 3:3 + N], conv_w_l[:, 3, t:t + 1], conv_b_l[:, t:t + 1], ALU.mult, ALU.add))
                for w in (2, 1):
                    link(stt(u_acc[:, 0:N], u_pad[:, t, w:w + N], conv_w_l[:, w, t:t + 1], u_acc[:, 0:N], ALU.mult, ALU.add))
                link(stt(u_acc[:, 0:N], u_pad[:, t, 0:N], conv_w_l[:, 0, t:t + 1], u_acc[:, 0:N], ALU.mult, ALU.add))
                cp(uc[:, t, 0:SEQ], u_acc[:, 0:SEQ])
                link(cp(uc[:, t, SEQ:T].rearrange("p (b n) -> p b n", b=DEC_B), of_samples(u_acc[:])))
                if t == 1:
                    l1(2)
            dve.sem_inc(uc_ok, 1)
            l1(3)
            c4 = lambda n: stat[:, 4 * n:4 * n + 4]
            stt(c4(1), lam, -1.0, lam, ALU.mult, ALU.max).then_inc(lam_e, 1)
            dve.wait_ge(lam_e, 2)
            link(tsc(c4(3), c4(2), 1.0, None, ALU.add))
            link(tsc(c4(5), c4(3), -1.0, None, ALU.add))
            dve.sem_inc(lam_u, 1)
            link(tsc(c4(6), c4(5), 0.0, None, ALU.is_equal))
            link(tt(c4(5), c4(5), c4(6), ALU.add))
            link(dve.reciprocal(c4(5), c4(5)))
            dve.wait_ge(lam_l, 1)
            link(tt(c4(4), c4(4), c4(6), ALU.add))
            link(tt(c4(4), c4(4), c4(2), ALU.mult))
            link(tt(c4(4), c4(4), c4(5), ALU.mult))
            link(tsc(c4(7), lam, -1.0, 0.0, ALU.mult, ALU.max))
            link(tt(c4(7), c4(7), c4(4), ALU.add))
            link(tsc(c4(7), c4(7), -8.0, None, ALU.mult))
            l1(4)
            l1(5)
            for t in range(LT):
                dve.wait_ge(gr_ok, t + 1)
                last = tsc(lru_a[:, t * T:(t + 1) * T], lru_a[:, t * T:(t + 1) * T], stat[:, 28 + t:29 + t], None, ALU.mult)
            last.then_inc(la_ok, 1)
            dve.wait_ge(gi_ok, LT)
            link(tt(lru_i[:], lru_i[:], uc[:].rearrange("p t n -> p (t n)"), ALU.mult))
            dve.wait_ge(a_ok, 1)
            a2 = u_pad[:].rearrange("p t n -> p (t n)")[:, 0:LT * T]
            link(tt(a2, lru_a[:], lru_a[:], ALU.mult))
            stt(lru_t[:], a2, 1.0, lru_t[:], ALU.add, ALU.mult).then_inc(a2_ok, 1)
            dve.wait_ge(s_ok, 1)
            link(tt(lru_i[:], lru_i[:], lru_t[:], ALU.mult))
            l1(6)
            a3 = lru_a[:].rearrange("p (t n) -> p t n", t=LT)
            b3 = lru_i[:].rearrange("p (t n) -> p t n", t=LT)
            a0, b0 = a3[:, :, SEQ:T:DEC_T], b3[:, :, SEQ:T:DEC_T]
            h1 = stat[:, 64:96].rearrange("p (t b) -> p t b", t=LT)
            link(tt(h1, a0, lru_h0[:], ALU.mult))
            tt(b0, b0, h1, ALU.add)
            link(dve.memset(a0, 0.0))
            link(dve.memset(a3[:, :, 0:1], 0.0))
            ucf = uc[:].rearrange("p t n -> p (t n)")
            link(dve.tensor_tensor_scan(ucf, lru_a[:], lru_i[:], 0.0, ALU.mult, ALU.add))
            cp(lru_tail[:, :, 0:1], uc[:, :, SEQ - 1:SEQ])
            cp(lru_tail[:, :, 1:9], uc[:, :, SEQ + DEC_T - 1:T:DEC_T])
            dve.wait_ge(g_ok, 1)
            tt(cat[:, AT:, :], uc[:], proj[:, 16:20, :], ALU.mult).then_inc(lru_end, 1)
            dve.wait_ge(lru_end, 1)
            for n in range(7, 10):
                l1(n)
            dve.wait_ge(free["l1"], 12)
            dve.wait_ge(free_act1, 12)

            for n in range(8):
                dve.wait_ge(kvt_tr, n + 1)
                dst = (k_tok if n < 4 else v_tok)
                cp(dst[:, 0:NCH, (n % 4) * P:(n % 4 + 1) * P], ps[:, 2 * (n % 4), :].rearrange("p (c d) -> p c d", c=NCH)).then_inc(kvt_up, 1)
            link(dve.memset(qx[:], 0.0))
            for t in range(AT):
                for hh in range(2):
                    r = 64 * hh
                    cp(qx[r:r + 64, t, :, 16 * t + 8 * hh:16 * t + 8 * hh + 8],
                       proj[r:r + 64, t, SEQ:T].rearrange("p (b n) -> p b n", b=DEC_B))
            cp(ks_T[:], proj[:, 4:8, SEQ:T]).then_inc(qx_ok, 1)

            NQ = HEADS * NCH

            def o_out(u):
                dve.wait_ge(o_mm, 8 * u + 8)
                cp(cat[:, u, 0:SEQ], ps[:, 4 + u % 2, :]).then_inc(o_up, 1)
            for n in range(NQ + 1):
                if n < NQ:
                    w = (n % NCH + 1) * P
                    dve.wait_ge(sc_mm, n + 1)
                    mx, neg = stat[:, 32 + n % 2:33 + n % 2], stat[:, 34 + n % 2:35 + n % 2]
                    link(dve.tensor_reduce(mx, ps[:, n % 3, 0:w], AX, ALU.max))
                    tsc(neg, mx, -(HD ** -0.5), None, ALU.mult).then_inc(mx_ok, 1)
                if n >= 1:
                    m = n - 1
                    w = (m % NCH + 1) * P
                    dve.wait_ge(ex_ok, m + 1)
                    rc = stat[:, 38 + m % 2:39 + m % 2]
                    link(dve.reciprocal(rc, stat[:, 36 + m % 2:37 + m % 2]))
                    tsc(pp[:, m % 2, 0:w], pp[:, m % 2, 0:w], rc, None, ALU.mult).then_inc(pn_ok, 1)
                if n >= 2 and (n - 2) % 8 == 7:
                    o_out((n - 2) // 8)
            o_out(3)

            def keys_out(n):
                if n >= 3:
                    dve.wait_ge(qs_mm, n - 2)
                for t in range(AT):
                    dve.wait_ge(kt_mm, 4 * n + t + 1)
                    cp(kt[n % 3][:, t, :], ps[:, t, :]).then_inc(kt_dve, 1)

            def heads_out(pr):
                dve.wait_ge(s_ot, pr + 1)
                for t in range(AT):
                    for hh in range(2):
                        r, c0 = 64 * hh, SEQ + DEC_T * 2 * pr
                        i = cp(cat[r:r + 64, t, c0:c0 + 2 * DEC_T].rearrange("p (b n) -> p b n", b=2),
                               ps[r:r + 64, 6, t * P:(t + 1) * P].rearrange("p (b n) -> p b n", b=2)[:, :, 16 * t + 8 * hh:16 * t + 8 * hh + 8])
                i.then_inc(s_ou, 1)

            keys_out(1)
            for pr in range(DEC_B // 2):
                if pr:
                    heads_out(pr - 1)
                keys_out(4 * pr + 3)
                dve.wait_ge(qs_mm, 4 * pr + 4)
                if pr:
                    dve.wait_ge(s_pn, pr)
                S = ps[:, 4:6, :].rearrange("p u (n k) -> p (u n) k", k=BLK)
                bs, bm = stat[:, 56:60], stat[:, 60:65]
                dve.tensor_reduce(bs, S, AX, ALU.add)
                dve.tensor_reduce(bm[:, 0:NBLK], S, AX, ALU.max)
                link(dve.tensor_reduce(bm[:, NBLK:], ps[:, 6, 0:NS], AX, ALU.max))
                gt = stat[:, 96:112].rearrange("p (a b) -> p a b", a=NBLK)
                eq = stat[:, 112:128].rearrange("p (a b) -> p a b", a=NBLK)
                mine, other = bs.unsqueeze(2).broadcast_to([P, NBLK, NBLK]), bs.unsqueeze(1).broadcast_to([P, NBLK, NBLK])
                tt(gt, other, mine, ALU.is_gt)
                link(tt(eq, other, mine, ALU.is_equal))
                link(tt(eq, eq, tri[:, 0:NBLK, 0:NBLK], ALU.mult))
                link(tt(gt, gt, eq, ALU.add))
                rank = stat[:, 128:132]
                link(dve.tensor_reduce(rank, gt, AX, ALU.add))
                pen = stat[:, 132:136]
                link(tsc(pen, rank, float(NBLK - 1), NEG, ALU.is_ge, ALU.mult))
                link(tt(bm[:, 0:NBLK], bm[:, 0:NBLK], pen, ALU.add))
                link(dve.tensor_reduce(stat[:, 136:137], bm, AX, ALU.max))
                link(tsc(stat[:, 44:45], stat[:, 136:137], -(HD ** -0.5), None, ALU.mult))
                tsc(stat[:, 40:44], pen, stat[:, 44:45], None, ALU.add).then_inc(s_bias, 1)
                if pr < DEC_B // 2 - 1:
                    keys_out(4 * pr + 5)
                dve.wait_ge(s_ex, pr + 1)
                link(dve.tensor_reduce(stat[:, 137:138], stat[:, 48:53], AX, ALU.add))
                link(dve.reciprocal(stat[:, 138:139], stat[:, 137:138]))
                tsc(p_s[:], p_s[:], stat[:, 138:139], None, ALU.mult).then_inc(s_pn, 1)
            heads_out(DEC_B // 2 - 1)

            dve.wait_ge(s_ou, 4)
            dve.sem_inc(free["l2"], 2)
            for j in range(KD // 2):
                residual("l2", j, 4 * (j % 2), ln_ready if j == 3 else None)
            def f_rest(n):
                u, m = n % TILES, n // 2
                K = KD if u // 2 < FET else FET
                dve.wait_ge(w_hi, n + 1)
                tt(fw_l[:, n % RAW, 0:K, :], ring[:, m % RAW, 0:K, (n % 2) * P:(n % 2 + 1) * P], fw_h[:, n % RAW, 0:K, :].bitcast(F32),
                   ALU.subtract).then_inc(w_lo, 1)

            for n in range(RAW):
                f_rest(n)
            layer_norm(0)
            for k in range(KD):
                dve.wait_ge(ln_out, k + 1)
                tt(xf_l[:, k, :], xT[:, k, :], xf_h[:, k, :].bitcast(F32), ALU.subtract).then_inc(x_lo, 1)
            for n in range(PER_E * FROUNDS):
                r, v = n // PER_E, n % PER_E
                for u in (2 * n + 3, 2 * n + 4):
                    if u < TILES * FROUNDS:
                        f_rest(u)
                if v < FET:
                    dve.wait_ge(f_silu, FET * r + v + 1)
                    if n:
                        dve.wait_ge(f_hid, FET * r + v)
                    tt(halves(f_m[:]), halves(f_s[:]), banks(4 * (n % 2) + 2), ALU.mult).then_inc(f_bank, 1)
                    dve.wait_ge(f_bank, n + 1)
                    link(cp(hid_h[:, v, :], f_m[:]))
                    tt(hid_l[:, v, :], f_m[:], hid_h[:, v, :].bitcast(F32), ALU.subtract).then_inc(f_hid, 1)
                else:
                    dve.wait_ge(w_used, RAW + 2 * n + 2)
                    for q in range(2):
                        y = halves(xT[:, 2 * (v - FET) + q, :])
                        p = banks(4 * (n % 2) + 2 * q)
                        i = stt(y, y, ALPHA, p, ALU.mult, ALU.add) if r == 0 else tt(y, y, p, ALU.add)
                    i.then_inc(ln_ready if n == PER_E * FROUNDS - 1 else f_bank, 1)
            def x_rest(n, q):
                dve.wait_ge(w_hi, TILES * FROUNDS + 2 * n + q + 1)
                tt(xw_l[q][:], x_raw[n % 2][:, :, q * P:(q + 1) * P], xw_h[q][:].bitcast(F32), ALU.subtract).then_inc(w_lo, 1)

            x_rest(0, 0)
            x_rest(0, 1)
            layer_norm(1)

            for k in range(KD):
                dve.wait_ge(ln_out, KD + k + 1)
                tt(xs_l[:, k, :], xT[:, k, :], xs_h[:, k, :].bitcast(F32), ALU.subtract).then_inc(x_lo, 1)

            link(dve.memset(raw[:, :, 0:HIST], 0.0))
            dve.sem_inc(cv_y, 2)

            def conv(n, j):
                dve.wait_ge(free["xb"], n + 3)
                s = 2 * (j % 2)
                for q in range(2):
                    smp = raw[:, s + q, HIST + SEQ:].rearrange("p (b t) -> p b t", b=DEC_B)
                    cp(smp[:, :, 0:HIST], ssd_hist[:, ds(2 * n + q, 1), :].rearrange("p o (b t) -> p (o b) t", b=DEC_B))
                    cp(ssd_tail[:, ds(2 * n + q, 1), HIST:].rearrange("p o (b t) -> p (o b) t", b=DEC_B), smp[:, :, DEC_T:])
                link(cp(ssd_tail[:, ds(2 * n, 2), 0:HIST], raw[:, s:s + 2, SEQ:SEQ + HIST]))
                dve.wait_ge(cv_s, n + 1)
                for w in (3, 2, 1, 0):
                    for q in range(2):
                        x = raw[:, s + q, w:w + N]
                        cw = conv_w_s[:, w, ds(2 * n + q, 1)]
                        if w == 3:
                            i = tsc(acc[:, q, 0:N], x, cw, conv_b_s[:, ds(2 * n + q, 1)], ALU.mult, ALU.add)
                        else:
                            i = stt(acc[:, q, 0:N], x, cw, acc[:, q, 0:N], ALU.mult, ALU.add)
                    if w:
                        link(i)
                    if w == 2 and n + 2 < XU:
                        x_rest(n + 2, 0)
                i.then_inc(cv_y, 1)
            x_rest(1, 0)
            for n in range(XU):
                if n + 1 < XU:
                    x_rest(n + 1, 1)
                conv(n, n)

            dve.sem_inc(free["dt"], 1)
            dve.wait_ge(used, done("dt", 0))
            dve.wait_ge(cv_s, XBC // 2 + 1)
            dve.wait_ge(in_small, 64)
            R = lambda n: tmpr[0:SH, n, :]
            W = lambda n: rows[0:SH, n, :]
            link(tsc(halves(R(0)), ps[0:SH, 0:2, 0:HALF], dt_par[:, 0:1], None, ALU.add))
            stt(R(1), R(0), -1.0, R(0), ALU.mult, ALU.max).then_inc(dt_a, 1)
            dve.wait_ge(dt_e, 1)
            link(tsc(dt_par[:, 3:4], dt_par[:, 3:4], -1.0, None, ALU.mult))
            link(tsc(R(3), R(2), 1.0, None, ALU.add))
            tsc(R(4), R(3), -1.0, None, ALU.add).then_inc(dt_u, 1)
            dve.wait_ge(dt_l, 1)
            link(tsc(R(3), R(4), 0.0, None, ALU.is_equal))
            link(tt(R(4), R(4), R(3), ALU.add))
            link(dve.reciprocal(R(4), R(4)))
            link(tt(R(1), R(1), R(3), ALU.add))
            link(tt(R(1), R(1), R(2), ALU.mult))
            link(tt(R(1), R(1), R(4), ALU.mult))
            link(stt(W(DTR), R(0), 0.0, R(1), ALU.max, ALU.add))
            link(tsc(R(0), W(DTR), dt_par[:, 3:4], None, ALU.mult))
            link(dve.tensor_tensor_scan(W(CSR), run_row[:], R(0), 0.0, ALU.mult, ALU.add))
            csp = W(CSR)[:, 0:SEQ].rearrange("p (c n) -> p c n", c=NCH)
            css = W(CSR)[:, SEQ:T].rearrange("p (c n) -> p c n", c=DEC_B)
            tt(R(0)[:, 0:SEQ].rearrange("p (c n) -> p c n", c=NCH), csp[:, :, P - 1:P].broadcast_to([SH, NCH, P]), csp, ALU.subtract)
            tt(R(0)[:, SEQ:T].rearrange("p (c n) -> p c n", c=DEC_B), css[:, :, DEC_T - 1:DEC_T].broadcast_to([SH, DEC_B, DEC_T]), css,
               ALU.subtract).then_inc(cs_ok, 1)
            dve.wait_ge(ec_ok, 1)
            tt(R(1)[:, 0:SH * NCH].rearrange("p (h c) -> p h c", h=SH), ident[0:SH, 0:SH].unsqueeze(2).broadcast_to([SH, SH, NCH]),
               W(ECR)[:, P - 1:SEQ:P].unsqueeze(1).broadcast_to([SH, SH, NCH]), ALU.mult)
            cp(ident_r[:], ident[:])
            cp(sl_mask_r[:], sl_mask[:])
            link(cp(cs_h[0:SH, :], W(CSR)[:, 0:SEQ]))
            tt(cs_l[0:SH, :], W(CSR)[:, 0:SEQ], cs_h[0:SH, :].bitcast(F32), ALU.subtract)
            tt(W(WDR), R(0), W(DTR), ALU.mult).then_inc(row_ok, 1)
            dve.wait_ge(tk_mm, 1)
            for n, sc in enumerate((1.0, -1.0, 1.0)):
                tsc(tok[:, n, 0:NCH * SH], ps[:, 2 + n, 0:NCH * SH], sc, None, ALU.mult)
                tsc(tok[0:NS, n, NCH * SH:], ps[0:NS, 2 + n, NCH * SH:5 * SH], sc, None, ALU.mult)
            cp(dec_p[:], ps[:, 5, 0:SH * NCH])
            cp(dec_s[:].rearrange("p t b -> p (t b)"), ps[:, 6, 0:P])
            cp(d_exp, ps[:, 6, P:P + XT]).then_inc(tk_up, 1)
            dve.wait_ge(tk_up, 1)

            for g in range(SG):
                dve.wait_ge(g_mm, g + 1)
                def scaled(dst, which, j):
                    h = 4 * g + 2 * j
                    fac = tok[:, which, 0:NCH * SH].rearrange("p (c h) -> p c h", c=NCH)
                    return tt(dst[:, 0:NCH, j * P:(j + 1) * P].rearrange("p c (h n) -> p c h n", h=2),
                              ps[:, 3 + 3 * j, :].rearrange("p (c h n) -> p c h n", c=NCH, h=2),
                              fac[:, :, h:h + 2].unsqueeze(3).broadcast_to([P, NCH, 2, 64]), ALU.mult)

                def scaled_samples(dst, which):
                    return tt(dst[0:NS, NCH, :].rearrange("p (h n) -> p h n", h=4), ps[0:NS, 1, 256:512].rearrange("p (h n) -> p h n", h=4),
                              tok[0:NS, which, NCH * SH + 4 * g:NCH * SH + 4 * g + 4].unsqueeze(2).broadcast_to([NS, 4, 64]), ALU.mult)
                scaled(x_w, 2, 0)
                scaled(x_w, 2, 1)
                scaled(x_dt, 0, 1).then_inc(g_up, 1)
                scaled(x_dt, 0, 0)
                scaled_samples(x_dt, 0)
                scaled_samples(x_w, 2)
                dve.wait_ge(st_mm, g + 1)
                dec = dec_p[:].rearrange("p (h c) -> p h c", h=SH)
                link(cp(state[:, 0, :], ps[:, 6, 0:256]))
                for c in range(1, NCH):
                    v = state[:, c, :].rearrange("p (h n) -> p h n", h=4)
                    link(tt(v, state[:, c - 1, :].rearrange("p (h n) -> p h n", h=4), dec[:, 4 * g:4 * g + 4, c:c + 1].broadcast_to([P, 4, 64]), ALU.mult))
                    i = tt(state[:, c, :], state[:, c, :], ps[:, 6 + c // 2, (c % 2) * 256:(c % 2 + 1) * 256], ALU.add)
                    if c < NCH - 1:
                        link(i)
                    else:
                        i.then_inc(st_up, 1)
                tt(b_seq[0:NS], ps[0:NS, 1, P:2 * P].unsqueeze(1).broadcast_to([NS, DEC_B, P]),
                   of_seq[:].unsqueeze(2).broadcast_to([NS, DEC_B, P]), ALU.mult)
                for j in range(2):
                    t = 2 * g + j
                    Ct = xbc[:, XT + BC + g, :]
                    if t:
                        dve.wait_ge(yt_mm, t)
                    for hh in range(2):
                        dve.wait_ge(e_ok, 3 * t + hh + 1)
                        tt(ce[:, hh, P:SEQ], Ct[:, P:SEQ], ebc[:, hh, P:SEQ], ALU.mult)
                        tt(m_buf[:, hh, 0:SEQ], ps[:, 0, :], e_buf[:, hh, 0:SEQ], ALU.mult).then_inc(m_ok, 1)
                    dve.wait_ge(e_ok, 3 * t + 3)
                    tt(ce[:, :, SEQ:T], Ct[:, SEQ:T].unsqueeze(1).broadcast_to([P, 2, NS]), ebc[:, :, SEQ:T], ALU.mult)
                    tt(m_buf[0:NS, :, SEQ:T], ps[0:NS, 1, 0:NS].unsqueeze(1).broadcast_to([NS, 2, NS]), e_buf[0:NS, :, SEQ:T], ALU.mult).then_inc(m_ok, 1)
                    dve.wait_ge(yt_mm, t + 1)
                    stt(xbc[:, t, SEQ:T], xbc[:, t, SEQ:T], d_exp[:, t:t + 1], ps[:, 3, 0:NS], ALU.mult, ALU.add)
                    stt(xbc[:, t, 0:SEQ], xbc[:, t, 0:SEQ], d_exp[:, t:t + 1], ps[:, 2, :], ALU.mult, ALU.add).then_inc(y_ok, 1)
                    dve.wait_ge(ss_mm, t + 1)
                    dve.wait_ge(hd_ok, t + 1)
                    v = h0n[t % 2].rearrange("p (u b) n -> p u (b n)", u=2)
                    tt(v, v, ps[:, 6:8, :], ALU.add).then_inc(ss_ok, 1)

            NZ = XT // 2

            def z_norm(n):
                dve.wait_ge(z_rt, n + 1)
                link(dve.reciprocal(z_i[:], z_r[:]))
                for q in range(2):
                    y = xbc[:, 2 * n + q, :]
                    last = stt(y, y, norm_g[:, 2 * n + q:2 * n + q + 1], z_i[:], ALU.mult, ALU.mult)
                last.then_inc(z_ok, 1)
            for n in range(NZ):
                v = xbc[:, 2 * n:2 * n + 2, :]
                dve.wait_ge(free["z"], n + 2)
                tt(v, v, z_s[:], ALU.mult).then_inc(z_gate, 1)
                if n:
                    z_norm(n - 1)
            z_norm(NZ - 1)
            dve.wait_ge(z_ok, NZ)
            dve.sem_inc(free["l6"], 2)
            for j in range(KD // 2):
                residual("l6", j, 4 * (j % 2), ln_ready if j == 3 else None)
            layer_norm(2)
            dve.wait_ge(ss_out, 16 * XT)
            dve.wait_ge(fs_out, 16 * SG)
            for n in range(9):
                dve.wait_ge(row_mm, n + 1)
                if n < 8:
                    cp(tail_s[0:27, n * 512:(n + 1) * 512], ps[0:27, n % 2, :]).then_inc(row_up, 1)
                else:
                    cp(tail_l[0:36, :], ps[0:36, n % 2, :]).then_inc(row_up, 1)

            dve.wait_ge(tl_out, 96)
            lg, gts = stat[:, 40:80], stat[:, 0:40]
            link(dve.memset(lg, 0.0))
            dve.wait_ge(rt_mm, 1)
            cp(lg[:, 0:32], ps[:, 4, 0:32])
            link(cp(lg[0:NS, 32:40], ps[0:NS, 4, 32:40]))
            l3 = lg.rearrange("p (c e) -> p c e", c=5)
            gg = g_w[:, 10:90].rearrange("p (u n) -> p u n", u=2)
            gt = g_w[:, 100:140].rearrange("p (c e) -> p c e", c=5)
            rank = g_w[:, 140:180].rearrange("p (c e) -> p c e", c=5)
            sel = g_w[:, 180:220].rearrange("p (c e) -> p c e", c=5)
            link(dve.memset(rank, 0.0))
            for o in range(NE):
                other = l3[:, :, o:o + 1].broadcast_to([P, 5, NE])
                link(tt(gt, other, l3, ALU.is_gt))
                link(tt(rank, rank, gt, ALU.add))
                if o < NE - 1:
                    n = NE - 1 - o
                    link(tt(gt[:, :, 0:n], l3[:, :, o:o + 1].broadcast_to([P, 5, n]), l3[:, :, o + 1:], ALU.is_equal))
                    link(tt(rank[:, :, o + 1:], rank[:, :, o + 1:], gt[:, :, 0:n], ALU.add))
            best = [g_w[:, 220:225], g_w[:, 225:230]]
            for r in range(2):
                link(tsc(sel, rank, float(r), None, ALU.is_equal))
                link(tt(sel, sel, l3, ALU.mult))
                link(dve.tensor_reduce(best[r], sel, AX, ALU.add))
            tt(g_w[:, 5:10], best[1], best[0], ALU.subtract).then_inc(rt_d, 1)
            dve.wait_ge(rt_e, 1)
            link(tsc(best[0], g_w[:, 0:5], 1.0, None, ALU.add))
            link(dve.reciprocal(best[0], best[0]))
            link(tt(best[1], best[0], g_w[:, 0:5], ALU.mult))
            G = gts.rearrange("p (c e) -> p c e", c=5)
            Mf = g_w[:, 10:50]
            M = Mf.rearrange("p (c e) -> p c e", c=5)
            link(tsc(Mf, g_w[:, 140:180], 1.5, None, ALU.is_lt))
            dve.memset(Mf[NS:P, 32:40], 0.0).then_inc(rt_m, 1)
            for r in range(2):
                link(tsc(sel, rank, float(r), None, ALU.is_equal))
                link(tt(sel, sel, best[r].unsqueeze(2).broadcast_to([P, 5, NE]), ALU.mult))
                if r == 0:
                    link(cp(G, sel))
            link(tt(G, G, sel, ALU.add))
            link(cp(iota, iota_i[:]))
            for n in range(10):
                m = CHUNKS[n // 2][0]
                dve.wait_ge(xt_hi, n + 1)
                c = slice(512 * (n % 2), 512 * (n % 2) + 512)
                tt(xt_l[0:m, n // 2, c], ps[0:m, n % 4, :], xt_h[0:m, n // 2, c].bitcast(F32), ALU.subtract).then_inc(xt_lo, 1)
            dve.wait_ge(xt_mm, 10)
            for k in range(KD):
                last = tsc(xT[:, k, :], xT[:, k, :], ALPHA, None, ALU.mult)
            link(last)
            dve.wait_ge(ct_mm, 1)
            Q, cnt, nr, incl, excl = g_w[:, 60:100], g_w[:, 230:238], g_w[:, 238:246], g_w[:, 246:254], g_w[:, 254:262]
            tmp8 = g_w[:, 262:270]
            link(stt(Q, ps[:, 5, 0:40], BIG, Mf, ALU.add, ALU.mult))
            link(cp(cnt, ps[:, 6, 0:NE]))
            link(tsc(nr, cnt, 0.5, None, ALU.is_gt))
            for m in (1, 2):
                link(tsc(tmp8, cnt, CAP * m + 0.5, None, ALU.is_gt))
                link(tt(nr, nr, tmp8, ALU.add))
            link(dve.tensor_tensor_scan(incl, ones[:, 0:NE], nr, 0.0, ALU.mult, ALU.add))
            link(tt(excl, incl, nr, ALU.subtract))
            NR = RMAX + 2
            rounds3 = [P, NR, NE]
            inr = g_w[:, 270:270 + NR * NE].rearrange("p (r e) -> p r e", e=NE)
            off = g_w[:, 400:400 + NR * NE].rearrange("p (r e) -> p r e", e=NE)
            sub = g_w[:, 530:530 + NR]
            big = g_w[:, 600:600 + NR * 5 * NE].rearrange("p (r c e) -> p r c e", c=5, e=NE)
            r_of = iota[:, 0:NR].unsqueeze(2).broadcast_to(rounds3)
            link(tt(off, r_of, excl.unsqueeze(1).broadcast_to(rounds3), ALU.subtract))
            link(tt(inr, r_of, incl.unsqueeze(1).broadcast_to(rounds3), ALU.is_lt))
            link(stt(inr, off, 0.0, inr, ALU.is_ge, ALU.mult))
            off2 = g_w[:, 1210:1210 + NR * NE].rearrange("p (r e) -> p r e", e=NE)
            link(tt(off2, inr, iota[:, 0:NE].unsqueeze(1).broadcast_to(rounds3), ALU.mult))
            link(dve.tensor_reduce(g_w[:, 550:550 + NR], off2, AX, ALU.add))
            link(cp(expert_of[0:1, 0:NR], g_w[0:1, 550:550 + NR]))
            link(cp(n_rounds[:], incl[0:1, NE - 1:NE]))
            link(tt(off, off, inr, ALU.mult))
            link(dve.tensor_reduce(sub, off, AX, ALU.add))
            link(tsc(sub, sub, float(CAP), BIG, ALU.mult, ALU.add))
            rounds4 = [P, NR, 5, NE]
            for src, dst in ((Q, slot_of), (gts, gate_of)):
                link(tt(big, src.rearrange("p (c e) -> p c e", c=5).unsqueeze(1).broadcast_to(rounds4), inr.unsqueeze(2).broadcast_to(rounds4), ALU.mult))
                link(dve.tensor_reduce(dst[:], big, AX, ALU.add))
            link(tt(slot_of[:], slot_of[:], sub.unsqueeze(2).broadcast_to([P, NR, 5]), ALU.subtract))
            dve.sem_inc(rt_ok, 1)

            rounds = dve.value_load(n_rounds[0:1, 0:1], min_val=1, max_val=RMAX)

            def w_rest(r, u):
                m, j = u // 2, u % 2
                K = KD if m < FET else FET
                dve.wait_ge(w_hi, TILES * (r + FROUNDS) + 2 * XU + u + 1)
                tt(w_l[:, u % RAW, 0:K, :], ring[:, m % RAW, 0:K, j * P:(j + 1) * P], w_h[:, u % RAW, 0:K, :].bitcast(F32), ALU.subtract).then_inc(w_lo, 1)

            def one_hot(r):
                i = cp(gate_now, gate_of[:, ds(r, 1), :].rearrange("p o c -> p (o c)"))
                for c in range(5):
                    i = tsc(hot[:, c, :], iota, slot_of[:, ds(r, 1), c:c + 1].rearrange("p o c -> p (o c)"), None, ALU.is_equal)
                i.then_inc(hot_ok, 1)

            def gather_hi(r):
                for s in range(4):
                    dve.wait_ge(ga_mm, 4 * r + s + 1)
                    cp(xg_h[:, 2 * s:2 * s + 2, :].rearrange("p k n -> p (k n)"), ps[:, 3 + 2 * (s % 2), 0:2 * CAP]).then_inc(ga_hi, 1)

            def turned(r):
                dve.wait_ge(th_mm, 2 * r + 1)
                for u, m in ((0, P), (1, NS)):
                    cp(hotT[0:m, u, 0:SEQ], ps[0:m, 3 + 2 * u, :])
                    i = cp(hotT[0:m, u, SEQ:T], ps[0:m, 4 + 2 * u, 0:NS])
                i.then_inc(th_ok, 1)
                dve.wait_ge(th_mm, 2 * r + 2)
                cp(slot_gate[:, 0:1], ps[:, 7, 0:1])
                cp(slot_gate[0:NS, 1:2], ps[0:NS, 7, 1:2]).then_inc(th_ok, 1)

            dve.sem_inc(e_bank, 2)
            dve.sem_inc(sc_ok, 1)
            one_hot(0)
            for u in range(RAW):
                w_rest(0, u)
            gather_hi(0)
            turned(0)
            with dve.Fori(0, rounds) as r:
                link.enter(r, FET)
                for v in range(PER_E):
                    for u in (2 * v + 3, 2 * v + 4):
                        w_rest(r + u // TILES, u % TILES)
                    if v < FET:
                        dve.wait_ge(e_silu, FET * r + v + 1)
                        hm = h_m[:, v % 2, :]
                        i = tt(hm, h_s[:, v % 2, :], ps[:, v % 3, CAP:2 * CAP], ALU.mult)
                        i.then_inc(e_bank, 1)
                        dve.wait_ge(e_bank, 2 + FET * r + v + 1)
                        link(cp(h_h[:, v, :], hm))
                        tt(h_l[:, v, :], hm, h_h[:, v, :].bitcast(F32), ALU.subtract).then_inc(e_h, 1)
                    if v == FET - 3:
                        one_hot(r + 1)
                    if v == FET - 1:
                        gather_hi(r + 1)
                for u, m in ((0, P), (1, NS)):
                    dve.wait_ge(ty_hi, 2 * r + u + 1)
                    stt(yt_l[0:m, u, :].rearrange("p (g n) -> p g n", g=2), ps[0:m, 3 + 2 * u:5 + 2 * u, :], slot_gate[0:m, u:u + 1],
                        yt_h[0:m, u, :].bitcast(F32).rearrange("p (g n) -> p g n", g=2), ALU.mult, ALU.subtract).then_inc(ty_lo, 1)
                for k in range(KD):
                    dve.wait_ge(sc_y, KD * r + k + 1)
                    tt(halves(xT[:, k, :]), halves(xT[:, k, :]), banks(3 + 2 * (k % 2)), ALU.add).then_inc(sc_ok, 1)
                turned(r + 1)
            dve.sem_inc(ln_ready, 1)
            layer_norm(3)
            for n in range(10):
                dve.wait_ge(row_mm, 9 + n + 1)
                m = CHUNKS[n // 2][0]
                cp(y_out[0:m, n // 2, 512 * (n % 2):512 * (n % 2) + 512], ps[0:m, n % 4, :]).then_inc(row_up, 1)


_INS = ["x_prompt", "x_sample", "cache_k", "cache_v", "page_table", "state_lru_h", "state_lru_conv", "state_ssm",
        "state_ssd_conv", "w_in_even", "lru_conv_w", "lru_conv_b", "lru_w_a", "lru_b_a", "lru_w_x", "lru_b_x", "lru_lambda",
        "w_out_even", "ssd_w_in", "ssd_conv_w", "ssd_conv_b", "ssd_dt_bias", "ssd_a_log", "ssd_d", "ssd_norm_g", "ssd_w_out",
        "ffn_w1", "ffn_w3", "ffn_w2", "moe_router", "moe_w1", "moe_w3", "moe_w2", "ln_mix_g", "ln_mix_b", "ln_ffn_g", "ln_ffn_b"]
_OUTS = [("y_prompt", (1, SEQ, D)), ("y_sample", (DEC_B, DEC_T, D)),
         ("k_prompt", (1, 1, SEQ, HEADS, HD)), ("v_prompt", (1, 1, SEQ, HEADS, HD)),
         ("k_sample", (1, DEC_B, DEC_T, HEADS, HD)), ("v_sample", (1, DEC_B, DEC_T, HEADS, HD)),
         ("lru_h_prompt", (1, 1, 512)), ("lru_h_sample", (1, DEC_B, 512)),
         ("lru_conv_prompt", (1, 1, HIST, 512)), ("lru_conv_sample", (1, DEC_B, HIST, 512)),
         ("ssm_prompt", (1, 1, SH, 64, SN)), ("ssm_sample", (1, DEC_B, SH, 64, SN)),
         ("ssd_conv_prompt", (1, 1, HIST, SCONV)), ("ssd_conv_sample", (1, DEC_B, HIST, SCONV))]


def kernel(**inputs):
    import concourse.bacc as bacc
    from concourse.bass_utils import run_bass_kernel_spmd

    nc = bacc.Bacc("TRN2", target_bir_lowering=False, num_devices=1)
    arrays, I, O = {}, {}, {}
    for name in _INS:
        a = np.ascontiguousarray(inputs[name])
        arrays["in_" + name] = a
        I[name] = nc.dram_tensor("in_" + name, a.shape, mybir.dt.from_np(a.dtype), kind="ExternalInput").ap()
    for name, shape in _OUTS:
        O[name] = nc.dram_tensor("out_" + name, shape, F32, kind="ExternalOutput").ap()
    build(nc, I, O)
    r = run_bass_kernel_spmd(nc, [arrays], core_ids=[0])
    return tuple(r.results[0]["out_" + name] for name, _ in _OUTS)
```
